# Optimizing a Trainium2 kernel written in Bass

```python
import jax, jax.numpy as jnp
from jax import lax
import numpy as np

D_MODEL = 1024
BATCH = 1
SEQ = 256
DEPTH = 2
DEC_BATCH = 1
DEC_SEQ = 64
PAST_LEN = 256

CHUNK = 64
MLA_HEADS = 8
Q_RANK = 256
KV_RANK = 256
NOPE_DIM = 64
ROPE_DIM = 32
V_DIM = 64
ROPE_THETA = 10000.0
Q_BLOCK = 128
ATTN_SCALE = (NOPE_DIM + ROPE_DIM) ** -0.5
MLSTM_HEADS = 4
MLSTM_DH = 128
MLSTM_WIDTH = MLSTM_HEADS * MLSTM_DH
GMLP_GROUPS = 4
GMLP_DG = 128
GMLP_WIDTH = GMLP_GROUPS * GMLP_DG
GMLP_CHUNK = 128
BRANCH_WIDTH = 512
N_BRANCH = 3
N_EXPERTS = 16
N_GROUPS = 4
EXPERTS_PER_GROUP = N_EXPERTS // N_GROUPS
TOP_K = 2
D_EXPERT = 256
D_SHARED = 256
DN_ALPHA = (2 * DEPTH) ** 0.25
DN_BETA = (8 * DEPTH) ** -0.25
EPS = 1e-5
IN_SIZES = (Q_RANK, KV_RANK, ROPE_DIM, MLSTM_WIDTH, MLSTM_WIDTH, MLSTM_WIDTH,
            MLSTM_HEADS, MLSTM_HEADS, MLSTM_WIDTH, GMLP_WIDTH, GMLP_WIDTH, N_BRANCH * D_MODEL)
D_IN = sum(IN_SIZES)
FGATE_OFF = sum(IN_SIZES[:7])

kernel_name = 'streaming_hybrid_mla_mlstm_gmlp_moe'

def _split(z):
    offs, acc = [], 0
    for s in IN_SIZES[:-1]:
        acc += s
        offs.append(acc)
    return jnp.split(z, offs, axis=-1)

def _rmsnorm(x, g):
    xf = x.astype(jnp.float32)
    y = xf * lax.rsqrt(jnp.mean(xf * xf, -1, keepdims=True) + EPS)
    return (y * g.astype(jnp.float32)).astype(x.dtype)

def _layernorm(x, g, b):
    xf = x.astype(jnp.float32)
    mu = jnp.mean(xf, -1, keepdims=True)
    var = jnp.mean(jnp.square(xf - mu), -1, keepdims=True)
    y = (xf - mu) * lax.rsqrt(var + EPS)
    return (y * g.astype(jnp.float32) + b.astype(jnp.float32)).astype(x.dtype)

def _rope(x, cos, sin):
    xf = x.astype(jnp.float32)
    x1, x2 = jnp.split(xf, 2, axis=-1)
    return jnp.concatenate([x1 * cos - x2 * sin, x2 * cos + x1 * sin], -1).astype(x.dtype)

def _attend_block(qn, qr, qpos, kn, kr, v, kpos):
    s = jnp.einsum('bqhd,bkhd->bhqk', qn, kn) + jnp.einsum('bqhd,bkd->bhqk', qr, kr)
    s = s.astype(jnp.float32) * ATTN_SCALE
    allowed = (kpos // CHUNK)[None, :] <= (qpos // CHUNK)[:, None]
    s = jnp.where(allowed[None, None], s, -jnp.inf)
    p = jax.nn.softmax(s, axis=-1)
    return jnp.einsum('bhqk,bkhd->bqhd', p.astype(v.dtype), v)

def _mla_attention(qn, qr, qpos, kn, kr, v, kpos):
    B, T = qn.shape[0], qn.shape[1]
    if T > Q_BLOCK and T % Q_BLOCK == 0:
        nb = T // Q_BLOCK
        def blk(a):
            return jnp.moveaxis(a.reshape((B, nb, Q_BLOCK) + a.shape[2:]), 1, 0)
        out = lax.map(lambda a: _attend_block(a[0], a[1], a[2], kn, kr, v, kpos),
                      (blk(qn), blk(qr), qpos.reshape(nb, Q_BLOCK)))
        out = jnp.moveaxis(out, 0, 1).reshape(B, T, MLA_HEADS, V_DIM)
    else:
        out = _attend_block(qn, qr, qpos, kn, kr, v, kpos)
    return out.reshape(B, T, MLA_HEADS * V_DIM)

def _mlstm_chunk(carry, inp):
    C, n, m = carry
    q, k, v, ig, lf = inp
    L = q.shape[2]
    b = jnp.cumsum(lf, axis=-1)
    causal = jnp.tril(jnp.ones((L, L), dtype=bool))
    d = jnp.where(causal, b[..., :, None] - b[..., None, :] + ig[..., None, :], -jnp.inf)
    g = b + m[..., None]
    mt = jnp.maximum(g, jnp.max(d, axis=-1))
    inter = jnp.exp(g - mt)
    w = jnp.exp(d - mt[..., None])
    qk = jnp.einsum('bhtd,bhsd->bhts', q, k) * w
    num = inter[..., None] * jnp.einsum('bhed,bhtd->bhte', C, q) + jnp.einsum('bhts,bhse->bhte', qk, v)
    den = inter * jnp.einsum('bhd,bhtd->bht', n, q) + jnp.sum(qk, axis=-1)
    h = num / jnp.maximum(jnp.abs(den), jnp.exp(-mt))[..., None]
    mL = mt[..., -1]
    bL = b[..., -1:]
    ws = jnp.exp(bL - b + ig - mL[..., None])
    decay = jnp.exp(bL[..., 0] + m - mL)
    C_new = decay[..., None, None] * C + jnp.einsum('bhs,bhse,bhsd->bhed', ws, v, k)
    n_new = decay[..., None] * n + jnp.einsum('bhs,bhsd->bhd', ws, k)
    return (C_new, n_new, mL), h

def _mlstm(q, k, v, ipre, fpre, C0, n0, m0):
    B, T, _ = q.shape
    L = CHUNK if T % CHUNK == 0 else T
    nc = T // L
    def heads(a):
        a = a.astype(jnp.float32).reshape(B, nc, L, MLSTM_HEADS, MLSTM_DH)
        return jnp.transpose(a, (1, 0, 3, 2, 4))
    def gates(a):
        return jnp.transpose(a.astype(jnp.float32).reshape(B, nc, L, MLSTM_HEADS), (1, 0, 3, 2))
    ig = gates(ipre)
    lf = jax.nn.log_sigmoid(gates(fpre))
    (C, n, m), h = lax.scan(_mlstm_chunk, (C0, n0, m0),
                            (heads(q), heads(k) * (MLSTM_DH ** -0.5), heads(v), ig, lf))
    h = jnp.transpose(h, (1, 0, 3, 2, 4)).reshape(B, T, MLSTM_WIDTH)
    return h, C, n, m

def _gmlp(u, v, ln_g, ln_b, ws, bs):
    B, T, _ = u.shape
    u = jax.nn.gelu(u)
    v = _layernorm(jax.nn.gelu(v), ln_g, ln_b)
    L = GMLP_CHUNK if T % GMLP_CHUNK == 0 else T
    nc = T // L
    w = jnp.where(jnp.tril(jnp.ones((L, L), dtype=bool)), ws[:, :L, :L], 0).astype(v.dtype)
    vc = v.reshape(B, nc, L, GMLP_GROUPS, GMLP_DG)
    sp = jnp.einsum('gts,bcsgd->bctgd', w, vc) + bs[:, :L].T[:, :, None].astype(v.dtype)
    return u * sp.reshape(B, T, GMLP_WIDTH), v

def _swiglu(x, wg, wu, wd):
    return (jax.nn.silu(x @ wg) * (x @ wu)) @ wd

def _moe(x, router_w, router_b, wg, wu, wd, sg, su, sd):
    B, T, D = x.shape
    xf = x.reshape(B * T, D)
    s = jax.nn.sigmoid((xf @ router_w).astype(jnp.float32))
    sb = s + router_b.astype(jnp.float32)
    gscore = jnp.sum(lax.top_k(sb.reshape(-1, N_GROUPS, EXPERTS_PER_GROUP), TOP_K)[0], axis=-1)
    gsel = jnp.argmax(gscore, axis=-1)
    emask = (jnp.arange(N_EXPERTS) // EXPERTS_PER_GROUP)[None, :] == gsel[:, None]
    _, idx = lax.top_k(jnp.where(emask, sb, -jnp.inf), TOP_K)
    wsel = jnp.take_along_axis(s, idx, axis=-1)
    wsel = wsel / jnp.sum(wsel, axis=-1, keepdims=True)
    gate = jnp.sum(jax.nn.one_hot(idx, N_EXPERTS, dtype=jnp.float32) * wsel[..., None], axis=1)
    out = _swiglu(xf, sg, su, sd).astype(jnp.float32)
    for e in range(N_EXPERTS):
        out = out + gate[:, e:e + 1] * _swiglu(xf, wg[e], wu[e], wd[e]).astype(jnp.float32)
    return out.astype(x.dtype).reshape(B, T, D)

def _trunk(x, ckv_past, kr_past, c0, n0, m0, w):
    (w_in, b_in, q_norm_g, kv_norm_g, w_uq, w_ukv, gmlp_ln_g, gmlp_ln_b, gmlp_ws, gmlp_bs,
     w_branch, w_out, ln1_g, ln1_b, router_w, router_b, moe_w_gate, moe_w_up, moe_w_down,
     shared_w_gate, shared_w_up, shared_w_down, ln2_g, ln2_b) = w
    B, T, _ = x.shape
    past = 0 if ckv_past is None else ckv_past.shape[2]
    positions = past + jnp.arange(T)
    kpos = jnp.arange(past + T)
    half = ROPE_DIM // 2
    inv = ROPE_THETA ** (-jnp.arange(half, dtype=jnp.float32) / half)
    ang = positions.astype(jnp.float32)[:, None] * inv[None, :]
    cos, sin = jnp.cos(ang), jnp.sin(ang)
    ckvs, krs, Cs, ns, ms, gvs = [], [], [], [], [], []
    for l in range(DEPTH):
        z = x @ w_in[l] + b_in[l]
        cq, ckv, kr, mq, mk, mv, mi, mf, mo, gu, gv, gt = _split(z)
        q = (_rmsnorm(cq, q_norm_g[l]) @ w_uq[l]).reshape(B, T, MLA_HEADS, NOPE_DIM + ROPE_DIM)
        qn = q[..., :NOPE_DIM]
        qr = _rope(q[..., NOPE_DIM:], cos[:, None], sin[:, None])
        ckv = _rmsnorm(ckv, kv_norm_g[l])
        kr = _rope(kr, cos, sin)
        if ckv_past is None:
            ckv_all, kr_all = ckv, kr
        else:
            ckv_all = jnp.concatenate([ckv_past[l].astype(ckv.dtype), ckv], axis=1)
            kr_all = jnp.concatenate([kr_past[l].astype(kr.dtype), kr], axis=1)
        kv = (ckv_all @ w_ukv[l]).reshape(B, past + T, MLA_HEADS, NOPE_DIM + V_DIM)
        a_out = _mla_attention(qn, qr, positions, kv[..., :NOPE_DIM], kr_all, kv[..., NOPE_DIM:], kpos)
        if c0 is None:
            C_init = jnp.zeros((B, MLSTM_HEADS, MLSTM_DH, MLSTM_DH), jnp.float32)
            n_init = jnp.zeros((B, MLSTM_HEADS, MLSTM_DH), jnp.float32)
            m_init = jnp.zeros((B, MLSTM_HEADS), jnp.float32)
        else:
            C_init = c0[l].astype(jnp.float32)
            n_init = n0[l].astype(jnp.float32)
            m_init = m0[l].astype(jnp.float32)
        h, C, n, m = _mlstm(mq, mk, mv, mi, mf, C_init, n_init, m_init)
        b_out = (jax.nn.sigmoid(mo.astype(jnp.float32)) * h).astype(x.dtype)
        c_out, v_rows = _gmlp(gu, gv, gmlp_ln_g[l], gmlp_ln_b[l], gmlp_ws[l], gmlp_bs[l])
        merged = jax.nn.sigmoid(gt[..., :D_MODEL]) * (a_out @ w_branch[l, 0])
        merged = merged + jax.nn.sigmoid(gt[..., D_MODEL:2 * D_MODEL]) * (b_out @ w_branch[l, 1])
        merged = merged + jax.nn.sigmoid(gt[..., 2 * D_MODEL:]) * (c_out @ w_branch[l, 2])
        x = _layernorm(DN_ALPHA * x + merged @ w_out[l], ln1_g[l], ln1_b[l])
        moe_out = _moe(x, router_w, router_b, moe_w_gate[l], moe_w_up[l], moe_w_down[l],
                       shared_w_gate[l], shared_w_up[l], shared_w_down[l])
        x = _layernorm(DN_ALPHA * x + moe_out, ln2_g[l], ln2_b[l])
        ckvs.append(ckv); krs.append(kr); Cs.append(C); ns.append(n); ms.append(m); gvs.append(v_rows)
    return (x, jnp.stack(ckvs), jnp.stack(krs), jnp.stack(Cs), jnp.stack(ns), jnp.stack(ms), jnp.stack(gvs))

def setup_inputs(seed: int = 0) -> dict:
    key = jax.random.key(seed)
    ks = jax.random.split(key, 32)
    f32 = jnp.float32
    def nrm(k, shape, scale):
        return jax.random.normal(k, shape, f32) * scale
    def gain(k, shape):
        return 1.0 + 0.01 * jax.random.normal(k, shape, f32)
    b_in = nrm(ks[8], (DEPTH, D_IN), 0.01)
    b_in = b_in.at[:, FGATE_OFF:FGATE_OFF + MLSTM_HEADS].add(3.0)
    return {
        'x_prompt': nrm(ks[0], (BATCH, SEQ, D_MODEL), 1.0),
        'x_sample': nrm(ks[1], (DEC_BATCH, DEC_SEQ, D_MODEL), 1.0),
        'cache_mla_ckv': nrm(ks[2], (DEPTH, DEC_BATCH, PAST_LEN, KV_RANK), 1.0),
        'cache_mla_krope': nrm(ks[3], (DEPTH, DEC_BATCH, PAST_LEN, ROPE_DIM), 1.0),
        'state_mlstm_c': nrm(ks[4], (DEPTH, DEC_BATCH, MLSTM_HEADS, MLSTM_DH, MLSTM_DH), 0.3),
        'state_mlstm_n': jnp.abs(nrm(ks[5], (DEPTH, DEC_BATCH, MLSTM_HEADS, MLSTM_DH), 0.5)),
        'state_mlstm_m': nrm(ks[6], (DEPTH, DEC_BATCH, MLSTM_HEADS), 0.5),
        'w_in': nrm(ks[7], (DEPTH, D_MODEL, D_IN), D_MODEL ** -0.5),
        'b_in': b_in,
        'q_norm_g': gain(ks[9], (DEPTH, Q_RANK)),
        'kv_norm_g': gain(ks[10], (DEPTH, KV_RANK)),
        'w_uq': nrm(ks[11], (DEPTH, Q_RANK, MLA_HEADS * (NOPE_DIM + ROPE_DIM)), Q_RANK ** -0.5),
        'w_ukv': nrm(ks[12], (DEPTH, KV_RANK, MLA_HEADS * (NOPE_DIM + V_DIM)), KV_RANK ** -0.5),
        'gmlp_ln_g': gain(ks[13], (DEPTH, GMLP_WIDTH)),
        'gmlp_ln_b': nrm(ks[14], (DEPTH, GMLP_WIDTH), 0.01),
        'gmlp_ws': nrm(ks[15], (DEPTH, GMLP_GROUPS, GMLP_CHUNK, GMLP_CHUNK), GMLP_CHUNK ** -0.5),
        'gmlp_bs': gain(ks[16], (DEPTH, GMLP_GROUPS, GMLP_CHUNK)),
        'w_branch': nrm(ks[17], (DEPTH, N_BRANCH, BRANCH_WIDTH, D_MODEL), DN_BETA * BRANCH_WIDTH ** -0.5),
        'w_out': nrm(ks[18], (DEPTH, D_MODEL, D_MODEL), DN_BETA * D_MODEL ** -0.5),
        'ln1_g': gain(ks[19], (DEPTH, D_MODEL)),
        'ln1_b': nrm(ks[20], (DEPTH, D_MODEL), 0.01),
        'router_w': nrm(ks[21], (D_MODEL, N_EXPERTS), D_MODEL ** -0.5),
        'router_b': nrm(ks[22], (N_EXPERTS,), 0.01),
        'moe_w_gate': nrm(ks[23], (DEPTH, N_EXPERTS, D_MODEL, D_EXPERT), D_MODEL ** -0.5),
        'moe_w_up': nrm(ks[24], (DEPTH, N_EXPERTS, D_MODEL, D_EXPERT), D_MODEL ** -0.5),
        'moe_w_down': nrm(ks[25], (DEPTH, N_EXPERTS, D_EXPERT, D_MODEL), DN_BETA * D_EXPERT ** -0.5),
        'shared_w_gate': nrm(ks[26], (DEPTH, D_MODEL, D_SHARED), D_MODEL ** -0.5),
        'shared_w_up': nrm(ks[27], (DEPTH, D_MODEL, D_SHARED), D_MODEL ** -0.5),
        'shared_w_down': nrm(ks[28], (DEPTH, D_SHARED, D_MODEL), DN_BETA * D_SHARED ** -0.5),
        'ln2_g': gain(ks[29], (DEPTH, D_MODEL)),
        'ln2_b': nrm(ks[30], (DEPTH, D_MODEL), 0.01),
    }

def reference(x_prompt, x_sample, cache_mla_ckv, cache_mla_krope, state_mlstm_c, state_mlstm_n,
              state_mlstm_m, w_in, b_in, q_norm_g, kv_norm_g, w_uq, w_ukv, gmlp_ln_g, gmlp_ln_b,
              gmlp_ws, gmlp_bs, w_branch, w_out, ln1_g, ln1_b, router_w, router_b, moe_w_gate,
              moe_w_up, moe_w_down, shared_w_gate, shared_w_up, shared_w_down, ln2_g, ln2_b):
    w = (w_in, b_in, q_norm_g, kv_norm_g, w_uq, w_ukv, gmlp_ln_g, gmlp_ln_b, gmlp_ws, gmlp_bs,
         w_branch, w_out, ln1_g, ln1_b, router_w, router_b, moe_w_gate, moe_w_up, moe_w_down,
         shared_w_gate, shared_w_up, shared_w_down, ln2_g, ln2_b)
    y_prompt, p_ckv, p_kr, p_c, p_n, p_m, _ = _trunk(x_prompt, None, None, None, None, None, w)
    y_sample, s_ckv, s_kr, s_c, s_n, s_m, s_gv = _trunk(
        x_sample, cache_mla_ckv, cache_mla_krope, state_mlstm_c, state_mlstm_n, state_mlstm_m, w)
    return (y_prompt, y_sample, p_ckv, p_kr, p_c, p_n, p_m, s_ckv, s_kr, s_c, s_n, s_m, s_gv)


_drawn_inputs = setup_inputs


def setup_inputs(seed=0):
    import zlib

    import numpy as np

    out = dict(_drawn_inputs(seed))
    spreads = {}
    factors = {'cache_mla_krope': 2.817,
     'q_norm_g': 8.0,
     'kv_norm_g': 5.432,
     'gmlp_ln_g': 5.489,
     'gmlp_ln_b': 5.742,
     'gmlp_bs': 8.0,
     'ln2_g': 2.683}
    for name, (base, spread) in spreads.items():
        noise = np.random.default_rng([zlib.crc32(name.encode()), seed]).standard_normal(out[name].shape)
        drawn = base * np.exp(spread * noise) if base else spread * noise
        out[name] = __import__('jax').numpy.asarray(drawn.astype(out[name].dtype))
    for name, factor in factors.items():
        out[name] = (out[name] * factor).astype(out[name].dtype)
    return out
```

```python
from contextlib import ExitStack

import concourse.bass as bass
import numpy as np
from concourse import mybir

F32, F16 = mybir.dt.float32, mybir.dt.float16
ALU = mybir.AluOpType
ACT = mybir.ActivationFunctionType
AXX = mybir.AxisListType.X

P = 128
DM, L = 1024, 2
TP, TS, PAST = 256, 64, 256
T = TP + TS
KD = DM // P
HEADS, NOPE, ROPE, VD, RANK = 8, 64, 32, 64, 256
MH, DH, CH = 4, 128, 64
NCH = T // CH
GW = 512
EXPERTS, GROUPS, PER_GROUP, DE = 16, 4, 4, 256
ALPHA = (2 * L) ** 0.25
EPS = 1e-5
ATT_SCALE = (NOPE + ROPE) ** -0.5
KSCALE = DH ** -0.5
NEG = -1e30
MROW = NOPE + ROPE
KATT = MROW + 2
KEYS = PAST + T
KH = KEYS // 2

WS = 64.0
XS = 4.0
UN = 1.0 / (WS * XS)
GS = 1024.0

SLOTS = 4
LEAD = 2
BLK = 8 * P
FRONT = 10
M0, MPER = FRONT, 8
A0, APER = M0 + MH * MPER, 8
B0 = A0 + 2 * APER
O0 = B0 + 12
U0 = O0 + KD
D0 = U0 + 4 * (EXPERTS + 1)
D1 = D0 + EXPERTS + 1
NB = D1 + EXPERTS + 1
assert NB % SLOTS == 0 and MPER % SLOTS == 0 and APER % SLOTS == 0

C_FRONT, C_MLSTM, C_GATE = 0, 6, 22
C_QG, C_KVG, C_L1G, C_L1B, C_L2G, C_L2B, NPAR = 46, 48, 50, 58, 66, 74, 82

TILES = [(0, P), (P, P), (2 * P, TS)]


class Signal:

    def __init__(self, ctx, nc, name, per, before=0):
        self.sem, self.per, self.before = ctx.enter_context(nc.semaphore(name)), per, before

    def value(self, layer, n):
        return layer * self.per + (self.before + n)


def build_trunk(nc, d):
    with ExitStack() as ctx:
        def sb(name, shape, dt=F32):
            return ctx.enter_context(nc.sbuf_tensor(name, shape, dt))

        def sig(name, per, before=0):
            return Signal(ctx, nc, name, per, before)

        w32 = sb("w32", [P, SLOTS, BLK])
        whi = sb("whi", [P, SLOTS, BLK], F16)
        wlo = sb("wlo", [P, SLOTS, BLK], F16)
        xT = sb("xT", [P, KD * T])
        xhi = sb("xhi", [P, KD, T], F16)
        xlo = sb("xlo", [P, KD, T], F16)
        acc = sb("acc", [P, KD * T])
        ysq = sb("ysq", [P, 4, T])
        br_hi = sb("br_hi", [P, 12 * T], F16)
        br_lo = sb("br_lo", [P, 12 * T], F16)
        arena_a = sb("arena_a", [P, 24 * T])
        arena_b = sb("arena_b", [P, 17 * T])
        gates = arena_a[:, :]
        hhi = arena_a[:, 0:17 * T].bitcast(F16)
        hlo = arena_b[:, :].bitcast(F16)
        mrow_m = arena_b[:, 0:4 * T]
        mrow_i = arena_b[:, 4 * T:8 * T]
        mrow_e = arena_b[:, 8 * T:12 * T]
        gvt = arena_b[:, 12 * T:12 * T + 3 * GW].rearrange("p (i n) -> p i n", i=3)
        mhi = arena_b[:, 0:4 * T].bitcast(F16).rearrange("p (n t) -> p n t", t=T)
        mlo = arena_b[:, 4 * T:8 * T].bitcast(F16).rearrange("p (n t) -> p n t", t=T)
        par = sb("par", [P, L * NPAR])
        par_c = sb("par_c", [P, NPAR])
        par_h = sb("par_h", [P, NPAR])
        par_x = sb("par_x", [P, NPAR])
        rows = sb("rows", [P, 4 * GW])
        ws_t = sb("ws_t", [P, 4 * P])
        c_init = sb("c_init", [P, MH * (DH + 1)])
        m_init = sb("m_init", [MH, L])
        rw = sb("rw", [P, KD, EXPERTS])
        rb = sb("rb", [P, 3, EXPERTS])
        cosT = sb("cosT", [P, T])
        sinT = sb("sinT", [P, T])
        ident = sb("ident", [P, P])
        ones = sb("ones", [P, P])
        ones_dm = sb("ones_dm", [P, P])
        eps_col = sb("eps_col", [P, 1])
        tri = sb("tri", [P, P])
        mmask = sb("mmask", [P, T])
        scan_keep = sb("scan_keep", [MH, T])
        head_sel = sb("head_sel", [MH, MH, P])
        att_mask = sb("att_mask", [MROW + 2, T + KEYS])[MROW:MROW + 2, :]
        bs_row = sb("bs_row", [1, 4 * P])
        exp_sel = sb("exp_sel", [P, EXPERTS * P], F16)
        rank4 = sb("rank4", [P, 3, GROUPS])
        rank16 = sb("rank16", [P, 3, EXPERTS])
        acc3 = acc[:, :].rearrange("p (n t) -> p n t", t=T)
        front3 = arena_a[:, :].rearrange("p (n t) -> p n t", t=T)
        zf = acc3[:, 0:6, :]
        rstd = acc3[:, 6:8, :]
        znorm = front3[:, 20:24, :]
        cache = arena_a[:, 0:2 * PAST]
        cq_hi = sb("cq_hi", [P, 2, T], F16)
        cq_lo = sb("cq_lo", [P, 2, T], F16)
        kv_hi = sb("kv_hi", [P, 2, KEYS], F16)
        kv_lo = sb("kv_lo", [P, 2, KEYS], F16)
        kv_out = front3[:, 16:18, :]
        kr_t = front3[0:ROPE, 18:20, :]
        kr = sb("kr", [MROW, KEYS])[NOPE:MROW, :]
        stat = sb("stat", [P, 3, 8])
        r_f = front3[0:MH, 8:12, :]
        r_b = front3[0:MH, 5, :]
        r_a = front3[0:MH, 6, :]
        r_m = front3[0:MH, 7, :]
        scan_drop = front3[0:MH, 4, :]
        r_x = front3[0:MH, 12:16, :]
        m_at = sb("m_at", [MH, 8])
        cols = sb("cols", [P, 6 * MH])
        mq = sb("mq", [P, T])
        mk = sb("mk", [P, T])
        mo = sb("mo", [P, T])
        gu = sb("gu", [P, T])
        k_tok = sb("k_tok", [P, 3, P])
        v_tok = sb("v_tok", [P, 3, P])
        v_ws = sb("v_ws", [P, 3, DH + 1])
        dec_w = sb("dec_w", [P, 3, P])
        att = sb("att", [P, 3, P])
        q_in = sb("q_in", [P, T])
        c_st = sb("c_st", [P, 6, DH + 1])
        n_bc = sb("n_bc", [P, 4, P])
        hden = sb("hden", [P, T])
        hout = sb("hout", [P, T])
        vg = sb("vg", [P, 3, P])
        gout = hden
        q_att = arena_b[:, 0:4 * T].rearrange("p (n t) -> p n t", t=T)
        qr_t = arena_b[:, 4 * T:6 * T].rearrange("p (n t) -> p n t", t=T)
        v_kv = arena_b[:, 6 * T:6 * T + 10 * P].rearrange("p (i n) -> p i n", i=5)
        k_att = acc[:, 0:4 * KEYS].rearrange("p (n t) -> p n t", t=KEYS)
        sm = sb("sm", [P, 8])
        mu_var = sb("mu_var", [P, 4 * T])
        prob = mu_var[:, 0:6 * P].rearrange("p (b n) -> p b n", b=2)
        prob_t = ysq[:, :, :].rearrange("p a t -> p (a t)")[:, 0:6 * P].rearrange(
            "p (b i n) -> p b i n", b=2, i=3)
        mtmp = (gu, mo)
        mu = mu_var[:, 0:2 * T].rearrange("p (n t) -> p n t", t=T)
        var = mu_var[:, 2 * T:4 * T].rearrange("p (n t) -> p n t", t=T)
        ln_r = q_in
        rt = sb("rt", [P, 10, 3, EXPERTS])
        rp = sb("rp", [P, 3 * GROUPS, 6])
        rg = sb("rg", [P, 8, 3, GROUPS])
        gate_hi = sb("gate_hi", [P, T], F16)
        gate_lo = sb("gate_lo", [P, T], F16)
        gate32 = hout[0:EXPERTS, :]
        ht, h1, h2 = mq, mk, mo

        bank = [ctx.enter_context(nc.psum_tensor(f"bank{i}", [P, 512], F32)) for i in range(8)]

        loaded = [sig(f"loaded{s}", 16 * NB // SLOTS) for s in range(SLOTS)]
        consts_in = sig("consts_in", 0)
        x_in = sig("x_in", 0)
        stored = sig("stored", 16 * (4 + 2 * MH))
        consts_set = sig("consts_set", 0)
        ws_masked = sig("ws_masked", 1)
        layer_in = sig("layer_in", 16 * 6)
        hi_done = sig("hi_done", NB)
        lo_done = sig("lo_done", NB)
        blk_done = sig("blk_done", NB)
        x_hi = sig("x_hi", 2 * KD, KD)
        x_split = sig("x_split", 2 * KD, KD)
        pars = sig("pars", 1)
        z_ev = sig("z_ev", 54)
        tokv = sig("tokv", 8)
        gv_act = sig("gv_act", 4)
        sq_c = sig("sq_c", 2)
        rms_ps = sig("rms_ps", 2)
        rms_std = sig("rms_std", 2)
        z_norm = sig("z_norm", 2)
        c_hi = sig("c_hi", 3)
        c_lo = sig("c_lo", 3)
        kr_done = sig("kr_done", 1)
        f_abs = sig("f_abs", 1)
        f_ln = sig("f_ln", 1)
        r_arg = sig("r_arg", 1)
        r_exp = sig("r_exp", 1)
        cols_ps = sig("cols_ps", 1)
        cols_sb = sig("cols_sb", 1)
        bc_ps = sig("bc_ps", 3 * MH)
        bc_m = sig("bc_m", MH)
        bc_ie = sig("bc_ie", 2 * MH)
        gv_std = sig("gv_std", 1)
        gv_var = sig("gv_var", 1)
        gv_done = sig("gv_done", 1)
        k_tr = sig("k_tr", MH)
        a_ps = sig("a_ps", MH)
        k_sb = sig("k_sb", MH)
        dec_done = sig("dec_done", MH)
        v_wsd = sig("v_wsd", MH)
        att_done = sig("att_done", MH)
        dc_ps = sig("dc_ps", MH)
        st_done = sig("st_done", MH)
        num_ps = sig("num_ps", MH)
        h_done = sig("h_done", MH)
        vg_done = sig("vg_done", MH)
        sp_ps = sig("sp_ps", MH)
        g_done = sig("g_done", MH)
        bc_hi = sig("bc_hi", 2 * MH)
        bc_lo = sig("bc_lo", 2 * MH)
        q_ev = sig("q_ev", 2)
        q_rot = sig("q_rot", 2)
        v_ev = sig("v_ev", 2)
        s_ps = sig("s_ps", 12)
        s_max = sig("s_max", 12)
        p_exp = sig("p_exp", 12)
        p_norm = sig("p_norm", 12)
        t_ps = sig("t_ps", 12)
        t_sb = sig("t_sb", 12)
        o_ps = sig("o_ps", 12)
        o_hi = sig("o_hi", 4)
        o_lo = sig("o_lo", 4)
        m_used = sig("m_used", 24)
        m_hi = sig("m_hi", KD)
        m_lo = sig("m_lo", KD)
        acc_pre = sig("acc_pre", 2)
        y_done = sig("y_done", 2 * KD)
        y_sq = sig("y_sq", 2 * KD)
        ln_ps = sig("ln_ps", 2 * KD)
        ln_mu = sig("ln_mu", 2)
        ln_var = sig("ln_var", 2)
        ln_std = sig("ln_std", 2)
        ln_t = sig("ln_t", 2 * KD)
        r_ps = sig("r_ps", 1)
        r_e = sig("r_e", 1)
        g_sel = sig("g_sel", 1)
        g_tr = sig("g_tr", 1)
        g_hi = sig("g_hi", 1)
        g_lo = sig("g_lo", 1)
        gb_ps = sig("gb_ps", EXPERTS)
        u_tanh = sig("u_tanh", 2 * (EXPERTS + 1))
        u_free = sig("u_free", 2 * (EXPERTS + 1))
        u_prod = sig("u_prod", 2 * (EXPERTS + 1))
        u_hi = sig("u_hi", 2 * (EXPERTS + 1))
        u_lo = sig("u_lo", 2 * (EXPERTS + 1))

        N_CONST = 15
        block = ctx.enter_context(nc.Block())

        @block.sync
        def _(sp):
            sp.dma_start(xT[:, :], d["x"]).then_inc(x_in.sem, 16)
            for s in range(SLOTS):
                sp.dma_start(w32[:, s, :], d["w"][s * P:(s + 1) * P, :]).then_inc(loaded[s].sem, 16)
            for dst, name in ((par[:, :], "par"), (ident[:, :], "ident"), (mmask[:, :], "mmask"),
                              (scan_keep[:, :], "scan_keep"), (m_init[:, :], "m_init"),
                              (head_sel[:, :, :], "head_sel"), (cosT[:, :], "cos"), (sinT[:, :], "sin"),
                              (tri[:, :], "tri"), (att_mask, "att_mask"),
                              (rw[:, :, :], "rw"), (exp_sel[:, :], "exp_sel"),
                              (rank4[:, :, :], "rank4"), (rank16[:, :, :], "rank16")):
                sp.dma_start(dst, d[name]).then_inc(consts_in.sem, 16)
            sp.dma_start(rb[:, :, :].rearrange("p a e -> p (a e)"),
                         d["rb"].partition_broadcast(P)).then_inc(consts_in.sem, 16)
            with sp.Fori(1, L * NB // SLOTS) as i:
                for s in range(SLOTS):
                    sp.wait_ge(lo_done.sem, i * SLOTS + (s + 1 - SLOTS))
                    sp.dma_start(w32[:, s, :], d["w"][bass.ds(i * (SLOTS * P) + s * P, P), :]
                                 ).then_inc(loaded[s].sem, 16)

        @block.gpsimd
        def _(pool):
            nc.gpsimd.memset(ones[:, :], 1.0).then_inc(consts_set.sem, 1)
            nc.gpsimd.memset(ones_dm[:, :], 1.0 / DM).then_inc(consts_set.sem, 1)
            nc.gpsimd.memset(eps_col[:, :], EPS).then_inc(consts_set.sem, 1)
            nc.gpsimd.memset(gate_hi[:, :], 0.0).then_inc(consts_set.sem, 1)
            nc.gpsimd.memset(gate_lo[:, :], 0.0).then_inc(consts_set.sem, 1)
            nc.gpsimd.memset(m_at[:, :], 0.0).then_inc(consts_set.sem, 1)
            nc.gpsimd.memset(stat[:, :, :], 1.0).then_inc(consts_set.sem, 1)

        N_SET = 7

        @block.scalar
        def _(act):
            A = nc.scalar.activation

            def hi_at(l, n, s):
                act.wait_ge(loaded[s].sem, l * loaded[s].per + (n + (SLOTS - s)) * (16 // SLOTS))
                act.wait_ge(blk_done.sem, l * NB + (n + (1 - SLOTS)))
                A(whi[:, s, :], w32[:, s, :], ACT.Copy, scale=WS).then_inc(hi_done.sem, 1)

            def ln_scalar(l, k, gain, bias):
                act.wait_ge(ln_ps.sem, ln_ps.value(l, KD * (k + 1)))
                A(mu[:, 0, :], bank[4 + 2 * k][:, 0:T], ACT.Copy)
                A(mu[:, 1, :], bank[4 + 2 * k][:, 0:T], ACT.Square).then_inc(ln_mu.sem, 1)
                act.wait_ge(ln_var.sem, ln_var.value(l, k + 1))
                A(var[:, 1, :], var[:, 0, :], ACT.Sqrt, bias=eps_col[:, 0:1]).then_inc(ln_std.sem, 1)
                for c in range(KD):
                    act.wait_ge(ln_t.sem, ln_t.value(l, KD * k + c + 1))
                    A(xT[:, c * T:(c + 1) * T], acc[:, c * T:(c + 1) * T], ACT.Identity,
                      scale=par_c[:, gain + c:gain + c + 1], bias=par_c[:, bias + c:bias + c + 1])
                    A(xhi[:, c, :], acc[:, c * T:(c + 1) * T], ACT.Identity,
                      scale=par_x[:, gain + c:gain + c + 1],
                      bias=par_x[:, bias + c:bias + c + 1]).then_inc(x_hi.sem, 1)

            def square(l, k, c):
                act.wait_ge(y_done.sem, y_done.value(l, KD * k + c + 1))
                if c >= 4:
                    act.wait_ge(ln_ps.sem, ln_ps.value(l, KD * k + c - 3))
                A(ysq[:, c % 4, :], acc[:, c * T:(c + 1) * T], ACT.Square).then_inc(y_sq.sem, 1)

            act.wait_ge(x_in.sem, 16)
            for c in range(KD):
                A(xhi[:, c, :], xT[:, c * T:(c + 1) * T], ACT.Copy, scale=XS).then_inc(x_hi.sem, 1)
            act.wait_ge(consts_set.sem, N_SET)
            act.wait_ge(consts_in.sem, 16 * N_CONST)

            with act.Fori(0, L) as l:
                def hi_first(n):
                    act.wait_ge(loaded[n].sem, loaded[n].value(l, 16))
                    A(whi[:, n, :], w32[:, n, :], ACT.Copy, scale=WS).then_inc(hi_done.sem, 1)

                def hi_lead(g):
                    n = g + LEAD
                    if n < SLOTS:
                        hi_first(n)
                    elif n < NB:
                        hi_at(l, n, n % SLOTS)

                act.wait_ge(x_split.sem, x_split.value(l, 0))
                W4 = MH * (DH + 1)
                for dst, src in ((cache, d["cache"][bass.ds(l * P, P), :]),
                                 (kr[:, 0:PAST], d["krope"][bass.ds(l * ROPE, ROPE), :]),
                                 (rows[:, :], d["rows"][bass.ds(l, 1), :].broadcast_to([P, 4 * GW])),
                                 (ws_t[:, :], d["ws_t"][bass.ds(l * P, P), :]),
                                 (bs_row[:, :], d["bs_row"][bass.ds(l, 1), :]),
                                 (c_init[:, :], d["c_init"][bass.ds(l * P, P), :])):
                    act.dma_start(dst, src).then_inc(layer_in.sem, 16)
                for n in range(LEAD):
                    hi_first(n)
                layer_par = par[:, bass.ds(l * NPAR, NPAR)]
                A(par_c[:, :], layer_par, ACT.Copy)
                A(par_h[:, :], layer_par, ACT.Copy, scale=0.5)
                A(par_x[:, :], layer_par, ACT.Copy, scale=XS).then_inc(pars.sem, 1)
                act.wait_ge(pars.sem, pars.value(l, 1))

                for g in range(6):
                    hi_lead(g)
                    act.wait_ge(blk_done.sem, blk_done.value(l, g + 1))
                    A(zf[:, g, :], bank[g % 4][:, 0:T], ACT.Identity, scale=UN,
                      bias=par_c[:, C_FRONT + g:C_FRONT + g + 1]).then_inc(z_ev.sem, 1)
                    if g == 1:
                        act.wait_ge(f_abs.sem, f_abs.value(l, 1))
                        A(r_f[:, 2, :], r_f[:, 1, :], ACT.Exp, scale=-1.0)
                        act.drain()
                        A(r_f[:, 3, :], r_f[:, 2, :], ACT.Ln, bias=1.0).then_inc(f_ln.sem, 1)
                    if g == 2:
                        act.wait_ge(layer_in.sem, layer_in.value(l, 96))
                        A(kv_hi[:, :, 0:PAST], cache.rearrange("p (k t) -> p k t", k=2), ACT.Copy,
                          scale=XS).then_inc(c_hi.sem, 1)
                    if g == 3:
                        act.wait_ge(z_ev.sem, z_ev.value(l, 3))
                        A(ysq[:, 0:2, :], zf[:, 1:3, :], ACT.Square).then_inc(sq_c.sem, 1)
                    if g == 5:
                        act.wait_ge(z_ev.sem, z_ev.value(l, 5))
                        A(ysq[:, 2:4, :], zf[:, 3:5, :], ACT.Square).then_inc(sq_c.sem, 1)
                for i in range(4):
                    hi_lead(6 + i)
                    if i == 1:
                        for k in range(2):
                            act.wait_ge(rms_ps.sem, rms_ps.value(l, k + 1))
                            A(rstd[:, k, :], bank[4 + k][:, 0:T], ACT.Sqrt, scale=DM / RANK,
                              bias=eps_col[:, 0:1]).then_inc(rms_std.sem, 1)
                        act.wait_ge(r_arg.sem, r_arg.value(l, 1))
                        A(r_x[:, 1:4, :], r_x[:, 1:4, :], ACT.Exp).then_inc(r_exp.sem, 1)
                    if i == 3:
                        act.wait_ge(z_norm.sem, z_norm.value(l, 2))
                        A(cq_hi[:, 0, :], znorm[:, 0, :], ACT.Copy, scale=par_x[:, C_QG:C_QG + 1])
                        A(cq_hi[:, 1, :], znorm[:, 1, :], ACT.Copy,
                          scale=par_x[:, C_QG + 1:C_QG + 2]).then_inc(c_hi.sem, 1)
                        act.wait_ge(stored.sem, stored.value(l, 0))
                        for c in range(2):
                            A(kv_out[:, c, :], znorm[:, 2 + c, :], ACT.Copy,
                              scale=par_c[:, C_KVG + c:C_KVG + c + 1])
                        A(kv_hi[:, 0, PAST:KEYS], znorm[:, 2, :], ACT.Copy,
                          scale=par_x[:, C_KVG:C_KVG + 1])
                        A(kv_hi[:, 1, PAST:KEYS], znorm[:, 3, :], ACT.Copy,
                          scale=par_x[:, C_KVG + 1:C_KVG + 2]).then_inc(c_hi.sem, 1)
                    act.wait_ge(tokv.sem, tokv.value(l, i + 1))
                    A(gvt[:, 0:2, i * P:(i + 1) * P], gvt[:, 0:2, i * P:(i + 1) * P], ACT.Gelu_apprx_tanh)
                    A(gvt[0:TS, 2, i * P:(i + 1) * P], gvt[0:TS, 2, i * P:(i + 1) * P],
                      ACT.Gelu_apprx_tanh).then_inc(gv_act.sem, 1)
                act.wait_ge(c_hi.sem, c_hi.value(l, 3))
                act.dma_start(d["ckv"][bass.ds(l * P, P), :],
                              kv_out[:, :, :].rearrange("p k t -> p (k t)")).then_inc(stored.sem, 16)
                act.wait_ge(kr_done.sem, kr_done.value(l, 1))
                act.dma_start(d["kr_out"][bass.ds(l * ROPE, ROPE), :],
                              kr[:, PAST:KEYS]).then_inc(stored.sem, 16)
                act.dma_start(d["m_out"][bass.ds(l * MH, MH), :], m_at[:, :]).then_inc(stored.sem, 16)
                for h in range(MH):
                    for j, dst in ((1, mrow_i), (2, mrow_e)):
                        n = 3 * h + j
                        act.wait_ge(bc_ps.sem, bc_ps.value(l, n + 1))
                        A(dst[:, h * T:(h + 1) * T], bank[4 + n % 4][:, 0:T], ACT.Copy
                          ).then_inc(bc_ie.sem, 1)
                act.wait_ge(gv_var.sem, gv_var.value(l, 1))
                A(stat[:, :, 2:3], stat[:, :, 1:2], ACT.Sqrt, bias=eps_col[:, 0:1]).then_inc(gv_std.sem, 1)
                act.wait_ge(gv_done.sem, gv_done.value(l, 1))
                act.dma_start(d["gv_out"][bass.ds(l * TS, TS), :], gvt[0:TS, 2, :]).then_inc(stored.sem, 16)

                with act.Fori(0, MH) as h:
                    g0 = h * MPER + M0

                    def evac(step, dst, func, par_t, col, scale=UN):
                        act.wait_ge(blk_done.sem, l * NB + g0 + (step + 1))
                        A(dst, bank[(M0 + step) % 4][:, 0:T], func, scale=scale,
                          bias=par_t[:, bass.ds(col, 1)]).then_inc(z_ev.sem, 1)

                    def hi_m(step):
                        hi_at(l, g0 + (step + LEAD), (M0 + step + LEAD) % SLOTS)

                    hi_m(0)
                    act.wait_ge(num_ps.sem, l * MH + h)
                    evac(0, mq[:, :], ACT.Identity, par_c, h * 4 + C_MLSTM)
                    hi_m(1)
                    evac(1, mk[:, :], ACT.Identity, par_c, h * 4 + (C_MLSTM + 1))
                    hi_m(2)
                    act.wait_ge(att_done.sem, l * MH + h)
                    act.wait_ge(cols_sb.sem, cols_sb.value(l, 1))
                    act.wait_ge(bc_m.sem, bc_m.value(l, MH))
                    for i, (t0, n) in enumerate(TILES):
                        a = A(dec_w[0:n, i, 0:n], mrow_m[0:n, bass.ds(h * T + t0, n)], ACT.Exp,
                              bias=cols[0:n, bass.ds(h + i * MH, 1)])
                    a.then_inc(dec_done.sem, 1)
                    act.wait_ge(k_tr.sem, l * MH + h + 1)
                    act.wait_ge(dc_ps.sem, l * MH + h)
                    A(k_tok[:, 0:2, :], bank[4][:, 0:2 * P].rearrange("p (i n) -> p i n", i=2), ACT.Copy)
                    A(k_tok[0:TS, 2, :], bank[4][0:TS, 2 * P:3 * P], ACT.Copy).then_inc(k_sb.sem, 1)
                    hi_m(3)
                    act.wait_ge(h_done.sem, l * MH + h)
                    evac(3, mo[:, :], ACT.Tanh, par_h, h * 4 + (C_MLSTM + 2), scale=UN / 2)
                    hi_m(4)
                    act.wait_ge(g_done.sem, l * MH + h)
                    evac(4, gu[:, :], ACT.Gelu_apprx_tanh, par_c, h * 4 + (C_MLSTM + 3))
                    for j in range(3):
                        hi_m(5 + j)
                        evac(5 + j, gates[:, bass.ds((h * 3 + j) * T, T)], ACT.Tanh, par_h,
                             h * 3 + (C_GATE + j), scale=UN / 2)
                    act.wait_ge(st_done.sem, l * MH + h + 1)
                    act.dma_start(d["c_prompt"][bass.ds((l * MH + h) * P, P), :], c_st[:, 3, :]
                                  ).then_inc(stored.sem, 16)
                    act.dma_start(d["c_sample"][bass.ds((l * MH + h) * P, P), :], c_st[:, 5, :]
                                  ).then_inc(stored.sem, 16)
                    act.wait_ge(h_done.sem, l * MH + h + 1)
                    A(br_hi[:, bass.ds((h + 4) * T, T)], hout[:, :], ACT.Copy, scale=XS / 2
                      ).then_inc(bc_hi.sem, 1)
                    act.wait_ge(g_done.sem, l * MH + h + 1)
                    A(br_hi[:, bass.ds((h + 8) * T, T)], gout[:, :], ACT.Copy, scale=XS
                      ).then_inc(bc_hi.sem, 1)

                with act.Fori(0, 2) as hf:
                    g0 = hf * APER + A0

                    def hi_a(step):
                        hi_at(l, g0 + (step + LEAD), (A0 + step + LEAD) % SLOTS)

                    hi_a(0)
                    act.wait_ge(blk_done.sem, l * NB + g0 + 1)
                    act.wait_ge(s_ps.sem, l * 12 + hf * 6)
                    for j in range(4):
                        r0 = NOPE * (j % 2)
                        a = A(q_att[0:NOPE, j, :], bank[4 + j // 2][r0:r0 + NOPE, 0:T], ACT.Copy,
                              scale=UN)
                    a.then_inc(q_ev.sem, 1)
                    hi_a(1)
                    act.wait_ge(blk_done.sem, l * NB + g0 + 2)
                    for j in range(4):
                        for r in range(2):
                            a = A(k_att[0:NOPE, 2 * (j // 2) + r, (j % 2) * KH:(j % 2 + 1) * KH],
                                  bank[j][NOPE * r:NOPE * (r + 1), 0:KH], ACT.Copy, scale=UN)
                        a.then_inc(z_ev.sem, 1)

                    def gate_tanh(j):
                        act.wait_ge(blk_done.sem, l * NB + g0 + (3 + j))
                        A(gates[:, bass.ds((hf * 6 + (12 + j)) * T, T)],
                          bank[(A0 + 2 + j) % 4][:, 0:T], ACT.Tanh, scale=UN / 2,
                          bias=par_h[:, bass.ds(hf * 6 + (C_GATE + 12 + j), 1)]).then_inc(z_ev.sem, 1)

                    def exps(j):
                        u = l * 12 + hf * 6 + j
                        act.wait_ge(s_max.sem, u + 1)
                        if j >= 2:
                            act.wait_ge(t_ps.sem, u - 1)
                        b = bank[4 + j % 2]
                        if j % 3 < 2:
                            A(prob[:, j % 2, 0:P], b[:, 0:P], ACT.Exp, scale=ATT_SCALE,
                              bias=sm[:, 2:3], accum_out=sm[:, 4:5])
                            A(prob[:, j % 2, P:3 * P], b[:, P:3 * P], ACT.Exp, scale=ATT_SCALE,
                              bias=sm[:, 3:4], accum_out=sm[:, 5:6]).then_inc(p_exp.sem, 1)
                        else:
                            A(prob[:, j % 2, 0:T], b[:, 0:T], ACT.Exp, scale=ATT_SCALE,
                              bias=sm[:, 2:3], accum_out=sm[:, 4:5]).then_inc(p_exp.sem, 1)

                    def probs_out(j):
                        u = l * 12 + hf * 6 + j
                        act.wait_ge(t_ps.sem, u + 1)
                        if j >= 2:
                            act.wait_ge(o_ps.sem, u - 1)
                        if j % 3 < 2:
                            A(prob_t[:, j % 2, :, :], bank[6][:, 0:3 * P].rearrange(
                                "p (i n) -> p i n", i=3), ACT.Copy).then_inc(t_sb.sem, 1)
                        else:
                            A(prob_t[:, j % 2, 0:2, :], bank[6][:, 0:2 * P].rearrange(
                                "p (i n) -> p i n", i=2), ACT.Copy)
                            A(prob_t[0:TS, j % 2, 2, :], bank[6][0:TS, 2 * P:3 * P], ACT.Copy
                              ).then_inc(t_sb.sem, 1)

                    def out_hi(p):
                        act.wait_ge(o_ps.sem, l * 12 + hf * 6 + (3 * p + 3))
                        A(br_hi[:, bass.ds((hf * 2 + p) * T, T)], bank[7][:, 0:T], ACT.Copy,
                          scale=XS).then_inc(o_hi.sem, 1)

                    for j in range(6):
                        hi_a(2 + j)
                        if j:
                            gate_tanh(j - 1)
                        if j == 5:
                            out_hi(0)
                        exps(j)
                        if j:
                            probs_out(j - 1)
                    gate_tanh(5)
                    probs_out(5)
                    out_hi(1)

                with act.Fori(0, 3) as k:
                    for j in range(4):
                        hi_at(l, k * 4 + (B0 + j + LEAD), (B0 + j + LEAD) % SLOTS)
                act.wait_ge(m_used.sem, m_used.value(l, 24))
                for c in range(KD):
                    A(mhi[:, c, :], acc[:, c * T:(c + 1) * T], ACT.Copy, scale=UN * XS / 2
                      ).then_inc(m_hi.sem, 1)
                act.wait_ge(m_lo.sem, m_lo.value(l, KD))
                A(acc[:, :], xT[:, :], ACT.Copy, scale=ALPHA).then_inc(acc_pre.sem, 1)

                for c in range(KD):
                    hi_lead(O0 + c)
                    square(l, 0, c)
                ln_scalar(l, 0, C_L1G, C_L1B)
                act.drain()
                A(acc[:, :], xT[:, :], ACT.Copy, scale=ALPHA).then_inc(acc_pre.sem, 1)

                UPB = [(U0 + j) % 4 for j in range(4)]
                UE = 2 * (EXPERTS + 1)

                hi_lead(U0)
                act.wait_ge(r_ps.sem, r_ps.value(l, 1))
                A(rt[:, 0, :, :], bank[7][:, 0:3 * EXPERTS].rearrange("p (i e) -> p i e", i=3), ACT.Exp,
                  scale=-1.0).then_inc(r_e.sem, 1)
                hi_lead(U0 + 1)
                for f in range(2):
                    act.wait_ge(blk_done.sem, blk_done.value(l, U0 + 2 * f + 1))
                    if f:
                        hi_lead(U0 + 2)
                        hi_lead(U0 + 3)
                        act.wait_ge(u_free.sem, u_free.value(l, f))
                    A(ht[:, :], bank[UPB[2 * f]][:, 0:T], ACT.Tanh, scale=UN / 2).then_inc(u_tanh.sem, 1)
                    act.wait_ge(u_prod.sem, u_prod.value(l, f + 1))
                    A(hhi[:, f * T:(f + 1) * T], h2[:, :], ACT.Copy, scale=UN * UN * XS / 2
                      ).then_inc(u_hi.sem, 1)
                act.wait_ge(g_tr.sem, g_tr.value(l, 1))
                A(gate32[:, 0:TP], bank[6][0:EXPERTS, 0:TP], ACT.Copy, scale=GS)
                A(gate32[:, TP:T], bank[6][0:EXPERTS, 3 * P - TS:3 * P], ACT.Copy, scale=GS)
                A(gate_hi[0:EXPERTS, 0:TP], bank[6][0:EXPERTS, 0:TP], ACT.Copy, scale=GS)
                A(gate_hi[0:EXPERTS, TP:T], bank[6][0:EXPERTS, 3 * P - TS:3 * P], ACT.Copy, scale=GS
                  ).then_inc(g_hi.sem, 1)

                with act.Fori(0, EXPERTS) as e:
                    g0 = e * 4 + (U0 + 4)
                    for f in range(2):
                        hi_at(l, g0 + (2 * f + LEAD), (U0 + 2 * f + LEAD) % SLOTS)
                        hi_at(l, g0 + (2 * f + 1 + LEAD), (U0 + 2 * f + 1 + LEAD) % SLOTS)
                        n = l * UE + e * 2 + (2 + f)
                        act.wait_ge(blk_done.sem, l * NB + g0 + (2 * f + 1))
                        act.wait_ge(u_free.sem, n)
                        A(ht[:, :], bank[UPB[2 * f]][:, 0:T], ACT.Tanh, scale=UN / 2
                          ).then_inc(u_tanh.sem, 1)
                        act.wait_ge(u_prod.sem, n + 1)
                        A(hhi[:, bass.ds((e * 2 + (2 + f)) * T, T)], h2[:, :], ACT.Copy,
                          scale=UN * UN * XS / (2 * GS)).then_inc(u_hi.sem, 1)

                hi_lead(D0)
                with act.Fori(0, 4) as i:
                    for j in range(4):
                        hi_at(l, i * 4 + (D0 + 1 + j + LEAD), (D0 + 1 + j + LEAD) % SLOTS)
                hi_lead(D1)
                for c in range(4):
                    square(l, 1, c)
                with act.Fori(0, 3) as i:
                    for j in range(4):
                        hi_at(l, i * 4 + (D1 + 1 + j + LEAD), (D1 + 1 + j + LEAD) % SLOTS)
                for j in range(4):
                    hi_lead(D1 + 13 + j)
                for c in range(4, KD):
                    square(l, 1, c)
                ln_scalar(l, 1, C_L2G, C_L2B)

            act.wait_ge(x_hi.sem, x_hi.value(L, 0))
            act.dma_start(d["y"], xT[:, :]).then_inc(stored.sem, 16)
            act.wait_ge(stored.sem, stored.value(L, 16))

        @block.vector
        def _(dve):
            V = nc.vector

            def lo_at(l, n, s):
                dve.wait_ge(hi_done.sem, l * NB + (n + 1))
                V.scalar_tensor_tensor(wlo[:, s, :], w32[:, s, :], WS, whi[:, s, :], ALU.mult,
                                       ALU.subtract).then_inc(lo_done.sem, 1)

            def ln_vector(l, k):
                dve.wait_ge(ln_mu.sem, ln_mu.value(l, k + 1))
                V.tensor_tensor(var[:, 0, :], bank[5 + 2 * k][:, 0:T], mu[:, 1, :], ALU.subtract)
                dve.drain()
                V.tensor_scalar(var[:, 0, :], var[:, 0, :], 0.0, None, ALU.max).then_inc(ln_var.sem, 1)
                y = [acc[:, c * T:(c + 1) * T] for c in range(KD)]
                V.tensor_tensor(y[0], y[0], mu[:, 0, :], ALU.subtract)
                dve.wait_ge(ln_std.sem, ln_std.value(l, k + 1))
                V.reciprocal(ln_r[:, :], var[:, 1, :])

                def split(c):
                    dve.wait_ge(x_hi.sem, x_hi.value(l, KD * k + c + 1))
                    V.scalar_tensor_tensor(xlo[:, c, :], xT[:, c * T:(c + 1) * T], XS, xhi[:, c, :],
                                           ALU.mult, ALU.subtract).then_inc(x_split.sem, 1)

                for c in range(KD):
                    dve.drain()
                    V.tensor_tensor(y[c], y[c], ln_r[:, :], ALU.mult).then_inc(ln_t.sem, 1)
                    if c + 1 < KD:
                        V.tensor_tensor(y[c + 1], y[c + 1], mu[:, 0, :], ALU.subtract)
                    if c:
                        split(c - 1)
                split(KD - 1)

            def residual(l, k, c, b):
                V.scalar_tensor_tensor(acc[:, c * T:(c + 1) * T], bank[b][:, 0:T], UN,
                                       acc[:, c * T:(c + 1) * T], ALU.mult, ALU.add
                                       ).then_inc(y_done.sem, 1)

            for c in range(KD):
                dve.wait_ge(x_hi.sem, c + 1)
                V.scalar_tensor_tensor(xlo[:, c, :], xT[:, c * T:(c + 1) * T], XS, xhi[:, c, :],
                                       ALU.mult, ALU.subtract).then_inc(x_split.sem, 1)
            dve.wait_ge(consts_set.sem, N_SET)
            dve.wait_ge(consts_in.sem, 16 * N_CONST)

            with dve.Fori(0, L) as l:
                def lo_lead(g):
                    n = g + LEAD
                    if n < NB:
                        lo_at(l, n, n % SLOTS)

                lo_at(l, 0, 0)
                lo_at(l, 1, 1)
                dve.wait_ge(stored.sem, stored.value(l, 0))
                V.tensor_scalar(scan_drop, scan_keep[:, :], -1.0, -NEG, ALU.add, ALU.mult)
                V.tensor_copy(m_at[:, 5:6], m_init[:, bass.ds(l, 1)])

                lo_lead(0)
                dve.wait_ge(z_ev.sem, z_ev.value(l, 1))
                V.tensor_copy(r_f[:, 0, :], zf[32:32 + MH, 0, :])
                dve.drain()
                V.scalar_tensor_tensor(r_f[:, 1, :], r_f[:, 0, :], -1.0, r_f[:, 0, :], ALU.mult, ALU.max
                                       ).then_inc(f_abs.sem, 1)
                lo_lead(1)
                lo_lead(2)
                dve.wait_ge(f_ln.sem, f_ln.value(l, 1))
                V.scalar_tensor_tensor(r_f[:, 0, :], r_f[:, 0, :], 0.0, r_f[:, 3, :], ALU.min,
                                       ALU.subtract)
                dve.drain()
                V.tensor_tensor_scan(r_b, scan_keep[:, :], r_f[:, 0, :], 0.0, ALU.mult, ALU.add)
                dve.drain()
                V.tensor_tensor(r_a, zf[0:MH, 0, :], r_b, ALU.subtract)
                dve.drain()
                V.tensor_tensor_scan(r_m, scan_drop, r_a, 0.0, ALU.add, ALU.max)
                lo_lead(3)
                dve.wait_ge(c_hi.sem, c_hi.value(l, 1))
                V.scalar_tensor_tensor(kv_lo[:, :, 0:PAST], cache.rearrange("p (k t) -> p k t", k=2),
                                       XS, kv_hi[:, :, 0:PAST], ALU.mult, ALU.subtract
                                       ).then_inc(c_lo.sem, 1)
                ws3 = ws_t[:, :].rearrange("p (n t) -> p n t", t=P)
                V.tensor_tensor(ws3, ws3, tri[:, :].unsqueeze(1).broadcast_to([P, 4, P]), ALU.mult
                                ).then_inc(ws_masked.sem, 1)
                for c in range(NCH):
                    s = c if c < 4 else 5
                    e = (c + 1) * CH - 1
                    dve.drain()
                    V.scalar_tensor_tensor(m_at[:, s + 1:s + 2], r_m[:, e:e + 1], m_at[:, s:s + 1],
                                           r_b[:, e:e + 1], ALU.max, ALU.add)
                dve.drain()
                m_p = m_at[:, 0:4].unsqueeze(2).broadcast_to([MH, 4, CH])
                rm_p = r_m[:, 0:TP].rearrange("p (c t) -> p c t", t=CH)
                V.tensor_tensor(rm_p, rm_p, m_p, ALU.max)
                V.tensor_scalar(r_m[:, TP:T], r_m[:, TP:T], m_at[:, 5:6], None, ALU.max)
                dve.drain()
                V.tensor_scalar(r_x[:, 0, :], r_m, -1.0, None, ALU.mult)
                dve.drain()

                def chunks(ap):
                    return ap.rearrange("p (c t) -> p c t", t=CH)

                V.tensor_tensor(chunks(r_x[:, 1, 0:TP]), chunks(r_x[:, 0, 0:TP]), m_p, ALU.add)
                V.tensor_scalar(r_x[:, 1, TP:T], r_x[:, 0, TP:T], m_at[:, 5:6], None, ALU.add)
                V.tensor_tensor(r_x[:, 2, :], r_x[:, 0, :], r_b, ALU.subtract)
                V.tensor_tensor(chunks(r_x[:, 3, :]), chunks(r_a),
                                chunks(r_x[:, 0, :])[:, :, CH - 1:CH].broadcast_to([MH, NCH, CH]),
                                ALU.add).then_inc(r_arg.sem, 1)
                lo_lead(4)
                lo_lead(5)
                dve.wait_ge(z_ev.sem, z_ev.value(l, 6))
                V.tensor_tensor(kr_t[:, 0, :], zf[0:ROPE, 5, :], cosT[0:ROPE, :], ALU.mult)
                V.tensor_tensor(kr_t[:, 1, :], zf[ROPE:2 * ROPE, 5, :], sinT[ROPE:2 * ROPE, :], ALU.mult)
                dve.drain()
                V.tensor_tensor(kr[:, PAST:KEYS], kr_t[:, 0, :], kr_t[:, 1, :], ALU.add
                                ).then_inc(kr_done.sem, 1)

                def tok_out(b, dst2, dst1, row, last):
                    V.scalar_tensor_tensor(dst2, bank[b][:, 0:2 * P].rearrange("p (i n) -> p i n", i=2),
                                           UN, row.unsqueeze(1).broadcast_to([P, 2, P]), ALU.mult,
                                           ALU.add)
                    V.scalar_tensor_tensor(dst1, bank[b][0:TS, 2 * P:3 * P], UN, row[0:TS, :],
                                           ALU.mult, ALU.add).then_inc(last.sem, 1)

                for i in range(4):
                    lo_lead(6 + i)
                    if i == 1:
                        for k in range(2):
                            dve.wait_ge(rms_std.sem, rms_std.value(l, k + 1))
                            V.reciprocal(rstd[:, k, :], rstd[:, k, :])
                            dve.drain()
                            V.tensor_tensor(znorm[:, 2 * k:2 * k + 2, :], zf[:, 1 + 2 * k:3 + 2 * k, :],
                                            rstd[:, k:k + 1, :].broadcast_to([P, 2, T]), ALU.mult
                                            ).then_inc(z_norm.sem, 1)
                    dve.wait_ge(blk_done.sem, blk_done.value(l, 7 + i))
                    tok_out((6 + i) % 4, gvt[:, 0:2, i * P:(i + 1) * P],
                            gvt[0:TS, 2, i * P:(i + 1) * P],
                            rows[:, i * P:(i + 1) * P], tokv)
                dve.wait_ge(c_hi.sem, c_hi.value(l, 2))
                V.scalar_tensor_tensor(cq_lo[:, 0, :], znorm[:, 0, :], par_x[:, C_QG:C_QG + 1],
                                       cq_hi[:, 0, :], ALU.mult, ALU.subtract)
                V.scalar_tensor_tensor(cq_lo[:, 1, :], znorm[:, 1, :], par_x[:, C_QG + 1:C_QG + 2],
                                       cq_hi[:, 1, :], ALU.mult, ALU.subtract).then_inc(c_lo.sem, 1)
                dve.wait_ge(c_hi.sem, c_hi.value(l, 3))
                V.scalar_tensor_tensor(kv_lo[:, 0, PAST:KEYS], znorm[:, 2, :],
                                       par_x[:, C_KVG:C_KVG + 1], kv_hi[:, 0, PAST:KEYS], ALU.mult,
                                       ALU.subtract)
                V.scalar_tensor_tensor(kv_lo[:, 1, PAST:KEYS], znorm[:, 3, :],
                                       par_x[:, C_KVG + 1:C_KVG + 2], kv_hi[:, 1, PAST:KEYS], ALU.mult,
                                       ALU.subtract).then_inc(c_lo.sem, 1)
                dve.wait_ge(cols_ps.sem, cols_ps.value(l, 1))
                V.tensor_copy(cols[:, 0:2 * MH], bank[7][:, 0:2 * MH])
                V.tensor_copy(cols[0:TS, 2 * MH:3 * MH], bank[7][0:TS, 2 * MH:3 * MH])
                V.tensor_scalar(cols[:, 3 * MH:5 * MH], bank[7][:, 3 * MH:5 * MH], KSCALE, None, ALU.mult)
                V.tensor_scalar(cols[0:TS, 5 * MH:6 * MH], bank[7][0:TS, 5 * MH:6 * MH], KSCALE, None,
                                ALU.mult).then_inc(cols_sb.sem, 1)
                for h in range(MH):
                    n = 3 * h
                    dve.wait_ge(bc_ps.sem, bc_ps.value(l, n + 1))
                    V.tensor_tensor(mrow_m[:, h * T:(h + 1) * T], bank[4 + n % 4][:, 0:T], mmask[:, :],
                                    ALU.add).then_inc(bc_m.sem, 1)
                dve.wait_ge(gv_act.sem, gv_act.value(l, 4))
                for i, (t0, n) in enumerate(TILES):
                    V.bn_stats(rp[0:n, i, :], gvt[0:n, i, :])
                dve.drain()
                for i, (t0, n) in enumerate(TILES):
                    a = V.bn_aggr(stat[0:n, i, 0:2], rp[0:n, i, :])
                a.then_inc(gv_var.sem, 1)
                dve.wait_ge(gv_std.sem, gv_std.value(l, 1))
                V.reciprocal(stat[:, :, 3:4], stat[:, :, 2:3])
                dve.drain()
                gain = rows[:, 2 * GW:3 * GW]
                bias = rows[:, 3 * GW:4 * GW]
                for i, (t0, n) in enumerate(TILES):
                    V.tensor_scalar(gvt[0:n, i, :], gvt[0:n, i, :], stat[0:n, i, 0:1],
                                    stat[0:n, i, 3:4], ALU.subtract, ALU.mult)
                dve.drain()
                for i, (t0, n) in enumerate(TILES):
                    V.tensor_tensor(gvt[0:n, i, :], gvt[0:n, i, :], gain[0:n, :], ALU.mult)
                dve.drain()
                for i, (t0, n) in enumerate(TILES):
                    a = V.tensor_tensor(gvt[0:n, i, :], gvt[0:n, i, :], bias[0:n, :], ALU.add)
                a.then_inc(gv_done.sem, 1)

                with dve.Fori(0, MH) as h:
                    g0 = h * MPER + M0

                    def lo_m(step):
                        lo_at(l, g0 + (step + LEAD), (M0 + step + LEAD) % SLOTS)

                    lo_m(0)
                    lo_m(1)
                    dve.wait_ge(z_ev.sem, l * z_ev.per + h * 7 + 7)
                    dve.wait_ge(bc_ie.sem, bc_ie.value(l, 2 * MH))
                    V.tensor_tensor(q_in[:, :], mq[:, :], mrow_i[:, bass.ds(h * T, T)], ALU.mult)
                    lo_m(2)
                    dve.wait_ge(blk_done.sem, l * NB + g0 + 3)
                    tok_out((M0 + 2) % 4, v_tok[:, 0:2, :], v_tok[0:TS, 2, :],
                            rows[:, bass.ds(h * P + GW, P)], tokv)
                    dve.drain()
                    for i, (t0, n) in enumerate(TILES):
                        w = cols[0:n, bass.ds(h + (3 + i) * MH, 1)]
                        V.tensor_scalar(v_ws[0:n, i, 0:DH], v_tok[0:n, i, :], w, None, ALU.mult)
                        a = V.tensor_copy(v_ws[0:n, i, DH:DH + 1], w)
                    a.then_inc(v_wsd.sem, 1)
                    dve.wait_ge(dec_done.sem, l * MH + h + 1)
                    dve.wait_ge(a_ps.sem, l * MH + h + 1)
                    V.scalar_tensor_tensor(att[:, 0:2, :], bank[5][:, 0:2 * P].rearrange(
                        "p (i n) -> p i n", i=2), KSCALE, dec_w[:, 0:2, :], ALU.mult, ALU.mult)
                    V.scalar_tensor_tensor(att[0:TS, 2, 0:TS], bank[5][0:TS, 2 * P:2 * P + TS], KSCALE,
                                           dec_w[0:TS, 2, 0:TS], ALU.mult, ALU.mult
                                           ).then_inc(att_done.sem, 1)
                    lo_m(3)
                    dve.wait_ge(dc_ps.sem, l * MH + h + 1)
                    dve.wait_ge(stored.sem, l * stored.per + h * 32 + 64)

                    def decay(c):
                        return mrow_i[:, bass.ds(h * T + (c * CH + CH - 1), 1)]

                    W1 = DH + 1
                    V.tensor_copy(c_st[:, 4, :], c_init[:, bass.ds(h * W1, W1)])
                    V.tensor_copy(c_st[:, 0, :], bank[6][:, 0:W1])
                    dve.drain()
                    V.scalar_tensor_tensor(c_st[:, 5, :], c_st[:, 4, :], decay(4),
                                           bank[6][:, 2 * W1:3 * W1], ALU.mult, ALU.add)
                    V.scalar_tensor_tensor(c_st[:, 1, :], c_st[:, 0, :], decay(1),
                                           bank[7][:, 0:W1], ALU.mult, ALU.add)
                    dve.drain()
                    V.scalar_tensor_tensor(c_st[:, 2, :], c_st[:, 1, :], decay(2),
                                           bank[6][:, W1:2 * W1], ALU.mult, ALU.add)
                    dve.drain()
                    V.scalar_tensor_tensor(c_st[:, 3, :], c_st[:, 2, :], decay(3),
                                           bank[7][:, W1:2 * W1], ALU.mult, ALU.add)
                    for j, c in enumerate((0, 1, 2, 4)):
                        a = V.tensor_scalar(n_bc[:, j, :], ones[:, :], c_st[:, c, DH:DH + 1], None,
                                            ALU.mult)
                    a.then_inc(st_done.sem, 1)
                    lo_m(4)
                    dve.wait_ge(sp_ps.sem, l * MH + h)
                    V.tensor_copy(vg[:, 0:2, :], gvt[:, 0:2, bass.ds(h * P, P)])
                    V.tensor_copy(vg[0:TS, 2, :], gvt[0:TS, 2, bass.ds(h * P, P)]).then_inc(vg_done.sem, 1)
                    lo_m(5)
                    dve.wait_ge(num_ps.sem, l * MH + h + 1)
                    dve.wait_ge(z_ev.sem, l * z_ev.per + h * 7 + 9)
                    V.tensor_scalar(hden[:, :], bank[5][:, 0:T], -1.0, None, ALU.mult)
                    dve.drain()
                    V.tensor_tensor(hden[:, :], hden[:, :], bank[5][:, 0:T], ALU.max)
                    dve.drain()
                    V.tensor_tensor(hden[:, :], hden[:, :], mrow_e[:, bass.ds(h * T, T)], ALU.max)
                    dve.drain()
                    V.reciprocal(hden[:, :], hden[:, :])
                    dve.drain()
                    V.scalar_tensor_tensor(hout[:, :], mo[:, :], 1.0, hden[:, :], ALU.add, ALU.mult)
                    dve.drain()
                    V.tensor_tensor(hout[:, :], hout[:, :], bank[4][:, 0:T], ALU.mult
                                    ).then_inc(h_done.sem, 1)
                    lo_m(6)
                    dve.wait_ge(sp_ps.sem, l * MH + h + 1)
                    dve.wait_ge(z_ev.sem, l * z_ev.per + h * 7 + 10)
                    V.tensor_tensor(gout[:, :], gu[:, :], bank[6][:, 0:T], ALU.mult
                                    ).then_inc(g_done.sem, 1)
                    lo_m(7)
                    dve.wait_ge(bc_hi.sem, l * 2 * MH + h * 2 + 1)
                    V.scalar_tensor_tensor(br_lo[:, bass.ds((h + 4) * T, T)], hout[:, :], XS / 2,
                                           br_hi[:, bass.ds((h + 4) * T, T)], ALU.mult, ALU.subtract
                                           ).then_inc(bc_lo.sem, 1)
                    dve.wait_ge(bc_hi.sem, l * 2 * MH + h * 2 + 2)
                    V.scalar_tensor_tensor(br_lo[:, bass.ds((h + 8) * T, T)], gout[:, :], XS,
                                           br_hi[:, bass.ds((h + 8) * T, T)], ALU.mult, ALU.subtract
                                           ).then_inc(bc_lo.sem, 1)

                dve.wait_ge(num_ps.sem, num_ps.value(l, MH))
                V.tensor_copy(q_att[MROW:KATT, :, :],
                              att_mask[:, 0:T].unsqueeze(1).broadcast_to([2, 4, T]))
                V.tensor_copy(k_att[MROW:KATT, :, :],
                              att_mask[:, T:T + KEYS].unsqueeze(1).broadcast_to([2, 4, KEYS]))
                V.tensor_copy(k_att[NOPE:MROW, :, :],
                              kr.unsqueeze(1).broadcast_to([ROPE, 4, KEYS]))
                with dve.Fori(0, 2) as hf:
                    g0 = hf * APER + A0

                    def lo_a(step):
                        lo_at(l, g0 + (step + LEAD), (A0 + step + LEAD) % SLOTS)

                    lo_a(0)
                    dve.wait_ge(s_ps.sem, l * 12 + hf * 6)
                    dve.wait_ge(blk_done.sem, l * NB + g0 + 1)
                    V.scalar_tensor_tensor(qr_t[:, 0, :], bank[6][:, 0:T], UN, cosT[:, :], ALU.mult,
                                           ALU.mult)
                    V.scalar_tensor_tensor(qr_t[:, 1, :], bank[7][:, 0:T], UN, sinT[:, :], ALU.mult,
                                           ALU.mult)
                    dve.drain()
                    for j in range(4):
                        rs = slice(ROPE * j, ROPE * (j + 1))
                        a = V.tensor_tensor(q_att[NOPE:MROW, j, :], qr_t[rs, 0, :], qr_t[rs, 1, :],
                                            ALU.add)
                    a.then_inc(q_rot.sem, 1)
                    lo_a(1)
                    dve.wait_ge(blk_done.sem, l * NB + g0 + 2)
                    for j in range(2):
                        V.tensor_scalar(v_kv[:, 2 * j:2 * j + 2, :], bank[4 + j][:, :].rearrange(
                            "p (i n) -> p i n", i=2), UN, None, ALU.mult)
                    V.tensor_scalar(v_kv[0:TS, 4, :], bank[6][0:TS, 0:2 * P], UN, None, ALU.mult
                                    ).then_inc(v_ev.sem, 1)

                    def out_lo(p):
                        dve.wait_ge(o_hi.sem, l * 4 + hf * 2 + (p + 1))
                        V.scalar_tensor_tensor(br_lo[:, bass.ds((hf * 2 + p) * T, T)],
                                               bank[7][:, 0:T], XS,
                                               br_hi[:, bass.ds((hf * 2 + p) * T, T)], ALU.mult,
                                               ALU.subtract).then_inc(o_lo.sem, 1)

                    for j in range(6):
                        lo_a(2 + j)
                        if j == 5:
                            out_lo(0)
                        u = l * 12 + hf * 6 + j
                        b = bank[4 + j % 2]
                        dve.wait_ge(s_ps.sem, u + 1)
                        w = 2 if j % 3 < 2 else 1
                        if w == 2:
                            V.tensor_reduce(sm[:, 0:1], b[:, 0:P], AXX, ALU.max)
                            V.tensor_reduce(sm[:, 1:2], b[:, P:3 * P], AXX, ALU.max)
                        else:
                            V.tensor_reduce(sm[:, 0:1], b[:, 0:T], AXX, ALU.max)
                        dve.drain()
                        V.tensor_scalar(sm[:, 2:2 + w], sm[:, 0:w], -ATT_SCALE, None, ALU.mult
                                        ).then_inc(s_max.sem, 1)
                        dve.wait_ge(p_exp.sem, u + 1)
                        V.reciprocal(sm[:, 6:6 + w], sm[:, 4:4 + w])
                        dve.drain()
                        if w == 2:
                            V.tensor_scalar(prob[:, j % 2, 0:P], prob[:, j % 2, 0:P], sm[:, 6:7], None,
                                            ALU.mult)
                            V.tensor_scalar(prob[:, j % 2, P:3 * P], prob[:, j % 2, P:3 * P],
                                            sm[:, 7:8], None, ALU.mult).then_inc(p_norm.sem, 1)
                        else:
                            V.tensor_scalar(prob[:, j % 2, 0:T], prob[:, j % 2, 0:T], sm[:, 6:7], None,
                                            ALU.mult).then_inc(p_norm.sem, 1)
                    out_lo(1)

                V.memset(acc[:, :], 0.0)
                with dve.Fori(0, 3) as k:
                    for j in range(4):
                        lo_at(l, k * 4 + (B0 + j + LEAD), (B0 + j + LEAD) % SLOTS)
                        dve.wait_ge(blk_done.sem, l * NB + k * 4 + (B0 + j + 1))
                        dve.wait_ge(z_ev.sem, z_ev.value(l, 54))
                        for i in range(2):
                            c = 2 * j + i
                            V.scalar_tensor_tensor(mtmp[c % 2][:, :], gates[:, bass.ds((k * 8 + c) * T, T)], 1.0,
                                                   bank[c % 4][:, 0:T], ALU.add, ALU.mult)
                            dve.drain()
                            V.tensor_tensor(acc[:, c * T:(c + 1) * T], acc[:, c * T:(c + 1) * T],
                                            mtmp[c % 2][:, :], ALU.add).then_inc(m_used.sem, 1)
                for c in range(KD):
                    dve.wait_ge(m_hi.sem, m_hi.value(l, c + 1))
                    V.scalar_tensor_tensor(mlo[:, c, :], acc[:, c * T:(c + 1) * T], UN * XS / 2,
                                           mhi[:, c, :], ALU.mult, ALU.subtract).then_inc(m_lo.sem, 1)

                for c in range(KD):
                    lo_lead(O0 + c)
                    dve.wait_ge(acc_pre.sem, acc_pre.value(l, 1))
                    dve.wait_ge(blk_done.sem, blk_done.value(l, O0 + c + 1))
                    residual(l, 0, c, (O0 + c) % 4)
                ln_vector(l, 0)

                UPB = [(U0 + j) % 4 for j in range(4)]
                UE = 2 * (EXPERTS + 1)
                lo_lead(U0)
                dve.wait_ge(r_e.sem, r_e.value(l, 1))
                S, SB, SM, EQ, KY, O1, O2 = range(1, 8)
                V.tensor_scalar(rt[:, S], rt[:, 0], 1.0, None, ALU.add)
                dve.drain()
                V.reciprocal(rt[:, S], rt[:, S])
                dve.drain()
                V.tensor_tensor(rt[:, SB], rt[:, S], rb[:, :, :], ALU.add)
                dve.drain()
                v4 = rt[:, SB].rearrange("p i (g q) -> p (i g) q", q=PER_GROUP)
                for n, (a, b) in enumerate(((0, 1), (0, 2), (0, 3), (1, 2), (1, 3), (2, 3))):
                    V.tensor_tensor(rp[:, :, n:n + 1], v4[:, :, a:a + 1], v4[:, :, b:b + 1], ALU.add)
                dve.drain()
                lo_lead(U0 + 1)

                def g3(n):
                    return rg[:, n]

                V.tensor_reduce(g3(0).rearrange("p i g -> p (i g)"), rp[:, :, :], AXX, ALU.max)
                dve.drain()
                V.tensor_reduce(rg[:, 1, :, 0:1], g3(0), AXX, ALU.max)
                dve.drain()
                V.tensor_tensor(g3(2), g3(0), rg[:, 1, :, 0:1].broadcast_to([P, 3, GROUPS]), ALU.is_equal)
                dve.drain()
                V.tensor_tensor(g3(3), g3(2), rank4[:, :, :], ALU.mult)
                dve.drain()
                V.tensor_reduce(rg[:, 1, :, 1:2], g3(3), AXX, ALU.max)
                dve.drain()
                V.tensor_tensor(g3(4), g3(3), rg[:, 1, :, 1:2].broadcast_to([P, 3, GROUPS]), ALU.is_equal)
                dve.drain()
                V.tensor_scalar(g3(5), g3(4), -1.0, -NEG, ALU.add, ALU.mult)
                dve.drain()
                V.tensor_tensor(rt[:, SM].rearrange("p i (g q) -> p (i g) q", q=PER_GROUP), v4,
                                g3(5).rearrange("p i g -> p (i g)").unsqueeze(2).broadcast_to(
                                    [P, 3 * GROUPS, PER_GROUP]), ALU.add)
                for n, o in enumerate((O1, O2)):
                    dve.drain()
                    V.tensor_reduce(rg[:, 6, :, n:n + 1], rt[:, SM], AXX, ALU.max)
                    dve.drain()
                    V.tensor_tensor(rt[:, EQ], rt[:, SM],
                                    rg[:, 6, :, n:n + 1].broadcast_to([P, 3, EXPERTS]), ALU.is_equal)
                    dve.drain()
                    V.tensor_tensor(rt[:, KY], rt[:, EQ], rank16[:, :, :], ALU.mult)
                    dve.drain()
                    V.tensor_reduce(rg[:, 6, :, 2 + n:3 + n], rt[:, KY], AXX, ALU.max)
                    dve.drain()
                    V.tensor_tensor(rt[:, o], rt[:, KY],
                                    rg[:, 6, :, 2 + n:3 + n].broadcast_to([P, 3, EXPERTS]), ALU.is_equal)
                    if n == 0:
                        dve.drain()
                        V.scalar_tensor_tensor(rt[:, SM], rt[:, O1], 3 * NEG, rt[:, SM], ALU.mult,
                                               ALU.add)
                dve.drain()
                V.tensor_tensor(rt[:, O1], rt[:, O1], rt[:, O2], ALU.add)
                dve.drain()
                V.tensor_tensor(rt[:, O1], rt[:, O1], rt[:, S], ALU.mult)
                dve.drain()
                V.tensor_reduce(rg[:, 7, :, 0:1], rt[:, O1], AXX, ALU.add)
                dve.drain()
                V.reciprocal(rg[:, 7, :, 1:2], rg[:, 7, :, 0:1])
                dve.drain()
                V.tensor_tensor(rt[:, O2], rt[:, O1], rg[:, 7, :, 1:2].broadcast_to([P, 3, EXPERTS]),
                                ALU.mult).then_inc(g_sel.sem, 1)

                def hidden(g_end, n, f, chunk, gate):
                    dve.wait_ge(u_tanh.sem, n + 1)
                    V.scalar_tensor_tensor(h1[:, :], ht[:, :], 1.0, bank[UPB[2 * f]][:, 0:T], ALU.add,
                                           ALU.mult)
                    dve.drain()
                    dve.wait_ge(blk_done.sem, g_end + (2 * f + 2))
                    V.tensor_tensor(h1[:, :], h1[:, :], bank[UPB[2 * f + 1]][:, 0:T], ALU.mult
                                    ).then_inc(u_free.sem, 1)
                    if gate is not None:
                        dve.drain()
                        dve.wait_ge(gb_ps.sem, gate)
                        V.tensor_tensor(h2[:, :], h1[:, :], bank[4][:, 0:T], ALU.mult
                                        ).then_inc(u_prod.sem, 1)
                    else:
                        dve.drain()
                        V.tensor_copy(h2[:, :], h1[:, :]).then_inc(u_prod.sem, 1)
                    dve.wait_ge(u_hi.sem, n + 1)
                    V.scalar_tensor_tensor(hlo[:, bass.ds(chunk * T, T)], h2[:, :],
                                           UN * UN * XS / (2 * GS) if gate is not None else UN * UN * XS / 2,
                                           hhi[:, bass.ds(chunk * T, T)], ALU.mult, ALU.subtract
                                           ).then_inc(u_lo.sem, 1)

                for f in range(2):
                    if f:
                        lo_lead(U0 + 2)
                        lo_lead(U0 + 3)
                    hidden(l * NB + U0, l * UE + f, f, f, None)
                dve.wait_ge(g_hi.sem, g_hi.value(l, 1))
                V.tensor_tensor(gate_lo[0:EXPERTS, :], gate32[:, :], gate_hi[0:EXPERTS, :], ALU.subtract
                                ).then_inc(g_lo.sem, 1)
                with dve.Fori(0, EXPERTS) as e:
                    g0 = e * 4 + (U0 + 4)
                    for f in range(2):
                        lo_at(l, g0 + (2 * f + LEAD), (U0 + 2 * f + LEAD) % SLOTS)
                        lo_at(l, g0 + (2 * f + 1 + LEAD), (U0 + 2 * f + 1 + LEAD) % SLOTS)
                        hidden(l * NB + g0, l * UE + e * 2 + (2 + f), f, e * 2 + (2 + f),
                               l * EXPERTS + e + 1)

                lo_lead(D0)
                with dve.Fori(0, 4) as i:
                    for j in range(4):
                        lo_at(l, i * 4 + (D0 + 1 + j + LEAD), (D0 + 1 + j + LEAD) % SLOTS)
                lo_lead(D1)
                dve.wait_ge(acc_pre.sem, acc_pre.value(l, 2))
                dve.wait_ge(blk_done.sem, blk_done.value(l, D1))
                for c in range(4):
                    residual(l, 1, c, c)
                with dve.Fori(0, 3) as i:
                    for j in range(4):
                        lo_at(l, i * 4 + (D1 + 1 + j + LEAD), (D1 + 1 + j + LEAD) % SLOTS)
                for j in range(4):
                    lo_lead(D1 + 13 + j)
                dve.wait_ge(blk_done.sem, blk_done.value(l, NB))
                for c in range(4, KD):
                    residual(l, 1, c, (4, 5, 0, 1)[c - 4])
                ln_vector(l, 1)

        @block.tensor
        def _(pe):
            M = nc.tensor.matmul
            TR = nc.tensor.transpose

            def group(out, subs, s, rhs):
                n = 0
                for k, sub in enumerate(subs):
                    for w, part in ((whi, 0), (whi, 1), (wlo, 0)):
                        ins = M(out, w[:, s, sub * P:(sub + 1) * P], rhs(part, k), start=(n == 0),
                                stop=(n == 3 * len(subs) - 1))
                        n += 1
                return ins

            def x_rhs(part, k):
                return (xlo if part else xhi)[:, k, :]

            def ready(l, n):
                pe.wait_ge(lo_done.sem, l * NB + (n + 1))

            def z_block(l, n, s, b):
                ready(l, n)
                group(bank[b][:, 0:T], range(8), s, x_rhs).then_inc(blk_done.sem, 1)

            def tok_block(l, n, s, b):
                ready(l, n)
                for i, (t0, m) in enumerate(TILES):
                    j = 0
                    for k in range(KD):
                        for x, w in ((xhi, whi), (xhi, wlo), (xlo, whi)):
                            ins = M(bank[b][0:m, i * P:(i + 1) * P], x[:, k, t0:t0 + m],
                                    w[:, s, k * P:(k + 1) * P], start=(j == 0), stop=(j == 3 * KD - 1))
                            j += 1
                ins.then_inc(blk_done.sem, 1)

            def stats(l, k, c):
                pe.wait_ge(y_sq.sem, y_sq.value(l, KD * k + c + 1))
                M(bank[4 + 2 * k][:, 0:T], ones_dm[:, :], acc[:, c * T:(c + 1) * T], start=(c == 0),
                  stop=(c == KD - 1))
                M(bank[5 + 2 * k][:, 0:T], ones_dm[:, :], ysq[:, c % 4, :], start=(c == 0),
                  stop=(c == KD - 1)).then_inc(ln_ps.sem, 1)

            pe.wait_ge(consts_in.sem, 16 * N_CONST)
            pe.wait_ge(consts_set.sem, N_SET)
            with pe.Fori(0, L) as l:
                def z_wait(n):
                    pe.wait_ge(z_ev.sem, z_ev.value(l, n))

                pe.wait_ge(x_split.sem, x_split.value(l, 0))
                for g in range(6):
                    if g >= 4:
                        z_wait(g - 3)
                    z_block(l, g, g % SLOTS, g % 4)
                for i in range(4):
                    g = 6 + i
                    if g - 4 < 6:
                        z_wait(g - 3)
                    tok_block(l, g, g % SLOTS, g % 4)
                    if i == 0:
                        for k in range(2):
                            pe.wait_ge(sq_c.sem, sq_c.value(l, k + 1))
                            for c in range(2):
                                a = M(bank[4 + k][:, 0:T], ones_dm[:, :], ysq[:, 2 * k + c, :],
                                      start=(c == 0), stop=(c == 1))
                            a.then_inc(rms_ps.sem, 1)
                pe.wait_ge(r_exp.sem, r_exp.value(l, 1))
                pe.wait_ge(rms_std.sem, rms_std.value(l, 2))
                for n in range(3 * MH):
                    h, j = n // 3, n % 3
                    if n >= 4:
                        hh, jj = (n - 4) // 3, (n - 4) % 3
                        if jj == 0:
                            pe.wait_ge(bc_m.sem, bc_m.value(l, hh + 1))
                        else:
                            pe.wait_ge(bc_ie.sem, bc_ie.value(l, 2 * hh + jj))
                    if n == 3:
                        pe.wait_ge(cols_sb.sem, cols_sb.value(l, 1))
                    M(bank[4 + n % 4][:, 0:T], head_sel[:, h, :], r_x[:, j, :], start=True, stop=True
                      ).then_inc(bc_ps.sem, 1)
                    if n == 0:
                        for j, src in enumerate((r_a, r_x[:, 3, :])):
                            for i, (t0, m) in enumerate(TILES):
                                c0 = (3 * j + i) * MH
                                a = TR(bank[7][0:m, c0:c0 + MH], src[:, t0:t0 + m], ident[0:MH, 0:MH])
                        a.then_inc(cols_ps.sem, 1)

                with pe.Fori(0, MH) as h:
                    g0 = h * MPER + M0

                    def zb(step, freed_z, freed_v=None):
                        pe.wait_ge(z_ev.sem, l * z_ev.per + h * 7 + freed_z)
                        if freed_v is not None:
                            pe.wait_ge(tokv.sem, l * tokv.per + freed_v)
                        return (l, g0 + step, (M0 + step) % SLOTS, (M0 + step) % 4)

                    z_block(*zb(0, 3, 1))
                    z_block(*zb(1, 4, 2))
                    tok_block(*zb(2, 5, 3))
                    pe.wait_ge(z_ev.sem, l * z_ev.per + h * 7 + 8)
                    pe.wait_ge(h_done.sem, l * MH + h)
                    pe.wait_ge(bc_ie.sem, bc_ie.value(l, 2 * MH))
                    pe.wait_ge(bc_m.sem, bc_m.value(l, MH))
                    for i, (t0, n) in enumerate(TILES):
                        a = TR(bank[4][0:n, i * P:(i + 1) * P], mk[:, t0:t0 + n], ident[:, :])
                    a.then_inc(k_tr.sem, 1)
                    for i, (t0, n) in enumerate(TILES):
                        a = M(bank[5][0:n, i * P:i * P + n], mk[:, t0:t0 + n], mq[:, t0:t0 + n],
                              start=True, stop=True)
                    a.then_inc(a_ps.sem, 1)
                    z_block(*zb(3, 6, 4))
                    pe.wait_ge(k_sb.sem, l * MH + h + 1)
                    pe.wait_ge(v_wsd.sem, l * MH + h + 1)
                    pe.wait_ge(g_done.sem, l * MH + h)
                    for c in range(NCH):
                        r0, b, o = CH * (c % 2), bank[6 + c % 2], (c // 2) * (DH + 1)
                        a = M(b[:, o:o + DH + 1], k_tok[r0:r0 + CH, c // 2, :],
                              v_ws[r0:r0 + CH, c // 2, :], start=True, stop=True)
                    a.then_inc(dc_ps.sem, 1)
                    z_block(*zb(4, 7))
                    z_block(*zb(5, 8))
                    pe.wait_ge(att_done.sem, l * MH + h + 1)
                    pe.wait_ge(st_done.sem, l * MH + h + 1)
                    for num, b in ((True, bank[4]), (False, bank[5])):
                        for i, (t0, n) in enumerate(TILES):
                            M(b[:, t0:t0 + n], v_tok[0:n, i, :] if num else ones[0:n, :],
                              att[0:n, i, 0:n], start=True, stop=False)
                            for j, (c, st) in enumerate(((1, 0), (2, 1), (3, 2), (4, 4))):
                                if t0 <= c * CH < t0 + n:
                                    last = (c + 1) * CH == t0 + n
                                    a = M(b[:, c * CH:(c + 1) * CH],
                                          c_st[:, st, 0:DH] if num else n_bc[:, j, :],
                                          q_in[:, c * CH:(c + 1) * CH], start=False, stop=last)
                    a.then_inc(num_ps.sem, 1)
                    z_block(*zb(6, 8, 5 + h))
                    pe.wait_ge(vg_done.sem, l * MH + h + 1)
                    pe.wait_ge(ws_masked.sem, ws_masked.value(l, 1))
                    for i, (t0, n) in enumerate(TILES):
                        off = h * P
                        M(bank[6][:, t0:t0 + n], vg[0:n, i, :], ws_t[0:n, bass.ds(off, n)], start=True,
                          stop=False)
                        a = M(bank[6][:, t0:t0 + n], ones[0:1, :], bs_row[:, bass.ds(off, n)],
                              start=False, stop=True)
                    a.then_inc(sp_ps.sem, 1)
                    z_block(*zb(7, 9))

                with pe.Fori(0, 2) as hf:
                    g0 = hf * APER + A0
                    s0, s1 = A0 % SLOTS, (A0 + 1) % SLOTS
                    ready(l, g0)
                    pe.wait_ge(c_lo.sem, c_lo.value(l, 3))
                    pe.wait_ge(g_done.sem, g_done.value(l, MH))
                    pe.wait_ge(h_done.sem, h_done.value(l, MH))
                    pe.wait_ge(o_lo.sem, l * 4 + hf * 2)
                    for j in range(4):
                        a = group(bank[4 + j][:, 0:T], (2 * j, 2 * j + 1), s0,
                                  lambda part, k: (cq_lo if part else cq_hi)[:, k, :])
                    a.then_inc(blk_done.sem, 1)
                    ready(l, g0 + 1)
                    pe.wait_ge(z_ev.sem, l * z_ev.per + hf * 10 + 34)
                    pe.wait_ge(t_sb.sem, l * 12 + hf * 6)
                    for j in range(4):
                        k0 = (j % 2) * KH
                        group(bank[j][:, 0:KH], (2 * (j // 2), 2 * (j // 2) + 1), s1,
                              lambda part, k: (kv_lo if part else kv_hi)[:, k, k0:k0 + KH])
                    pe.wait_ge(q_ev.sem, l * 2 + hf + 1)
                    pe.wait_ge(q_rot.sem, l * 2 + hf + 1)
                    for i in range(5):
                        n = P if i < 4 else TS
                        j = 0
                        for k in range(2):
                            for x, w in ((kv_hi, whi), (kv_hi, wlo), (kv_lo, whi)):
                                a = M(bank[4 + i // 2][0:n, (i % 2) * 2 * P:(i % 2 + 1) * 2 * P],
                                      x[:, k, i * P:i * P + n],
                                      w[:, s1, (4 + 2 * k) * P:(6 + 2 * k) * P], start=(j == 0),
                                      stop=(j == 5))
                                j += 1
                    a.then_inc(blk_done.sem, 1)

                    def scores(j):
                        p, r = j // 3, j % 3
                        b = bank[4 + j % 2]
                        if j < 2:
                            pe.wait_ge(v_ev.sem, l * 2 + hf + 1)
                        if j >= 2:
                            pe.wait_ge(p_exp.sem, l * 12 + hf * 6 + (j - 1))
                        if j == 0:
                            pe.wait_ge(kr_done.sem, kr_done.value(l, 1))
                            pe.wait_ge(z_ev.sem, l * z_ev.per + hf * 10 + 38)
                        if r < 2:
                            hh = 2 * p + r
                            for q in range(2):
                                a = M(b[:, P * q:P * q + P * (q + 1)],
                                      q_att[0:KATT, hh, P * q:P * (q + 1)],
                                      k_att[0:KATT, hh, PAST:PAST + P * (q + 1)], start=True, stop=True)
                        else:
                            for r_ in range(2):
                                hh = 2 * p + r_
                                for o, k0, n in ((0, 0, PAST), (PAST, PAST + TP, TS)):
                                    a = M(b[TS * r_:TS * (r_ + 1), o:o + n], q_att[0:KATT, hh, TP:T],
                                          k_att[0:KATT, hh, k0:k0 + n], start=True, stop=True)
                        a.then_inc(s_ps.sem, 1)

                    def transposes(j):
                        pe.wait_ge(p_norm.sem, l * 12 + hf * 6 + (j + 1))
                        if j:
                            pe.wait_ge(t_sb.sem, l * 12 + hf * 6 + j)
                        for i in range(3):
                            n = P if j % 3 < 2 or i < 2 else TS
                            a = TR(bank[6][0:n, i * P:(i + 1) * P], prob[:, j % 2, i * P:i * P + n],
                                   ident[:, :])
                        a.then_inc(t_ps.sem, 1)

                    def values(j):
                        p, r = j // 3, j % 3
                        pe.wait_ge(t_sb.sem, l * 12 + hf * 6 + (j + 1))
                        if j == 3:
                            pe.wait_ge(o_lo.sem, l * 4 + hf * 2 + 1)
                        for r_ in ((r,) if r < 2 else (0, 1)):
                            vc = slice((2 * p + r_) * VD, (2 * p + r_ + 1) * VD)
                            o = bank[7][VD * r_:VD * (r_ + 1), :]
                            if r < 2:
                                M(o[:, 0:P], v_kv[:, 2, vc], prob_t[:, j % 2, 0, :], start=True,
                                  stop=True)
                                M(o[:, P:2 * P], v_kv[:, 2, vc], prob_t[:, j % 2, 1, :], start=True,
                                  stop=False)
                                a = M(o[:, P:2 * P], v_kv[:, 3, vc], prob_t[:, j % 2, 2, :],
                                      start=False, stop=True)
                            else:
                                qs = slice(TS * r_, TS * (r_ + 1))
                                for n, (kt, rows_) in enumerate(((0, P), (1, P), (4, TS))):
                                    a = M(o[:, TP:T], v_kv[0:rows_, kt, vc],
                                          prob_t[0:rows_, j % 2, n, qs], start=(n == 0), stop=(n == 2))
                        a.then_inc(o_ps.sem, 1)

                    for j in range(6):
                        scores(j)
                        if j:
                            transposes(j - 1)
                        if j >= 2:
                            values(j - 2)
                        pe.wait_ge(z_ev.sem, l * z_ev.per + hf * 10 + (35 + j))
                        z_block(l, g0 + (2 + j), (A0 + 2 + j) % SLOTS, (A0 + 2 + j) % 4)
                    transposes(5)
                    values(4)
                    values(5)

                with pe.Fori(0, 3) as k:
                    pe.wait_ge(z_ev.sem, z_ev.value(l, 54))
                    pe.wait_ge(bc_lo.sem, bc_lo.value(l, 2 * MH))
                    pe.wait_ge(o_lo.sem, o_lo.value(l, 4))
                    for j in range(4):
                        ready(l, k * 4 + (B0 + j))
                        for i in range(2):
                            c = 2 * j + i
                            pe.wait_ge(m_used.sem, l * 24 + k * 8 + max(0, c - 3))
                            a = group(bank[c % 4][:, 0:T], range(4 * i, 4 * i + 4), (B0 + j) % SLOTS,
                                      lambda part, kt: (br_lo if part else br_hi)[
                                          :, bass.ds((k * 4 + kt) * T, T)])
                        a.then_inc(blk_done.sem, 1)

                for c in range(KD):
                    ready(l, O0 + c)
                    if c == 0:
                        pe.wait_ge(m_lo.sem, m_lo.value(l, KD))
                    if c >= 4:
                        pe.wait_ge(y_done.sem, y_done.value(l, c - 3))
                    group(bank[(O0 + c) % 4][:, 0:T], range(8), (O0 + c) % SLOTS,
                          lambda part, k: (mlo if part else mhi)[:, k, :]).then_inc(blk_done.sem, 1)
                    if c >= 2:
                        stats(l, 0, c - 2)
                stats(l, 0, KD - 2)
                stats(l, 0, KD - 1)

                UPB = [(U0 + j) % 4 for j in range(4)]
                UE = 2 * (EXPERTS + 1)
                pe.wait_ge(x_split.sem, x_split.value(l, KD))
                for i in range(3):
                    t0 = min(i * P, T - P)
                    for k in range(KD):
                        a = M(bank[7][:, i * EXPERTS:(i + 1) * EXPERTS], xT[:, k * T + t0:k * T + t0 + P],
                              rw[:, k, :], start=(k == 0), stop=(k == KD - 1))
                a.then_inc(r_ps.sem, 1)
                for j in range(4):
                    z_block(l, U0 + j, (U0 + j) % SLOTS, UPB[j])
                pe.wait_ge(g_sel.sem, g_sel.value(l, 1))
                for i in range(3):
                    a = TR(bank[6][0:EXPERTS, i * P:(i + 1) * P], rt[:, 7, i, :], ident[:, :])
                a.then_inc(g_tr.sem, 1)
                with pe.Fori(0, EXPERTS) as e:
                    g0 = e * 4 + (U0 + 4)
                    for j in range(4):
                        if j % 2 == 0:
                            pe.wait_ge(u_free.sem, l * UE + e * 2 + (1 + j // 2))
                        z_block(l, g0 + j, (U0 + j) % SLOTS, UPB[j])
                        if j == 0:
                            pe.wait_ge(g_lo.sem, g_lo.value(l, 1))
                            pe.wait_ge(u_prod.sem, l * UE + e * 2 + 2)
                            M(bank[4][:, 0:T], exp_sel[:, bass.ds(e * P, P)], gate_hi[:, :], start=True,
                              stop=False)
                            M(bank[4][:, 0:T], exp_sel[:, bass.ds(e * P, P)], gate_lo[:, :], start=False,
                              stop=True).then_inc(gb_ps.sem, 1)

                def down(l, n, s, banks, expert, first, last):
                    ready(l, n)
                    for kt in range(2):
                        for i, b in enumerate(banks):
                            for w, h_ in ((whi, hhi), (whi, hlo), (wlo, hhi)):
                                a = M(bank[b][:, 0:T], w[:, s, (4 * kt + i) * P:(4 * kt + i + 1) * P],
                                      h_[:, bass.ds((expert * 2 + kt) * T, T)],
                                      start=(first and kt == 0 and w is whi and h_ is hhi),
                                      stop=(last and kt == 1 and w is wlo))
                    a.then_inc(blk_done.sem, 1)

                pe.wait_ge(u_lo.sem, u_lo.value(l, UE))
                half0, half1 = (0, 1, 2, 3), (4, 5, 0, 1)
                down(l, D0, D0 % SLOTS, half0, 0, True, False)
                with pe.Fori(0, 3) as i:
                    for j in range(4):
                        down(l, i * 4 + (D0 + 1 + j), (D0 + 1 + j) % SLOTS, half0, i * 4 + (1 + j),
                             False, False)
                for j in range(4):
                    down(l, D0 + 13 + j, (D0 + 13 + j) % SLOTS, half0, 13 + j, False, j == 3)
                pe.wait_ge(y_done.sem, y_done.value(l, KD + 2))
                down(l, D1, D1 % SLOTS, half1, 0, True, False)
                for c in range(4):
                    stats(l, 1, c)
                with pe.Fori(0, 3) as i:
                    for j in range(4):
                        down(l, i * 4 + (D1 + 1 + j), (D1 + 1 + j) % SLOTS, half1, i * 4 + (1 + j),
                             False, False)
                for j in range(4):
                    down(l, D1 + 13 + j, (D1 + 13 + j) % SLOTS, half1, 13 + j, False, j == 3)
                for c in range(4, KD):
                    stats(l, 1, c)


def _blocks(inp):
    def kt(w):
        return w.reshape(-1, P, w.shape[1]).transpose(1, 0, 2)

    out = np.zeros((L, NB, P, BLK), np.float32)
    half = ROPE // 2
    swap = np.r_[half:ROPE, 0:half]
    zin = np.cumsum([0, RANK, RANK, ROPE, 512, 512, 512, MH, MH, 512, 512, 512])
    cq, ckv, kr, q, k, v, gi, gf, go, gu, gv, gt = (int(n) for n in zin)

    def cols(i):
        gate = np.full(P, -1)
        gate[0:MH] = gi + np.arange(MH)
        gate[32:32 + MH] = gf + np.arange(MH)
        rot = np.full(P, -1)
        rot[0:ROPE] = kr + np.arange(ROPE)
        rot[ROPE:2 * ROPE] = kr + swap
        tile = lambda base, n: base + n * P + np.arange(P)
        front = [gate, tile(cq, 0), tile(cq, 1), tile(ckv, 0), tile(ckv, 1), rot]
        heads = [[tile(q, h), tile(k, h), tile(v, h), tile(go, h), tile(gu, h)] for h in range(MH)]
        return front, [tile(gv, n) for n in range(4)], heads, [tile(gt, n) for n in range(24)]

    front, gvs, heads, gts = cols(0)
    z = {n: c for n, c in enumerate(front)}
    z.update({6 + n: c for n, c in enumerate(gvs)})
    for h in range(MH):
        for n, c in enumerate(heads[h] + gts[3 * h:3 * h + 3]):
            z[M0 + MPER * h + n] = c
    for hf in range(2):
        for n in range(6):
            z[A0 + APER * hf + 2 + n] = gts[12 + 6 * hf + n]
    par = np.zeros((P, L, NPAR), np.float32)
    for l in range(L):
        w, b = inp["w_in"][l], inp["b_in"][l]

        def take(a, c):
            return np.where(c >= 0, a[..., np.maximum(c, 0)], np.float32(0))

        for n, c in z.items():
            out[l, n] = kt(take(w, c)).reshape(P, BLK)
        for n, c in enumerate(front):
            par[:, l, C_FRONT + n] = take(b, c)
        for h in range(MH):
            for n, c in enumerate((heads[h][0], heads[h][1], heads[h][3], heads[h][4])):
                par[:, l, C_MLSTM + 4 * h + n] = take(b, c)
        for n, c in enumerate(gts):
            par[:, l, C_GATE + n] = take(b, c)
        for col, name in ((C_QG, "q_norm_g"), (C_KVG, "kv_norm_g"), (C_L1G, "ln1_g"), (C_L1B, "ln1_b"),
                          (C_L2G, "ln2_g"), (C_L2B, "ln2_b")):
            a = inp[name][l].reshape(-1, P).T
            par[:, l, col:col + a.shape[1]] = a
        uq = inp["w_uq"][l].reshape(RANK, HEADS, NOPE + ROPE)
        ukv = inp["w_ukv"][l].reshape(RANK, HEADS, NOPE + VD)
        for hf in range(2):
            hs = slice(4 * hf, 4 * hf + 4)
            n = A0 + APER * hf
            tiles = [uq[:, 4 * hf:4 * hf + 2, :NOPE], uq[:, 4 * hf + 2:4 * hf + 4, :NOPE],
                     uq[:, hs, NOPE:], uq[:, hs, NOPE:][:, :, swap]]
            out[l, n] = np.concatenate([kt(t.reshape(RANK, P)).reshape(P, 2 * P) for t in tiles], 1)
            kv = [kt(ukv[:, 4 * hf + 2 * j:4 * hf + 2 * j + 2, :NOPE].reshape(RANK, P)).reshape(P, 2 * P)
                  for j in range(2)]
            kv.append(kt(ukv[:, hs, NOPE:].reshape(RANK, 2 * P)).reshape(P, 4 * P))
            out[l, n + 1] = np.concatenate(kv, 1)
        for k_ in range(3):
            w4 = inp["w_branch"][l, k_].reshape(4, P, 4, 2, P).transpose(2, 1, 3, 0, 4)
            out[l, B0 + 4 * k_:B0 + 4 * k_ + 4] = w4.reshape(4, P, BLK)
        out[l, O0:U0] = inp["w_out"][l].reshape(KD, P, KD, P).transpose(2, 1, 0, 3).reshape(KD, P, BLK)
        wg = np.concatenate([inp["shared_w_gate"][l][None], inp["moe_w_gate"][l]])
        wu = np.concatenate([inp["shared_w_up"][l][None], inp["moe_w_up"][l]])
        wd = np.concatenate([inp["shared_w_down"][l][None], inp["moe_w_down"][l]])
        up = np.stack([wg, wu], 1).reshape(EXPERTS + 1, 2, KD, P, 2, P)
        out[l, U0:D0] = up.transpose(0, 4, 1, 3, 2, 5).reshape(-1, P, BLK)
        dn = wd.reshape(EXPERTS + 1, 2, P, 2, 4, P).transpose(3, 0, 2, 1, 4, 5)
        out[l, D0:NB] = dn.reshape(-1, P, BLK)
    rows = np.stack([inp["b_in"][:, gv:gv + 512], inp["b_in"][:, v:v + 512],
                     inp["gmlp_ln_g"], inp["gmlp_ln_b"]], 1)
    return out.reshape(L * NB * P, BLK), par.reshape(P, L * NPAR), rows.reshape(L, 4 * GW)


def _constants():
    half = ROPE // 2
    pos = np.r_[0:TP, PAST:PAST + TS].astype(np.float32)
    inv = (np.float32(10000.0) ** (-np.arange(half, dtype=np.float32) / half)).astype(np.float32)
    ang = pos[None, :] * inv[:, None]
    cos, sin = np.cos(ang), np.sin(ang)
    s, t = np.arange(P)[:, None], np.arange(T)[None, :]
    tt = t % P
    mmask = np.where((s <= tt) & (s // CH == tt // CH), 0, NEG)
    keep = np.broadcast_to(np.arange(T) % CH != 0, (MH, T))
    att = np.zeros((2, T + KEYS))
    for n in range(2):
        att[n, n * P:n * P + CH] = 1
        att[n, T + PAST + n * P + CH:T + PAST + (n + 1) * P] = NEG
    sel = np.zeros((P, EXPERTS, P), np.float16)
    sel[np.arange(EXPERTS), np.arange(EXPERTS)] = 1
    c = dict(
        cos=np.tile(np.concatenate([cos, cos]), (4, 1)), sin=np.tile(np.concatenate([-sin, sin]), (4, 1)),
        ident=np.eye(P), tri=np.triu(np.ones((P, P))), mmask=mmask, scan_keep=keep,
        att_mask=att,
        head_sel=np.broadcast_to(np.eye(MH)[:, :, None], (MH, MH, P)),
        rank4=np.broadcast_to(np.arange(GROUPS, 0, -1), (P, 3, GROUPS)),
        rank16=np.broadcast_to(np.arange(EXPERTS, 0, -1), (P, 3, EXPERTS)))
    c = {n: np.ascontiguousarray(a, dtype=np.float32) for n, a in c.items()}
    c["exp_sel"] = sel.reshape(P, EXPERTS * P)
    return c


_OUTS = dict(y=(P, KD * T), ckv=(L * P, 2 * T), kr_out=(L * ROPE, T), m_out=(L * MH, 8),
             gv_out=(L * TS, GW), c_prompt=(L * MH * P, DH + 1), c_sample=(L * MH * P, DH + 1))


def kernel(**inputs):
    import concourse.bacc as bacc
    from concourse.bass_utils import run_bass_kernel_spmd

    inp = {k: np.asarray(v) for k, v in inputs.items()}
    w, par, rows = _blocks(inp)
    x = np.concatenate([inp["x_prompt"][0], inp["x_sample"][0]])
    c0 = np.concatenate([inp["state_mlstm_c"][:, 0].transpose(0, 1, 3, 2),
                         inp["state_mlstm_n"][:, 0][..., None]], -1)
    arrays = dict(
        x=x.T.reshape(KD, P, T).transpose(1, 0, 2).reshape(P, KD * T), w=w, par=par, rows=rows,
        rb=np.tile(inp["router_b"], 3), rw=inp["router_w"].reshape(KD, P, EXPERTS).transpose(1, 0, 2),
        m_init=inp["state_mlstm_m"][:, 0].T, c_init=c0.transpose(0, 2, 1, 3).reshape(L * P, -1),
        cache=inp["cache_mla_ckv"][:, 0].reshape(L, PAST, 2, P).transpose(0, 3, 2, 1).reshape(L * P, -1),
        krope=inp["cache_mla_krope"][:, 0].transpose(0, 2, 1).reshape(L * ROPE, PAST),
        ws_t=inp["gmlp_ws"].transpose(0, 3, 1, 2).reshape(L * P, -1),
        bs_row=inp["gmlp_bs"].reshape(L, -1), **_constants())
    arrays = {n: np.ascontiguousarray(a) for n, a in arrays.items()}
    nc = bacc.Bacc("TRN2", target_bir_lowering=False, num_devices=1)
    d = {n: nc.dram_tensor(f"in_{n}", a.shape, mybir.dt.from_np(a.dtype), kind="ExternalInput").ap()
         for n, a in arrays.items()}
    d.update({n: nc.dram_tensor(f"out_{n}", s, F32, kind="ExternalOutput").ap() for n, s in _OUTS.items()})
    build_trunk(nc, d)
    r = run_bass_kernel_spmd(nc, [{f"in_{n}": a for n, a in arrays.items()}], core_ids=[0]).results[0]
    o = {n: np.asarray(r[f"out_{n}"]) for n in _OUTS}

    y = o["y"].reshape(P, KD, T).transpose(2, 1, 0).reshape(T, DM)
    ckv = o["ckv"].reshape(L, P, 2, T).transpose(0, 3, 2, 1).reshape(L, 1, T, RANK)
    kr = o["kr_out"].reshape(L, ROPE, T).transpose(0, 2, 1).reshape(L, 1, T, ROPE)
    m = o["m_out"].reshape(L, 1, MH, 8)
    cp, cs = (o[n].reshape(L, 1, MH, DH, DH + 1) for n in ("c_prompt", "c_sample"))
    c = np.ascontiguousarray
    return (c(y[None, :TP]), c(y[None, TP:]), c(ckv[:, :, :TP]), c(kr[:, :, :TP]),
            c(cp[..., :DH].swapaxes(3, 4)), c(cp[..., DH]), c(m[..., 4]),
            c(ckv[:, :, TP:]), c(kr[:, :, TP:]), c(cs[..., :DH].swapaxes(3, 4)), c(cs[..., DH]),
            c(m[..., 6]), c(o["gv_out"].reshape(L, 1, TS, GW)))
```

```python
from contextlib import ExitStack

import concourse.bass as bass
import numpy as np
from concourse import mybir

F32, F16 = mybir.dt.float32, mybir.dt.float16
ALU = mybir.AluOpType
ACT = mybir.ActivationFunctionType
AXX = mybir.AxisListType.X

P = 128
DM, L = 1024, 2
TP, TS, PAST = 256, 64, 256
T = TP + TS
KD = DM // P
HEADS, NOPE, ROPE, VD, RANK = 8, 64, 32, 64, 256
MH, DH, CH = 4, 128, 64
NCH = T // CH
GW = 512
EXPERTS, GROUPS, PER_GROUP, DE = 16, 4, 4, 256
ALPHA = (2 * L) ** 0.25
EPS = 1e-5
ATT_SCALE = (NOPE + ROPE) ** -0.5
KSCALE = DH ** -0.5
NEG = -1e30
MROW = NOPE + ROPE
KATT = MROW + 2
KEYS = PAST + T
KH = KEYS // 2

WS = 64.0
XS = 4.0
UN = 1.0 / (WS * XS)
GS = 1024.0

CAP = P
H0 = 2 * T

SLOTS = 4
LEAD = 2
BLK = 8 * P
FRONT = 10
M0, MPER = FRONT, 8
A0, APER = M0 + MH * MPER, 8
B0 = A0 + 2 * APER
O0 = B0 + 12
U0 = O0 + KD
D0 = U0 + 4 * (EXPERTS + 1)
D1 = D0 + EXPERTS + 1
NB = D1 + EXPERTS + 1
assert NB % SLOTS == 0 and MPER % SLOTS == 0 and APER % SLOTS == 0

C_FRONT, C_MLSTM, C_GATE = 0, 6, 22
C_QG, C_KVG, C_L1G, C_L1B, C_L2G, C_L2B, NPAR = 46, 48, 50, 58, 66, 74, 82

TILES = [(0, P), (P, P), (2 * P, TS)]


class Signal:

    def __init__(self, ctx, nc, name, per, before=0):
        self.sem, self.per, self.before = ctx.enter_context(nc.semaphore(name)), per, before

    def value(self, layer, n):
        return layer * self.per + (n + self.before)


def build_trunk(nc, d):
    with ExitStack() as ctx:
        def sb(name, shape, dt=F32):
            return ctx.enter_context(nc.sbuf_tensor(name, shape, dt))

        def sig(name, per, before=0):
            return Signal(ctx, nc, name, per, before)

        w32 = sb("w32", [P, SLOTS, BLK])
        whi = sb("whi", [P, SLOTS, BLK], F16)
        wlo = sb("wlo", [P, SLOTS, BLK], F16)
        xT = sb("xT", [P, KD * T])
        xhi = sb("xhi", [P, KD, T], F16)
        xlo = sb("xlo", [P, KD, T], F16)
        acc = sb("acc", [P, KD * T])
        ysq = sb("ysq", [P, 4, T])
        br_hi = sb("br_hi", [P, 12 * T], F16)
        br_lo = sb("br_lo", [P, 12 * T], F16)
        arena_a = sb("arena_a", [P, 24 * T])
        arena_b = sb("arena_b", [P, 17 * T])
        gates = arena_a[:, :]
        hhi = arena_a[:, 0:17 * T].bitcast(F16)
        hlo = arena_b[:, :].bitcast(F16)
        f16_a = arena_a[:, :].bitcast(F16)
        f16_b = arena_b[:, :].bitcast(F16)
        HEND = H0 + 2 * EXPERTS * CAP
        x_tok = f16_a[:, HEND:HEND + 12 * 512]
        ONE0 = 34 * T
        one_hot = f16_a[:, ONE0:ONE0 + (GROUPS + 1) * 3 * CAP]
        OT0 = ONE0 + (GROUPS + 1) * 3 * CAP
        slot_tok = f16_a[:, OT0:OT0 + GROUPS * T]
        x_grp = f16_b[:, HEND:HEND + 2 * 4 * 512].rearrange(
            "p (b a k n) -> p b a k n", b=2, a=2, k=KD)
        y_hi = f16_b[:, HEND:HEND + 4 * 512]
        y_lo = f16_b[:, HEND + 4 * 512:HEND + 8 * 512]
        mrow_m = arena_b[:, 0:4 * T]
        mrow_i = arena_b[:, 4 * T:8 * T]
        mrow_e = arena_b[:, 8 * T:12 * T]
        gvt = arena_b[:, 12 * T:12 * T + 3 * GW].rearrange("p (i n) -> p i n", i=3)
        mhi = arena_b[:, 0:4 * T].bitcast(F16).rearrange("p (n t) -> p n t", t=T)
        mlo = arena_b[:, 4 * T:8 * T].bitcast(F16).rearrange("p (n t) -> p n t", t=T)
        par = sb("par", [P, L * NPAR])
        par_c = sb("par_c", [P, NPAR])
        par_h = sb("par_h", [P, NPAR])
        par_x = sb("par_x", [P, NPAR])
        rows = sb("rows", [P, 4 * GW])
        ws_t = sb("ws_t", [P, 4 * P])
        c_init = sb("c_init", [P, MH * (DH + 1)])
        m_init = sb("m_init", [MH, L])
        rw = sb("rw", [P, KD, EXPERTS])
        rb = sb("rb", [P, 3, EXPERTS])
        cosT = sb("cosT", [P, T])
        sinT = sb("sinT", [P, T])
        ident = sb("ident", [P, P])
        ones = sb("ones", [P, P])
        ones_dm = sb("ones_dm", [P, P])
        eps_col = sb("eps_col", [P, 1])
        mmask = sb("mmask", [P, T])
        scan_keep = sb("scan_keep", [MH, T])
        head_sel = sb("head_sel", [MH, MH, P])
        att_mask = sb("att_mask", [MROW + 2, T + KEYS])[MROW:MROW + 2, :]
        bs_row = sb("bs_row", [1, 4 * P])
        mats16 = sb("mats16", [P, 3, P], F16)
        slot_no = sb("slot_no", [P, CAP])
        exp_sel = sb("exp_sel", [P, EXPERTS * P], F16)
        rank4 = sb("rank4", [P, 3, GROUPS])
        rank16 = sb("rank16", [P, 3, EXPERTS])
        acc3 = acc[:, :].rearrange("p (n t) -> p n t", t=T)
        front3 = arena_a[:, :].rearrange("p (n t) -> p n t", t=T)
        zf = acc3[:, 0:6, :]
        rstd = acc3[:, 6:8, :]
        znorm = front3[:, 20:24, :]
        cache = arena_a[:, 0:2 * PAST]
        cq_hi = sb("cq_hi", [P, 2, T], F16)
        cq_lo = sb("cq_lo", [P, 2, T], F16)
        kv_hi = sb("kv_hi", [P, 2, KEYS], F16)
        kv_lo = sb("kv_lo", [P, 2, KEYS], F16)
        kv_out = front3[:, 16:18, :]
        kr_t = front3[0:ROPE, 18:20, :]
        kr = sb("kr", [MROW, KEYS])[NOPE:MROW, :]
        stat = sb("stat", [P, 3, 8])
        r_f = front3[0:MH, 8:12, :]
        r_b = front3[0:MH, 5, :]
        r_a = front3[0:MH, 6, :]
        r_m = front3[0:MH, 7, :]
        scan_drop = front3[0:MH, 4, :]
        r_x = front3[0:MH, 12:16, :]
        m_at = sb("m_at", [MH, 8])
        cols = sb("cols", [P, 6 * MH])
        mq = sb("mq", [P, T])
        mk = sb("mk", [P, T])
        mo = sb("mo", [P, T])
        gu = sb("gu", [P, T])
        k_tok = sb("k_tok", [P, 3, P])
        v_tok = sb("v_tok", [P, 3, P])
        v_ws = sb("v_ws", [P, 3, DH + 1])
        dec_w = sb("dec_w", [P, 3, P])
        att = sb("att", [P, 3, P])
        q_in = sb("q_in", [P, T])
        c_st = sb("c_st", [P, 6, DH + 1])
        n_bc = sb("n_bc", [P, 4, P])
        hden = sb("hden", [P, T])
        hout = sb("hout", [P, T])
        vg = sb("vg", [P, 3, P])
        gout = hden
        q_att = arena_b[:, 0:4 * T].rearrange("p (n t) -> p n t", t=T)
        qr_t = arena_b[:, 4 * T:6 * T].rearrange("p (n t) -> p n t", t=T)
        v_kv = arena_b[:, 6 * T:6 * T + 10 * P].rearrange("p (i n) -> p i n", i=5)
        k_att = acc[:, 0:4 * KEYS].rearrange("p (n t) -> p n t", t=KEYS)
        sm = sb("sm", [P, 8])
        mu_var = sb("mu_var", [P, 4 * T])
        prob = mu_var[:, 0:6 * P].rearrange("p (b n) -> p b n", b=2)
        prob_t = ysq[:, :, :].rearrange("p a t -> p (a t)")[:, 0:6 * P].rearrange(
            "p (b i n) -> p b i n", b=2, i=3)
        mtmp = (gu, mo)
        mu = mu_var[:, 0:2 * T].rearrange("p (n t) -> p n t", t=T)
        var = mu_var[:, 2 * T:4 * T].rearrange("p (n t) -> p n t", t=T)
        ln_r = q_in
        rt = sb("rt", [P, 10, 3, EXPERTS])
        rp = sb("rp", [P, 3 * GROUPS, 6])
        rg = sb("rg", [P, 8, 3, GROUPS])
        gate_hi, gate_lo = (f16_a[:, OT0 + GROUPS * (T + n * CAP):][:, 0:GROUPS * CAP] for n in range(2))
        gate32 = hout[0:EXPERTS, :]
        gt_hi = sb("gt_hi", [P, 3, EXPERTS], F16)
        gt_lo = sb("gt_lo", [P, 3, EXPERTS], F16)
        gm16 = sb("gm16", [P, 3, GROUPS], F16)
        place = sb("place", [P, 3, GROUPS])
        most = sb("most", [P, 1])
        most_i = sb("most_i", [P, 1], mybir.dt.int32)
        ht, h1, h2 = mq, mk, mo

        bank = [ctx.enter_context(nc.psum_tensor(f"bank{i}", [P, 512], F32)) for i in range(8)]

        loaded = [sig(f"loaded{s}", 16 * NB // SLOTS) for s in range(SLOTS)]
        consts_in = sig("consts_in", 0)
        x_in = sig("x_in", 0)
        stored = sig("stored", 16 * (4 + 2 * MH), 1)
        consts_set = sig("consts_set", 0)
        ws_masked = sig("ws_masked", 1)
        layer_in = sig("layer_in", 16 * 6)
        hi_done = sig("hi_done", NB)
        lo_done = sig("lo_done", NB)
        blk_done = sig("blk_done", NB)
        x_hi = sig("x_hi", 2 * KD, KD)
        x_split = sig("x_split", 2 * KD, KD)
        pars = sig("pars", 1)
        z_ev = sig("z_ev", 54)
        tokv = sig("tokv", 8)
        gv_act = sig("gv_act", 4)
        sq_c = sig("sq_c", 2)
        rms_ps = sig("rms_ps", 2)
        rms_std = sig("rms_std", 2)
        z_norm = sig("z_norm", 2)
        c_hi = sig("c_hi", 3)
        c_lo = sig("c_lo", 3)
        kr_done = sig("kr_done", 1)
        f_abs = sig("f_abs", 1)
        f_ln = sig("f_ln", 1)
        r_arg = sig("r_arg", 1)
        r_exp = sig("r_exp", 1)
        cols_ps = sig("cols_ps", 1)
        cols_sb = sig("cols_sb", 1)
        bc_ps = sig("bc_ps", 3 * MH)
        bc_m = sig("bc_m", MH)
        bc_ie = sig("bc_ie", 2 * MH)
        gv_std = sig("gv_std", 1)
        gv_var = sig("gv_var", 1)
        gv_done = sig("gv_done", 1)
        k_tr = sig("k_tr", MH)
        a_ps = sig("a_ps", MH)
        k_sb = sig("k_sb", MH)
        dec_done = sig("dec_done", MH)
        v_wsd = sig("v_wsd", MH)
        att_done = sig("att_done", MH, 1)
        dc_ps = sig("dc_ps", MH, 1)
        st_done = sig("st_done", MH)
        num_ps = sig("num_ps", MH, 1)
        h_done = sig("h_done", MH, 1)
        vg_done = sig("vg_done", MH)
        sp_ps = sig("sp_ps", MH, 1)
        g_done = sig("g_done", MH, 1)
        bc_hi = sig("bc_hi", 2 * MH)
        bc_lo = sig("bc_lo", 2 * MH)
        q_ev = sig("q_ev", 2)
        q_rot = sig("q_rot", 2)
        v_ev = sig("v_ev", 2)
        s_ps = sig("s_ps", 12, 1)
        s_max = sig("s_max", 12)
        p_exp = sig("p_exp", 12)
        p_norm = sig("p_norm", 12)
        t_ps = sig("t_ps", 12)
        t_sb = sig("t_sb", 12, 1)
        o_ps = sig("o_ps", 12)
        o_hi = sig("o_hi", 4)
        o_lo = sig("o_lo", 4, 1)
        m_used = sig("m_used", 24, 1)
        m_hi = sig("m_hi", KD)
        m_lo = sig("m_lo", KD)
        acc_pre = sig("acc_pre", 2)
        y_done = sig("y_done", 2 * KD)
        y_sq = sig("y_sq", 2 * KD)
        ln_ps = sig("ln_ps", 2 * KD)
        ln_mu = sig("ln_mu", 2)
        ln_var = sig("ln_var", 2)
        ln_std = sig("ln_std", 2)
        ln_t = sig("ln_t", 2 * KD)
        r_ps = sig("r_ps", 1)
        r_e = sig("r_e", 1)
        g_sel = sig("g_sel", 1)
        g_tr = sig("g_tr", 1)
        g_hi = sig("g_hi", 1)
        g_lo = sig("g_lo", 1)
        gm_set = sig("gm_set", 1)
        pos_ps = sig("pos_ps", 1)
        oh_set = sig("oh_set", 1)
        most_set = sig("most_set", 1)
        xt_ps = sig("xt_ps", 12)
        xt_ev = sig("xt_ev", 12)
        gt_h = sig("gt_h", 1)
        gt_l = sig("gt_l", 1)
        xg_ps = sig("xg_ps", 20)
        xg_ev = sig("xg_ev", 20)
        ot_ps = sig("ot_ps", GROUPS)
        ot_ev = sig("ot_ev", GROUPS)
        yg_hi = sig("yg_hi", 2 * GROUPS)
        yg_lo = sig("yg_lo", 2 * GROUPS, 2)
        sums = sig("sums", 2)
        gb_ps = sig("gb_ps", EXPERTS)
        u_tanh = sig("u_tanh", 2 * (EXPERTS + 1))
        u_free = sig("u_free", 2 * (EXPERTS + 1))
        u_prod = sig("u_prod", 2 * (EXPERTS + 1))
        u_hi = sig("u_hi", 2 * (EXPERTS + 1))
        u_lo = sig("u_lo", 2 * (EXPERTS + 1))

        N_CONST = 16
        block = ctx.enter_context(nc.Block())

        @block.sync
        def _(sp):
            sp.dma_start(xT[:, :], d["x"]).then_inc(x_in.sem, 16)
            for s in range(SLOTS):
                sp.dma_start(w32[:, s, :], d["w"][s * P:(s + 1) * P, :]).then_inc(loaded[s].sem, 16)
            for dst, name in ((par[:, :], "par"), (ident[:, :], "ident"), (mmask[:, :], "mmask"),
                              (scan_keep[:, :], "scan_keep"), (mats16[:, :, :], "mats16"), (slot_no[:, :], "slot_no"),
                              (m_init[:, :], "m_init"),
                              (head_sel[:, :, :], "head_sel"), (cosT[:, :], "cos"), (sinT[:, :], "sin"),
                              (att_mask, "att_mask"),
                              (rw[:, :, :], "rw"), (exp_sel[:, :], "exp_sel"),
                              (rank4[:, :, :], "rank4"), (rank16[:, :, :], "rank16")):
                sp.dma_start(dst, d[name]).then_inc(consts_in.sem, 16)
            sp.dma_start(rb[:, :, :].rearrange("p a e -> p (a e)"),
                         d["rb"].partition_broadcast(P)).then_inc(consts_in.sem, 16)
            with sp.Fori(1, L * NB // SLOTS) as i:
                for s in range(SLOTS):
                    sp.wait_ge(lo_done.sem, i * SLOTS + (s + 1 - SLOTS))
                    sp.dma_start(w32[:, s, :], d["w"][bass.ds(i * (SLOTS * P) + s * P, P), :]
                                 ).then_inc(loaded[s].sem, 16)

        @block.gpsimd
        def _(pool):
            nc.gpsimd.memset(ones[:, :], 1.0).then_inc(consts_set.sem, 1)
            nc.gpsimd.memset(ones_dm[:, :], 1.0 / DM).then_inc(consts_set.sem, 1)
            nc.gpsimd.memset(eps_col[:, :], EPS).then_inc(consts_set.sem, 1)
            nc.gpsimd.memset(m_at[:, :], 0.0).then_inc(consts_set.sem, 1)
            nc.gpsimd.memset(stat[:, :, :], 1.0).then_inc(consts_set.sem, 1)
            nc.gpsimd.memset(gm16[:, :, :], 0.0).then_inc(consts_set.sem, 1)
            for first in (num_ps, att_done, dc_ps, h_done, g_done, s_ps, sp_ps, o_lo, t_sb, stored,
                          m_used, yg_lo):
                pool.sem_inc(first.sem, first.before)

        N_SET = 6

        @block.scalar
        def _(act):
            A = nc.scalar.activation

            def hi_at(l, n, s):
                act.wait_ge(loaded[s].sem, l * loaded[s].per + (n + (SLOTS - s)) * (16 // SLOTS))
                act.wait_ge(blk_done.sem, blk_done.value(l, n + (1 - SLOTS)))
                A(whi[:, s, :], w32[:, s, :], ACT.Copy, scale=WS).then_inc(hi_done.sem, 1)

            def ln_scalar(l, k, gain, bias):
                act.wait_ge(ln_ps.sem, ln_ps.value(l, KD * (k + 1)))
                A(mu[:, 0, :], bank[4 + 2 * k][:, 0:T], ACT.Copy)
                A(mu[:, 1, :], bank[4 + 2 * k][:, 0:T], ACT.Square).then_inc(ln_mu.sem, 1)
                act.wait_ge(ln_var.sem, ln_var.value(l, k + 1))
                A(var[:, 1, :], var[:, 0, :], ACT.Sqrt, bias=eps_col[:, 0:1]).then_inc(ln_std.sem, 1)
                for c in range(KD):
                    act.wait_ge(ln_t.sem, ln_t.value(l, KD * k + c + 1))
                    A(xT[:, c * T:(c + 1) * T], acc[:, c * T:(c + 1) * T], ACT.Identity,
                      scale=par_c[:, gain + c:gain + c + 1], bias=par_c[:, bias + c:bias + c + 1])
                    A(xhi[:, c, :], acc[:, c * T:(c + 1) * T], ACT.Identity,
                      scale=par_x[:, gain + c:gain + c + 1],
                      bias=par_x[:, bias + c:bias + c + 1]).then_inc(x_hi.sem, 1)

            def square(l, k, c):
                act.wait_ge(y_done.sem, y_done.value(l, KD * k + c + 1))
                if c >= 4:
                    act.wait_ge(ln_ps.sem, ln_ps.value(l, KD * k + c - 3))
                A(ysq[:, c % 4, :], acc[:, c * T:(c + 1) * T], ACT.Square).then_inc(y_sq.sem, 1)

            act.wait_ge(x_in.sem, 16)
            for c in range(KD):
                A(xhi[:, c, :], xT[:, c * T:(c + 1) * T], ACT.Copy, scale=XS).then_inc(x_hi.sem, 1)
            act.wait_ge(consts_set.sem, N_SET)
            act.wait_ge(consts_in.sem, 16 * N_CONST)

            with act.Fori(0, L) as l:
                def hi_first(n):
                    act.wait_ge(loaded[n].sem, loaded[n].value(l, 16))
                    A(whi[:, n, :], w32[:, n, :], ACT.Copy, scale=WS).then_inc(hi_done.sem, 1)

                def hi_lead(g):
                    n = g + LEAD
                    if n < SLOTS:
                        hi_first(n)
                    elif n < NB:
                        hi_at(l, n, n % SLOTS)

                act.wait_ge(x_split.sem, x_split.value(l, 0))
                W4 = MH * (DH + 1)
                for dst, src in ((cache, d["cache"][bass.ds(l * P, P), :]),
                                 (kr[:, 0:PAST], d["krope"][bass.ds(l * ROPE, ROPE), :]),
                                 (rows[:, :], d["rows"][bass.ds(l, 1), :].broadcast_to([P, 4 * GW])),
                                 (ws_t[:, :], d["ws_t"][bass.ds(l * P, P), :]),
                                 (bs_row[:, :], d["bs_row"][bass.ds(l, 1), :]),
                                 (c_init[:, :], d["c_init"][bass.ds(l * P, P), :])):
                    act.dma_start(dst, src).then_inc(layer_in.sem, 16)
                for n in range(LEAD):
                    hi_first(n)
                layer_par = par[:, bass.ds(l * NPAR, NPAR)]
                A(par_c[:, :], layer_par, ACT.Copy)
                A(par_h[:, :], layer_par, ACT.Copy, scale=0.5)
                A(par_x[:, :], layer_par, ACT.Copy, scale=XS).then_inc(pars.sem, 1)
                act.wait_ge(pars.sem, pars.value(l, 1))

                for g in range(6):
                    hi_lead(g)
                    act.wait_ge(blk_done.sem, blk_done.value(l, g + 1))
                    A(zf[:, g, :], bank[g % 4][:, 0:T], ACT.Identity, scale=UN,
                      bias=par_c[:, C_FRONT + g:C_FRONT + g + 1]).then_inc(z_ev.sem, 1)
                    if g == 1:
                        act.wait_ge(f_abs.sem, f_abs.value(l, 1))
                        A(r_f[:, 2, :], r_f[:, 1, :], ACT.Exp, scale=-1.0)
                        act.drain()
                        A(r_f[:, 3, :], r_f[:, 2, :], ACT.Ln, bias=1.0).then_inc(f_ln.sem, 1)
                    if g == 2:
                        act.wait_ge(layer_in.sem, layer_in.value(l, 96))
                        A(kv_hi[:, :, 0:PAST], cache.rearrange("p (k t) -> p k t", k=2), ACT.Copy,
                          scale=XS).then_inc(c_hi.sem, 1)
                    if g == 3:
                        act.wait_ge(z_ev.sem, z_ev.value(l, 3))
                        A(ysq[:, 0:2, :], zf[:, 1:3, :], ACT.Square).then_inc(sq_c.sem, 1)
                    if g == 5:
                        act.wait_ge(z_ev.sem, z_ev.value(l, 5))
                        A(ysq[:, 2:4, :], zf[:, 3:5, :], ACT.Square).then_inc(sq_c.sem, 1)
                for i in range(4):
                    hi_lead(6 + i)
                    if i == 1:
                        for k in range(2):
                            act.wait_ge(rms_ps.sem, rms_ps.value(l, k + 1))
                            A(rstd[:, k, :], bank[4 + k][:, 0:T], ACT.Sqrt, scale=DM / RANK,
                              bias=eps_col[:, 0:1]).then_inc(rms_std.sem, 1)
                        act.wait_ge(r_arg.sem, r_arg.value(l, 1))
                        A(r_x[:, 1:4, :], r_x[:, 1:4, :], ACT.Exp).then_inc(r_exp.sem, 1)
                    if i == 3:
                        act.wait_ge(z_norm.sem, z_norm.value(l, 2))
                        A(cq_hi[:, 0, :], znorm[:, 0, :], ACT.Copy, scale=par_x[:, C_QG:C_QG + 1])
                        A(cq_hi[:, 1, :], znorm[:, 1, :], ACT.Copy,
                          scale=par_x[:, C_QG + 1:C_QG + 2]).then_inc(c_hi.sem, 1)
                        act.wait_ge(stored.sem, stored.value(l, 0))
                        for c in range(2):
                            A(kv_out[:, c, :], znorm[:, 2 + c, :], ACT.Copy,
                              scale=par_c[:, C_KVG + c:C_KVG + c + 1])
                        A(kv_hi[:, 0, PAST:KEYS], znorm[:, 2, :], ACT.Copy,
                          scale=par_x[:, C_KVG:C_KVG + 1])
                        A(kv_hi[:, 1, PAST:KEYS], znorm[:, 3, :], ACT.Copy,
                          scale=par_x[:, C_KVG + 1:C_KVG + 2]).then_inc(c_hi.sem, 1)
                    act.wait_ge(tokv.sem, tokv.value(l, i + 1))
                    A(gvt[:, 0:2, i * P:(i + 1) * P], gvt[:, 0:2, i * P:(i + 1) * P], ACT.Gelu_apprx_tanh)
                    A(gvt[0:TS, 2, i * P:(i + 1) * P], gvt[0:TS, 2, i * P:(i + 1) * P],
                      ACT.Gelu_apprx_tanh).then_inc(gv_act.sem, 1)
                act.wait_ge(c_hi.sem, c_hi.value(l, 3))
                act.dma_start(d["ckv"][bass.ds(l * P, P), :],
                              kv_out[:, :, :].rearrange("p k t -> p (k t)")).then_inc(stored.sem, 16)
                act.wait_ge(kr_done.sem, kr_done.value(l, 1))
                act.dma_start(d["kr_out"][bass.ds(l * ROPE, ROPE), :],
                              kr[:, PAST:KEYS]).then_inc(stored.sem, 16)
                act.dma_start(d["m_out"][bass.ds(l * MH, MH), :], m_at[:, :]).then_inc(stored.sem, 16)
                for h in range(MH):
                    for j, dst in ((1, mrow_i), (2, mrow_e)):
                        n = 3 * h + j
                        act.wait_ge(bc_ps.sem, bc_ps.value(l, n + 1))
                        A(dst[:, h * T:(h + 1) * T], bank[4 + n % 4][:, 0:T], ACT.Copy
                          ).then_inc(bc_ie.sem, 1)
                act.wait_ge(gv_var.sem, gv_var.value(l, 1))
                A(stat[:, :, 2:3], stat[:, :, 1:2], ACT.Sqrt, bias=eps_col[:, 0:1]).then_inc(gv_std.sem, 1)
                act.wait_ge(gv_done.sem, gv_done.value(l, 1))
                act.dma_start(d["gv_out"][bass.ds(l * TS, TS), :], gvt[0:TS, 2, :]).then_inc(stored.sem, 16)

                with act.Fori(0, MH) as h:
                    g0 = h * MPER + M0

                    def evac(step, dst, func, par_t, col, scale=UN):
                        act.wait_ge(blk_done.sem, blk_done.value(l, g0 + (step + 1)))
                        A(dst, bank[(M0 + step) % 4][:, 0:T], func, scale=scale,
                          bias=par_t[:, bass.ds(col, 1)]).then_inc(z_ev.sem, 1)

                    def hi_m(step):
                        hi_at(l, g0 + (step + LEAD), (M0 + step + LEAD) % SLOTS)

                    hi_m(0)
                    act.wait_ge(num_ps.sem, num_ps.value(l, h))
                    evac(0, mq[:, :], ACT.Identity, par_c, h * 4 + C_MLSTM)
                    hi_m(1)
                    evac(1, mk[:, :], ACT.Identity, par_c, h * 4 + (C_MLSTM + 1))
                    hi_m(2)
                    act.wait_ge(att_done.sem, att_done.value(l, h))
                    act.wait_ge(cols_sb.sem, cols_sb.value(l, 1))
                    act.wait_ge(bc_m.sem, bc_m.value(l, MH))
                    for i, (t0, n) in enumerate(TILES):
                        a = A(dec_w[0:n, i, 0:n], mrow_m[0:n, bass.ds(h * T + t0, n)], ACT.Exp,
                              bias=cols[0:n, bass.ds(h + i * MH, 1)])
                    a.then_inc(dec_done.sem, 1)
                    act.wait_ge(k_tr.sem, k_tr.value(l, h + 1))
                    act.wait_ge(dc_ps.sem, dc_ps.value(l, h))
                    A(k_tok[:, 0:2, :], bank[4][:, 0:2 * P].rearrange("p (i n) -> p i n", i=2), ACT.Copy)
                    A(k_tok[0:TS, 2, :], bank[4][0:TS, 2 * P:3 * P], ACT.Copy).then_inc(k_sb.sem, 1)
                    hi_m(3)
                    act.wait_ge(h_done.sem, h_done.value(l, h))
                    evac(3, mo[:, :], ACT.Tanh, par_h, h * 4 + (C_MLSTM + 2), scale=UN / 2)
                    hi_m(4)
                    act.wait_ge(g_done.sem, g_done.value(l, h))
                    evac(4, gu[:, :], ACT.Gelu_apprx_tanh, par_c, h * 4 + (C_MLSTM + 3))
                    for j in range(3):
                        hi_m(5 + j)
                        evac(5 + j, gates[:, bass.ds((h * 3 + j) * T, T)], ACT.Tanh, par_h,
                             h * 3 + (C_GATE + j), scale=UN / 2)
                    act.wait_ge(st_done.sem, st_done.value(l, h + 1))
                    act.dma_start(d["c_prompt"][bass.ds((l * MH + h) * P, P), :], c_st[:, 3, :]
                                  ).then_inc(stored.sem, 16)
                    act.dma_start(d["c_sample"][bass.ds((l * MH + h) * P, P), :], c_st[:, 5, :]
                                  ).then_inc(stored.sem, 16)
                    act.wait_ge(h_done.sem, h_done.value(l, h + 1))
                    A(br_hi[:, bass.ds((h + 4) * T, T)], hout[:, :], ACT.Copy, scale=XS / 2
                      ).then_inc(bc_hi.sem, 1)
                    act.wait_ge(g_done.sem, g_done.value(l, h + 1))
                    A(br_hi[:, bass.ds((h + 8) * T, T)], gout[:, :], ACT.Copy, scale=XS
                      ).then_inc(bc_hi.sem, 1)

                with act.Fori(0, 2) as hf:
                    g0 = hf * APER + A0

                    def hi_a(step):
                        hi_at(l, g0 + (step + LEAD), (A0 + step + LEAD) % SLOTS)

                    hi_a(0)
                    act.wait_ge(blk_done.sem, blk_done.value(l, g0 + 1))
                    act.wait_ge(s_ps.sem, s_ps.value(l, hf * 6))
                    for j in range(4):
                        r0 = NOPE * (j % 2)
                        a = A(q_att[0:NOPE, j, :], bank[4 + j // 2][r0:r0 + NOPE, 0:T], ACT.Copy,
                              scale=UN)
                    a.then_inc(q_ev.sem, 1)
                    hi_a(1)
                    act.wait_ge(blk_done.sem, blk_done.value(l, g0 + 2))
                    for j in range(4):
                        for r in range(2):
                            a = A(k_att[0:NOPE, 2 * (j // 2) + r, (j % 2) * KH:(j % 2 + 1) * KH],
                                  bank[j][NOPE * r:NOPE * (r + 1), 0:KH], ACT.Copy, scale=UN)
                        a.then_inc(z_ev.sem, 1)

                    def gate_tanh(j):
                        act.wait_ge(blk_done.sem, blk_done.value(l, g0 + (3 + j)))
                        A(gates[:, bass.ds((hf * 6 + (12 + j)) * T, T)],
                          bank[(A0 + 2 + j) % 4][:, 0:T], ACT.Tanh, scale=UN / 2,
                          bias=par_h[:, bass.ds(hf * 6 + (C_GATE + 12 + j), 1)]).then_inc(z_ev.sem, 1)

                    def exps(j):
                        u = hf * 6 + j
                        act.wait_ge(s_max.sem, s_max.value(l, u + 1))
                        if j >= 2:
                            act.wait_ge(t_ps.sem, t_ps.value(l, u - 1))
                        b = bank[4 + j % 2]
                        if j % 3 < 2:
                            A(prob[:, j % 2, 0:P], b[:, 0:P], ACT.Exp, scale=ATT_SCALE,
                              bias=sm[:, 2:3], accum_out=sm[:, 4:5])
                            A(prob[:, j % 2, P:3 * P], b[:, P:3 * P], ACT.Exp, scale=ATT_SCALE,
                              bias=sm[:, 3:4], accum_out=sm[:, 5:6]).then_inc(p_exp.sem, 1)
                        else:
                            A(prob[:, j % 2, 0:T], b[:, 0:T], ACT.Exp, scale=ATT_SCALE,
                              bias=sm[:, 2:3], accum_out=sm[:, 4:5]).then_inc(p_exp.sem, 1)

                    def probs_out(j):
                        u = hf * 6 + j
                        act.wait_ge(t_ps.sem, t_ps.value(l, u + 1))
                        if j >= 2:
                            act.wait_ge(o_ps.sem, o_ps.value(l, u - 1))
                        if j % 3 < 2:
                            A(prob_t[:, j % 2, :, :], bank[6][:, 0:3 * P].rearrange(
                                "p (i n) -> p i n", i=3), ACT.Copy).then_inc(t_sb.sem, 1)
                        else:
                            A(prob_t[:, j % 2, 0:2, :], bank[6][:, 0:2 * P].rearrange(
                                "p (i n) -> p i n", i=2), ACT.Copy)
                            A(prob_t[0:TS, j % 2, 2, :], bank[6][0:TS, 2 * P:3 * P], ACT.Copy
                              ).then_inc(t_sb.sem, 1)

                    def out_hi(p):
                        act.wait_ge(o_ps.sem, o_ps.value(l, hf * 6 + (3 * p + 3)))
                        A(br_hi[:, bass.ds((hf * 2 + p) * T, T)], bank[7][:, 0:T], ACT.Copy,
                          scale=XS).then_inc(o_hi.sem, 1)

                    for j in range(6):
                        hi_a(2 + j)
                        if j:
                            gate_tanh(j - 1)
                        if j == 5:
                            out_hi(0)
                        exps(j)
                        if j:
                            probs_out(j - 1)
                    gate_tanh(5)
                    probs_out(5)
                    out_hi(1)

                with act.Fori(0, 3) as k:
                    for j in range(4):
                        hi_at(l, k * 4 + (B0 + j + LEAD), (B0 + j + LEAD) % SLOTS)
                act.wait_ge(m_used.sem, m_used.value(l, 24))
                for c in range(KD):
                    A(mhi[:, c, :], acc[:, c * T:(c + 1) * T], ACT.Copy, scale=UN * XS / 2
                      ).then_inc(m_hi.sem, 1)
                act.wait_ge(m_lo.sem, m_lo.value(l, KD))
                A(acc[:, :], xT[:, :], ACT.Copy, scale=ALPHA).then_inc(acc_pre.sem, 1)

                for c in range(KD):
                    hi_lead(O0 + c)
                    square(l, 0, c)
                ln_scalar(l, 0, C_L1G, C_L1B)
                act.drain()
                A(acc[:, :], xT[:, :], ACT.Copy, scale=ALPHA).then_inc(acc_pre.sem, 1)

                UPB = [(U0 + j) % 4 for j in range(4)]
                UE = 2 * (EXPERTS + 1)

                def x_tokens(j):
                    for n in range(3 * j, 3 * j + 3):
                        act.wait_ge(xt_ps.sem, xt_ps.value(l, n + 1))
                        A(x_tok[:, n * 512:(n + 1) * 512], bank[4 + n % 3][:, :], ACT.Copy
                          ).then_inc(xt_ev.sem, 1)

                hi_lead(U0)
                act.wait_ge(r_ps.sem, r_ps.value(l, 1))
                A(rt[:, 0, :, :], bank[7][:, 0:3 * EXPERTS].rearrange("p (i e) -> p i e", i=3), ACT.Exp,
                  scale=-1.0).then_inc(r_e.sem, 1)
                hi_lead(U0 + 1)
                x_tokens(0)
                for f in range(2):
                    act.wait_ge(blk_done.sem, blk_done.value(l, U0 + 2 * f + 1))
                    if f:
                        hi_lead(U0 + 2)
                        hi_lead(U0 + 3)
                        act.wait_ge(u_free.sem, u_free.value(l, f))
                    A(ht[:, :], bank[UPB[2 * f]][:, 0:T], ACT.Tanh, scale=UN / 2).then_inc(u_tanh.sem, 1)
                    if f == 0:
                        x_tokens(1)
                        act.wait_ge(g_sel.sem, g_sel.value(l, 1))
                        A(gt_hi[:, :, :], rt[:, 7], ACT.Copy, scale=GS).then_inc(gt_h.sem, 1)
                    else:
                        x_tokens(2)
                        x_tokens(3)
                        act.wait_ge(most_set.sem, most_set.value(l, 1))
                    act.wait_ge(u_prod.sem, u_prod.value(l, f + 1))
                    A(hhi[:, f * T:(f + 1) * T], h2[:, :], ACT.Copy, scale=UN * UN * XS / 2
                      ).then_inc(u_hi.sem, 1)

                def expert_hi(e, W, h0, between=None):
                    g0 = e * 4 + (U0 + 4)
                    for f in range(2):
                        hi_at(l, g0 + (2 * f + LEAD), (U0 + 2 * f + LEAD) % SLOTS)
                        hi_at(l, g0 + (2 * f + 1 + LEAD), (U0 + 2 * f + 1 + LEAD) % SLOTS)
                        n = e * 2 + (2 + f)
                        act.wait_ge(blk_done.sem, blk_done.value(l, g0 + (2 * f + 1)))
                        act.wait_ge(u_free.sem, u_free.value(l, n))
                        A(ht[:, 0:W], bank[UPB[2 * f]][:, 0:W], ACT.Tanh, scale=UN / 2
                          ).then_inc(u_tanh.sem, 1)
                        if f == 0 and between:
                            between()
                        act.wait_ge(u_prod.sem, u_prod.value(l, n + 1))
                        A(hhi[:, bass.ds((e * 2 + f) * W + h0, W)], h2[:, 0:W], ACT.Copy,
                          scale=UN * UN * XS / (2 * GS)).then_inc(u_hi.sem, 1)

                fits = act.value_load(most_i[0:1, 0:1]) < CAP + 1
                with act.If(fits):
                    for q in range(4):
                        act.wait_ge(xg_ps.sem, xg_ps.value(l, q + 1))
                        A(x_grp[:, 0, q // 2, 4 * (q % 2):4 * (q % 2) + 4, :], bank[5 + q % 2][:, :]
                          .rearrange("p (k n) -> p k n", k=4), ACT.Copy).then_inc(xg_ev.sem, 1)
                    act.wait_ge(g_tr.sem, g_tr.value(l, 1))
                    A(gate_hi[0:EXPERTS, :], bank[7][0:EXPERTS, :], ACT.Copy).then_inc(g_hi.sem, 1)
                    with act.Fori(0, GROUPS // 2) as gg:
                        for g2 in range(2):
                            act.wait_ge(ot_ps.sem, ot_ps.value(l, gg * 2 + (g2 + 1)))
                            A(slot_tok[:, bass.ds((gg * 2 + g2) * T, T)], bank[7][:, 0:T], ACT.Copy,
                              scale=1 / (UN * XS)).then_inc(ot_ev.sem, 1)
                            with act.Fori(0, 4) as q:
                                def gathered():
                                    act.wait_ge(xg_ps.sem, xg_ps.value(l, gg * 8 + q + (4 * g2 + 5)))
                                    A(f16_b[:, bass.ds(q * 512 + (HEND + (1 - g2) * 2048), 512)],
                                      bank[5][:, :], ACT.Copy).then_inc(xg_ev.sem, 1)

                                expert_hi(gg * 8 + q + 4 * g2, CAP, H0, gathered)
                    def group_out(g, g2, hf):
                        act.wait_ge(blk_done.sem, blk_done.value(l, g * 4 + ((D0, D1)[hf] + 5)))
                        A(y_hi[:, bass.ds(g * 512, 512)], bank[(4, 2)[hf] + g2][:, :], ACT.Copy,
                          scale=UN * XS).then_inc(yg_hi.sem, 1)

                    hi_lead(D0)
                    with act.Fori(0, GROUPS // 2) as gg:
                        for g2 in range(2):
                            for j in range(4):
                                n = D0 + 1 + 4 * g2 + j + LEAD
                                hi_at(l, gg * 8 + n, n % SLOTS)
                            group_out(gg * 2 + g2, g2, 0)
                    hi_lead(D1)
                    for c in range(4):
                        square(l, 1, c)
                    for g in range(GROUPS):
                        for j in range(4):
                            hi_lead(D1 + 1 + 4 * g + j)
                        group_out(g, g % 2, 1)
                with act.Else():
                    for s_, n in ((xg_ev, 20), (ot_ev, GROUPS), (yg_hi, 2 * GROUPS)):
                        act.sem_inc(s_.sem, n)
                    act.wait_ge(g_tr.sem, g_tr.value(l, 1))
                    A(gate32[:, 0:TP], bank[6][0:EXPERTS, 0:TP], ACT.Copy, scale=GS)
                    A(gate32[:, TP:T], bank[6][0:EXPERTS, 3 * P - TS:3 * P], ACT.Copy, scale=GS)
                    A(gate_hi[0:EXPERTS, 0:TP], bank[6][0:EXPERTS, 0:TP], ACT.Copy, scale=GS)
                    A(gate_hi[0:EXPERTS, TP:T], bank[6][0:EXPERTS, 3 * P - TS:3 * P], ACT.Copy, scale=GS
                      ).then_inc(g_hi.sem, 1)
                    with act.Fori(0, EXPERTS) as e:
                        expert_hi(e, T, H0)
                    hi_lead(D0)
                    with act.Fori(0, 4) as i:
                        for j in range(4):
                            hi_at(l, i * 4 + (D0 + 1 + j + LEAD), (D0 + 1 + j + LEAD) % SLOTS)
                    hi_lead(D1)
                    for c in range(4):
                        square(l, 1, c)
                    with act.Fori(0, 3) as i:
                        for j in range(4):
                            hi_at(l, i * 4 + (D1 + 1 + j + LEAD), (D1 + 1 + j + LEAD) % SLOTS)
                    for j in range(4):
                        hi_lead(D1 + 13 + j)
                for c in range(4, KD):
                    square(l, 1, c)
                ln_scalar(l, 1, C_L2G, C_L2B)

            act.wait_ge(x_hi.sem, x_hi.value(L, 0))
            act.dma_start(d["y"], xT[:, :]).then_inc(stored.sem, 16)
            act.wait_ge(stored.sem, stored.value(L, 16))

        @block.vector
        def _(dve):
            V = nc.vector

            def lo_at(l, n, s):
                dve.wait_ge(hi_done.sem, hi_done.value(l, n + 1))
                V.scalar_tensor_tensor(wlo[:, s, :], w32[:, s, :], WS, whi[:, s, :], ALU.mult,
                                       ALU.subtract).then_inc(lo_done.sem, 1)

            def ln_vector(l, k):
                dve.wait_ge(ln_mu.sem, ln_mu.value(l, k + 1))
                V.tensor_tensor(var[:, 0, :], bank[5 + 2 * k][:, 0:T], mu[:, 1, :], ALU.subtract)
                dve.drain()
                V.tensor_scalar(var[:, 0, :], var[:, 0, :], 0.0, None, ALU.max).then_inc(ln_var.sem, 1)
                y = [acc[:, c * T:(c + 1) * T] for c in range(KD)]
                V.tensor_tensor(y[0], y[0], mu[:, 0, :], ALU.subtract)
                dve.wait_ge(ln_std.sem, ln_std.value(l, k + 1))
                V.reciprocal(ln_r[:, :], var[:, 1, :])

                def split(c):
                    dve.wait_ge(x_hi.sem, x_hi.value(l, KD * k + c + 1))
                    V.scalar_tensor_tensor(xlo[:, c, :], xT[:, c * T:(c + 1) * T], XS, xhi[:, c, :],
                                           ALU.mult, ALU.subtract).then_inc(x_split.sem, 1)

                for c in range(KD):
                    dve.drain()
                    V.tensor_tensor(y[c], y[c], ln_r[:, :], ALU.mult).then_inc(ln_t.sem, 1)
                    if c + 1 < KD:
                        V.tensor_tensor(y[c + 1], y[c + 1], mu[:, 0, :], ALU.subtract)
                    if c:
                        split(c - 1)
                split(KD - 1)

            def residual(l, k, c, b):
                V.scalar_tensor_tensor(acc[:, c * T:(c + 1) * T], bank[b][:, 0:T], UN,
                                       acc[:, c * T:(c + 1) * T], ALU.mult, ALU.add
                                       ).then_inc(y_done.sem, 1)

            for c in range(KD):
                dve.wait_ge(x_hi.sem, c + 1)
                V.scalar_tensor_tensor(xlo[:, c, :], xT[:, c * T:(c + 1) * T], XS, xhi[:, c, :],
                                       ALU.mult, ALU.subtract).then_inc(x_split.sem, 1)
            dve.wait_ge(consts_set.sem, N_SET)
            dve.wait_ge(consts_in.sem, 16 * N_CONST)

            with dve.Fori(0, L) as l:
                def lo_lead(g):
                    n = g + LEAD
                    if n < NB:
                        lo_at(l, n, n % SLOTS)

                lo_at(l, 0, 0)
                lo_at(l, 1, 1)
                dve.wait_ge(stored.sem, stored.value(l, 0))
                V.tensor_scalar(scan_drop, scan_keep[:, :], -1.0, -NEG, ALU.add, ALU.mult)
                V.tensor_copy(m_at[:, 5:6], m_init[:, bass.ds(l, 1)])

                lo_lead(0)
                dve.wait_ge(z_ev.sem, z_ev.value(l, 1))
                V.tensor_copy(r_f[:, 0, :], zf[32:32 + MH, 0, :])
                dve.drain()
                V.scalar_tensor_tensor(r_f[:, 1, :], r_f[:, 0, :], -1.0, r_f[:, 0, :], ALU.mult, ALU.max
                                       ).then_inc(f_abs.sem, 1)
                lo_lead(1)
                lo_lead(2)
                dve.wait_ge(f_ln.sem, f_ln.value(l, 1))
                V.scalar_tensor_tensor(r_f[:, 0, :], r_f[:, 0, :], 0.0, r_f[:, 3, :], ALU.min,
                                       ALU.subtract)
                dve.drain()
                V.tensor_tensor_scan(r_b, scan_keep[:, :], r_f[:, 0, :], 0.0, ALU.mult, ALU.add)
                dve.drain()
                V.tensor_tensor(r_a, zf[0:MH, 0, :], r_b, ALU.subtract)
                dve.drain()
                V.tensor_tensor_scan(r_m, scan_drop, r_a, 0.0, ALU.add, ALU.max)
                lo_lead(3)
                dve.wait_ge(c_hi.sem, c_hi.value(l, 1))
                V.scalar_tensor_tensor(kv_lo[:, :, 0:PAST], cache.rearrange("p (k t) -> p k t", k=2),
                                       XS, kv_hi[:, :, 0:PAST], ALU.mult, ALU.subtract
                                       ).then_inc(c_lo.sem, 1)
                ws3 = ws_t[:, :].rearrange("p (n t) -> p n t", t=P)
                V.tensor_tensor(ws3, ws3, mats16[:, 1:2, :].broadcast_to([P, 4, P]), ALU.mult
                                ).then_inc(ws_masked.sem, 1)
                for c in range(NCH):
                    s = c if c < 4 else 5
                    e = (c + 1) * CH - 1
                    dve.drain()
                    V.scalar_tensor_tensor(m_at[:, s + 1:s + 2], r_m[:, e:e + 1], m_at[:, s:s + 1],
                                           r_b[:, e:e + 1], ALU.max, ALU.add)
                dve.drain()
                m_p = m_at[:, 0:4].unsqueeze(2).broadcast_to([MH, 4, CH])
                rm_p = r_m[:, 0:TP].rearrange("p (c t) -> p c t", t=CH)
                V.tensor_tensor(rm_p, rm_p, m_p, ALU.max)
                V.tensor_scalar(r_m[:, TP:T], r_m[:, TP:T], m_at[:, 5:6], None, ALU.max)
                dve.drain()
                V.tensor_scalar(r_x[:, 0, :], r_m, -1.0, None, ALU.mult)
                dve.drain()

                def chunks(ap):
                    return ap.rearrange("p (c t) -> p c t", t=CH)

                V.tensor_tensor(chunks(r_x[:, 1, 0:TP]), chunks(r_x[:, 0, 0:TP]), m_p, ALU.add)
                V.tensor_scalar(r_x[:, 1, TP:T], r_x[:, 0, TP:T], m_at[:, 5:6], None, ALU.add)
                V.tensor_tensor(r_x[:, 2, :], r_x[:, 0, :], r_b, ALU.subtract)
                V.tensor_tensor(chunks(r_x[:, 3, :]), chunks(r_a),
                                chunks(r_x[:, 0, :])[:, :, CH - 1:CH].broadcast_to([MH, NCH, CH]),
                                ALU.add).then_inc(r_arg.sem, 1)
                lo_lead(4)
                lo_lead(5)
                dve.wait_ge(z_ev.sem, z_ev.value(l, 6))
                V.tensor_tensor(kr_t[:, 0, :], zf[0:ROPE, 5, :], cosT[0:ROPE, :], ALU.mult)
                V.tensor_tensor(kr_t[:, 1, :], zf[ROPE:2 * ROPE, 5, :], sinT[ROPE:2 * ROPE, :], ALU.mult)
                dve.drain()
                V.tensor_tensor(kr[:, PAST:KEYS], kr_t[:, 0, :], kr_t[:, 1, :], ALU.add
                                ).then_inc(kr_done.sem, 1)

                def tok_out(b, dst2, dst1, row, last):
                    V.scalar_tensor_tensor(dst2, bank[b][:, 0:2 * P].rearrange("p (i n) -> p i n", i=2),
                                           UN, row.unsqueeze(1).broadcast_to([P, 2, P]), ALU.mult,
                                           ALU.add)
                    V.scalar_tensor_tensor(dst1, bank[b][0:TS, 2 * P:3 * P], UN, row[0:TS, :],
                                           ALU.mult, ALU.add).then_inc(last.sem, 1)

                for i in range(4):
                    lo_lead(6 + i)
                    if i == 1:
                        for k in range(2):
                            dve.wait_ge(rms_std.sem, rms_std.value(l, k + 1))
                            V.reciprocal(rstd[:, k, :], rstd[:, k, :])
                            dve.drain()
                            V.tensor_tensor(znorm[:, 2 * k:2 * k + 2, :], zf[:, 1 + 2 * k:3 + 2 * k, :],
                                            rstd[:, k:k + 1, :].broadcast_to([P, 2, T]), ALU.mult
                                            ).then_inc(z_norm.sem, 1)
                    dve.wait_ge(blk_done.sem, blk_done.value(l, 7 + i))
                    tok_out((6 + i) % 4, gvt[:, 0:2, i * P:(i + 1) * P],
                            gvt[0:TS, 2, i * P:(i + 1) * P],
                            rows[:, i * P:(i + 1) * P], tokv)
                dve.wait_ge(c_hi.sem, c_hi.value(l, 2))
                V.scalar_tensor_tensor(cq_lo[:, 0, :], znorm[:, 0, :], par_x[:, C_QG:C_QG + 1],
                                       cq_hi[:, 0, :], ALU.mult, ALU.subtract)
                V.scalar_tensor_tensor(cq_lo[:, 1, :], znorm[:, 1, :], par_x[:, C_QG + 1:C_QG + 2],
                                       cq_hi[:, 1, :], ALU.mult, ALU.subtract).then_inc(c_lo.sem, 1)
                dve.wait_ge(c_hi.sem, c_hi.value(l, 3))
                V.scalar_tensor_tensor(kv_lo[:, 0, PAST:KEYS], znorm[:, 2, :],
                                       par_x[:, C_KVG:C_KVG + 1], kv_hi[:, 0, PAST:KEYS], ALU.mult,
                                       ALU.subtract)
                V.scalar_tensor_tensor(kv_lo[:, 1, PAST:KEYS], znorm[:, 3, :],
                                       par_x[:, C_KVG + 1:C_KVG + 2], kv_hi[:, 1, PAST:KEYS], ALU.mult,
                                       ALU.subtract).then_inc(c_lo.sem, 1)
                dve.wait_ge(cols_ps.sem, cols_ps.value(l, 1))
                V.tensor_copy(cols[:, 0:2 * MH], bank[7][:, 0:2 * MH])
                V.tensor_copy(cols[0:TS, 2 * MH:3 * MH], bank[7][0:TS, 2 * MH:3 * MH])
                V.tensor_scalar(cols[:, 3 * MH:5 * MH], bank[7][:, 3 * MH:5 * MH], KSCALE, None, ALU.mult)
                V.tensor_scalar(cols[0:TS, 5 * MH:6 * MH], bank[7][0:TS, 5 * MH:6 * MH], KSCALE, None,
                                ALU.mult).then_inc(cols_sb.sem, 1)
                for h in range(MH):
                    n = 3 * h
                    dve.wait_ge(bc_ps.sem, bc_ps.value(l, n + 1))
                    V.tensor_tensor(mrow_m[:, h * T:(h + 1) * T], bank[4 + n % 4][:, 0:T], mmask[:, :],
                                    ALU.add).then_inc(bc_m.sem, 1)
                dve.wait_ge(gv_act.sem, gv_act.value(l, 4))
                for i, (t0, n) in enumerate(TILES):
                    V.bn_stats(rp[0:n, i, :], gvt[0:n, i, :])
                dve.drain()
                for i, (t0, n) in enumerate(TILES):
                    a = V.bn_aggr(stat[0:n, i, 0:2], rp[0:n, i, :])
                a.then_inc(gv_var.sem, 1)
                dve.wait_ge(gv_std.sem, gv_std.value(l, 1))
                V.reciprocal(stat[:, :, 3:4], stat[:, :, 2:3])
                dve.drain()
                gain = rows[:, 2 * GW:3 * GW]
                bias = rows[:, 3 * GW:4 * GW]
                for i, (t0, n) in enumerate(TILES):
                    V.tensor_scalar(gvt[0:n, i, :], gvt[0:n, i, :], stat[0:n, i, 0:1],
                                    stat[0:n, i, 3:4], ALU.subtract, ALU.mult)
                dve.drain()
                for i, (t0, n) in enumerate(TILES):
                    V.tensor_tensor(gvt[0:n, i, :], gvt[0:n, i, :], gain[0:n, :], ALU.mult)
                dve.drain()
                for i, (t0, n) in enumerate(TILES):
                    a = V.tensor_tensor(gvt[0:n, i, :], gvt[0:n, i, :], bias[0:n, :], ALU.add)
                a.then_inc(gv_done.sem, 1)

                with dve.Fori(0, MH) as h:
                    g0 = h * MPER + M0

                    def lo_m(step):
                        lo_at(l, g0 + (step + LEAD), (M0 + step + LEAD) % SLOTS)

                    lo_m(0)
                    lo_m(1)
                    dve.wait_ge(z_ev.sem, z_ev.value(l, h * 7 + 7))
                    dve.wait_ge(bc_ie.sem, bc_ie.value(l, 2 * MH))
                    V.tensor_tensor(q_in[:, :], mq[:, :], mrow_i[:, bass.ds(h * T, T)], ALU.mult)
                    lo_m(2)
                    dve.wait_ge(blk_done.sem, blk_done.value(l, g0 + 3))
                    tok_out((M0 + 2) % 4, v_tok[:, 0:2, :], v_tok[0:TS, 2, :],
                            rows[:, bass.ds(h * P + GW, P)], tokv)
                    dve.drain()
                    for i, (t0, n) in enumerate(TILES):
                        w = cols[0:n, bass.ds(h + (3 + i) * MH, 1)]
                        V.tensor_scalar(v_ws[0:n, i, 0:DH], v_tok[0:n, i, :], w, None, ALU.mult)
                        a = V.tensor_copy(v_ws[0:n, i, DH:DH + 1], w)
                    a.then_inc(v_wsd.sem, 1)
                    dve.wait_ge(dec_done.sem, dec_done.value(l, h + 1))
                    dve.wait_ge(a_ps.sem, a_ps.value(l, h + 1))
                    V.scalar_tensor_tensor(att[:, 0:2, :], bank[5][:, 0:2 * P].rearrange(
                        "p (i n) -> p i n", i=2), KSCALE, dec_w[:, 0:2, :], ALU.mult, ALU.mult)
                    V.scalar_tensor_tensor(att[0:TS, 2, 0:TS], bank[5][0:TS, 2 * P:2 * P + TS], KSCALE,
                                           dec_w[0:TS, 2, 0:TS], ALU.mult, ALU.mult
                                           ).then_inc(att_done.sem, 1)
                    lo_m(3)
                    dve.wait_ge(dc_ps.sem, dc_ps.value(l, h + 1))
                    dve.wait_ge(stored.sem, stored.value(l, h * 32 + 64))

                    def decay(c):
                        return mrow_i[:, bass.ds(h * T + (c * CH + CH - 1), 1)]

                    W1 = DH + 1
                    V.tensor_copy(c_st[:, 4, :], c_init[:, bass.ds(h * W1, W1)])
                    V.tensor_copy(c_st[:, 0, :], bank[6][:, 0:W1])
                    dve.drain()
                    V.scalar_tensor_tensor(c_st[:, 5, :], c_st[:, 4, :], decay(4),
                                           bank[6][:, 2 * W1:3 * W1], ALU.mult, ALU.add)
                    V.scalar_tensor_tensor(c_st[:, 1, :], c_st[:, 0, :], decay(1),
                                           bank[7][:, 0:W1], ALU.mult, ALU.add)
                    dve.drain()
                    V.scalar_tensor_tensor(c_st[:, 2, :], c_st[:, 1, :], decay(2),
                                           bank[6][:, W1:2 * W1], ALU.mult, ALU.add)
                    dve.drain()
                    V.scalar_tensor_tensor(c_st[:, 3, :], c_st[:, 2, :], decay(3),
                                           bank[7][:, W1:2 * W1], ALU.mult, ALU.add)
                    for j, c in enumerate((0, 1, 2, 4)):
                        a = V.tensor_scalar(n_bc[:, j, :], ones[:, :], c_st[:, c, DH:DH + 1], None,
                                            ALU.mult)
                    a.then_inc(st_done.sem, 1)
                    lo_m(4)
                    dve.wait_ge(sp_ps.sem, sp_ps.value(l, h))
                    V.tensor_copy(vg[:, 0:2, :], gvt[:, 0:2, bass.ds(h * P, P)])
                    V.tensor_copy(vg[0:TS, 2, :], gvt[0:TS, 2, bass.ds(h * P, P)]).then_inc(vg_done.sem, 1)
                    lo_m(5)
                    dve.wait_ge(num_ps.sem, num_ps.value(l, h + 1))
                    dve.wait_ge(z_ev.sem, z_ev.value(l, h * 7 + 9))
                    V.tensor_scalar(hden[:, :], bank[5][:, 0:T], -1.0, None, ALU.mult)
                    dve.drain()
                    V.tensor_tensor(hden[:, :], hden[:, :], bank[5][:, 0:T], ALU.max)
                    dve.drain()
                    V.tensor_tensor(hden[:, :], hden[:, :], mrow_e[:, bass.ds(h * T, T)], ALU.max)
                    dve.drain()
                    V.reciprocal(hden[:, :], hden[:, :])
                    dve.drain()
                    V.scalar_tensor_tensor(hout[:, :], mo[:, :], 1.0, hden[:, :], ALU.add, ALU.mult)
                    dve.drain()
                    V.tensor_tensor(hout[:, :], hout[:, :], bank[4][:, 0:T], ALU.mult
                                    ).then_inc(h_done.sem, 1)
                    lo_m(6)
                    dve.wait_ge(sp_ps.sem, sp_ps.value(l, h + 1))
                    dve.wait_ge(z_ev.sem, z_ev.value(l, h * 7 + 10))
                    V.tensor_tensor(gout[:, :], gu[:, :], bank[6][:, 0:T], ALU.mult
                                    ).then_inc(g_done.sem, 1)
                    lo_m(7)
                    dve.wait_ge(bc_hi.sem, bc_hi.value(l, h * 2 + 1))
                    V.scalar_tensor_tensor(br_lo[:, bass.ds((h + 4) * T, T)], hout[:, :], XS / 2,
                                           br_hi[:, bass.ds((h + 4) * T, T)], ALU.mult, ALU.subtract
                                           ).then_inc(bc_lo.sem, 1)
                    dve.wait_ge(bc_hi.sem, bc_hi.value(l, h * 2 + 2))
                    V.scalar_tensor_tensor(br_lo[:, bass.ds((h + 8) * T, T)], gout[:, :], XS,
                                           br_hi[:, bass.ds((h + 8) * T, T)], ALU.mult, ALU.subtract
                                           ).then_inc(bc_lo.sem, 1)

                dve.wait_ge(num_ps.sem, num_ps.value(l, MH))
                V.tensor_copy(q_att[MROW:KATT, :, :],
                              att_mask[:, 0:T].unsqueeze(1).broadcast_to([2, 4, T]))
                V.tensor_copy(k_att[MROW:KATT, :, :],
                              att_mask[:, T:T + KEYS].unsqueeze(1).broadcast_to([2, 4, KEYS]))
                V.tensor_copy(k_att[NOPE:MROW, :, :],
                              kr.unsqueeze(1).broadcast_to([ROPE, 4, KEYS]))
                with dve.Fori(0, 2) as hf:
                    g0 = hf * APER + A0

                    def lo_a(step):
                        lo_at(l, g0 + (step + LEAD), (A0 + step + LEAD) % SLOTS)

                    lo_a(0)
                    dve.wait_ge(s_ps.sem, s_ps.value(l, hf * 6))
                    dve.wait_ge(blk_done.sem, blk_done.value(l, g0 + 1))
                    V.scalar_tensor_tensor(qr_t[:, 0, :], bank[6][:, 0:T], UN, cosT[:, :], ALU.mult,
                                           ALU.mult)
                    V.scalar_tensor_tensor(qr_t[:, 1, :], bank[7][:, 0:T], UN, sinT[:, :], ALU.mult,
                                           ALU.mult)
                    dve.drain()
                    for j in range(4):
                        rs = slice(ROPE * j, ROPE * (j + 1))
                        a = V.tensor_tensor(q_att[NOPE:MROW, j, :], qr_t[rs, 0, :], qr_t[rs, 1, :],
                                            ALU.add)
                    a.then_inc(q_rot.sem, 1)
                    lo_a(1)
                    dve.wait_ge(blk_done.sem, blk_done.value(l, g0 + 2))
                    for j in range(2):
                        V.tensor_scalar(v_kv[:, 2 * j:2 * j + 2, :], bank[4 + j][:, :].rearrange(
                            "p (i n) -> p i n", i=2), UN, None, ALU.mult)
                    V.tensor_scalar(v_kv[0:TS, 4, :], bank[6][0:TS, 0:2 * P], UN, None, ALU.mult
                                    ).then_inc(v_ev.sem, 1)

                    def out_lo(p):
                        dve.wait_ge(o_hi.sem, o_hi.value(l, hf * 2 + (p + 1)))
                        V.scalar_tensor_tensor(br_lo[:, bass.ds((hf * 2 + p) * T, T)],
                                               bank[7][:, 0:T], XS,
                                               br_hi[:, bass.ds((hf * 2 + p) * T, T)], ALU.mult,
                                               ALU.subtract).then_inc(o_lo.sem, 1)

                    for j in range(6):
                        lo_a(2 + j)
                        if j == 5:
                            out_lo(0)
                        u = hf * 6 + j
                        b = bank[4 + j % 2]
                        dve.wait_ge(s_ps.sem, s_ps.value(l, u + 1))
                        w = 2 if j % 3 < 2 else 1
                        if w == 2:
                            V.tensor_reduce(sm[:, 0:1], b[:, 0:P], AXX, ALU.max)
                            V.tensor_reduce(sm[:, 1:2], b[:, P:3 * P], AXX, ALU.max)
                        else:
                            V.tensor_reduce(sm[:, 0:1], b[:, 0:T], AXX, ALU.max)
                        dve.drain()
                        V.tensor_scalar(sm[:, 2:2 + w], sm[:, 0:w], -ATT_SCALE, None, ALU.mult
                                        ).then_inc(s_max.sem, 1)
                        dve.wait_ge(p_exp.sem, p_exp.value(l, u + 1))
                        V.reciprocal(sm[:, 6:6 + w], sm[:, 4:4 + w])
                        dve.drain()
                        if w == 2:
                            V.tensor_scalar(prob[:, j % 2, 0:P], prob[:, j % 2, 0:P], sm[:, 6:7], None,
                                            ALU.mult)
                            V.tensor_scalar(prob[:, j % 2, P:3 * P], prob[:, j % 2, P:3 * P],
                                            sm[:, 7:8], None, ALU.mult).then_inc(p_norm.sem, 1)
                        else:
                            V.tensor_scalar(prob[:, j % 2, 0:T], prob[:, j % 2, 0:T], sm[:, 6:7], None,
                                            ALU.mult).then_inc(p_norm.sem, 1)
                    out_lo(1)

                V.memset(acc[:, :], 0.0)
                with dve.Fori(0, 3) as k:
                    for j in range(4):
                        lo_at(l, k * 4 + (B0 + j + LEAD), (B0 + j + LEAD) % SLOTS)
                        dve.wait_ge(blk_done.sem, blk_done.value(l, k * 4 + (B0 + j + 1)))
                        dve.wait_ge(z_ev.sem, z_ev.value(l, 54))
                        for i in range(2):
                            c = 2 * j + i
                            V.scalar_tensor_tensor(mtmp[c % 2][:, :], gates[:, bass.ds((k * 8 + c) * T, T)], 1.0,
                                                   bank[c % 4][:, 0:T], ALU.add, ALU.mult)
                            dve.drain()
                            V.tensor_tensor(acc[:, c * T:(c + 1) * T], acc[:, c * T:(c + 1) * T],
                                            mtmp[c % 2][:, :], ALU.add).then_inc(m_used.sem, 1)
                for c in range(KD):
                    dve.wait_ge(m_hi.sem, m_hi.value(l, c + 1))
                    V.scalar_tensor_tensor(mlo[:, c, :], acc[:, c * T:(c + 1) * T], UN * XS / 2,
                                           mhi[:, c, :], ALU.mult, ALU.subtract).then_inc(m_lo.sem, 1)

                for c in range(KD):
                    lo_lead(O0 + c)
                    dve.wait_ge(acc_pre.sem, acc_pre.value(l, 1))
                    dve.wait_ge(blk_done.sem, blk_done.value(l, O0 + c + 1))
                    residual(l, 0, c, (O0 + c) % 4)
                ln_vector(l, 0)

                UPB = [(U0 + j) % 4 for j in range(4)]
                UE = 2 * (EXPERTS + 1)
                lo_lead(U0)
                V.memset(gate_hi, 0.0)
                V.memset(gate_lo, 0.0)
                V.memset(one_hot[:, GROUPS * 3 * CAP:], 0.0)
                dve.wait_ge(r_e.sem, r_e.value(l, 1))
                S, SB, SM, EQ, KY, O1, O2 = range(1, 8)
                V.tensor_scalar(rt[:, S], rt[:, 0], 1.0, None, ALU.add)
                dve.drain()
                V.reciprocal(rt[:, S], rt[:, S])
                dve.drain()
                V.tensor_tensor(rt[:, SB], rt[:, S], rb[:, :, :], ALU.add)
                dve.drain()
                v4 = rt[:, SB].rearrange("p i (g q) -> p (i g) q", q=PER_GROUP)
                for n, (a, b) in enumerate(((0, 1), (0, 2), (0, 3), (1, 2), (1, 3), (2, 3))):
                    V.tensor_tensor(rp[:, :, n:n + 1], v4[:, :, a:a + 1], v4[:, :, b:b + 1], ALU.add)
                dve.drain()
                lo_lead(U0 + 1)

                def g3(n):
                    return rg[:, n]

                V.tensor_reduce(g3(0).rearrange("p i g -> p (i g)"), rp[:, :, :], AXX, ALU.max)
                dve.drain()
                V.tensor_reduce(rg[:, 1, :, 0:1], g3(0), AXX, ALU.max)
                dve.drain()
                V.tensor_tensor(g3(2), g3(0), rg[:, 1, :, 0:1].broadcast_to([P, 3, GROUPS]), ALU.is_equal)
                dve.drain()
                V.tensor_tensor(g3(3), g3(2), rank4[:, :, :], ALU.mult)
                dve.drain()
                V.tensor_reduce(rg[:, 1, :, 1:2], g3(3), AXX, ALU.max)
                dve.drain()
                V.tensor_tensor(g3(4), g3(3), rg[:, 1, :, 1:2].broadcast_to([P, 3, GROUPS]), ALU.is_equal)
                dve.drain()
                V.tensor_copy(gm16[:, 0:2, :], rg[:, 4, 0:2, :])
                V.tensor_copy(gm16[P - TS:P, 2, :], rg[P - TS:P, 4, 2, :]).then_inc(gm_set.sem, 1)
                V.tensor_scalar(g3(5), g3(4), -1.0, -NEG, ALU.add, ALU.mult)
                dve.drain()
                V.tensor_tensor(rt[:, SM].rearrange("p i (g q) -> p (i g) q", q=PER_GROUP), v4,
                                g3(5).rearrange("p i g -> p (i g)").unsqueeze(2).broadcast_to(
                                    [P, 3 * GROUPS, PER_GROUP]), ALU.add)
                for n, o in enumerate((O1, O2)):
                    dve.drain()
                    V.tensor_reduce(rg[:, 6, :, n:n + 1], rt[:, SM], AXX, ALU.max)
                    dve.drain()
                    V.tensor_tensor(rt[:, EQ], rt[:, SM],
                                    rg[:, 6, :, n:n + 1].broadcast_to([P, 3, EXPERTS]), ALU.is_equal)
                    dve.drain()
                    V.tensor_tensor(rt[:, KY], rt[:, EQ], rank16[:, :, :], ALU.mult)
                    dve.drain()
                    V.tensor_reduce(rg[:, 6, :, 2 + n:3 + n], rt[:, KY], AXX, ALU.max)
                    dve.drain()
                    V.tensor_tensor(rt[:, o], rt[:, KY],
                                    rg[:, 6, :, 2 + n:3 + n].broadcast_to([P, 3, EXPERTS]), ALU.is_equal)
                    if n == 0:
                        dve.drain()
                        V.scalar_tensor_tensor(rt[:, SM], rt[:, O1], 3 * NEG, rt[:, SM], ALU.mult,
                                               ALU.add)
                dve.drain()
                V.tensor_tensor(rt[:, O1], rt[:, O1], rt[:, O2], ALU.add)
                dve.drain()
                V.tensor_tensor(rt[:, O1], rt[:, O1], rt[:, S], ALU.mult)
                dve.drain()
                V.tensor_reduce(rg[:, 7, :, 0:1], rt[:, O1], AXX, ALU.add)
                dve.drain()
                V.reciprocal(rg[:, 7, :, 1:2], rg[:, 7, :, 0:1])
                dve.drain()
                V.tensor_tensor(rt[:, O2], rt[:, O1], rg[:, 7, :, 1:2].broadcast_to([P, 3, EXPERTS]),
                                ALU.mult).then_inc(g_sel.sem, 1)

                dve.wait_ge(pos_ps.sem, pos_ps.value(l, 1))
                V.tensor_tensor(place[:, :, :], bank[7][:, 64:64 + 3 * GROUPS].rearrange(
                    "p (i g) -> p i g", i=3), gm16[:, :, :], ALU.mult)
                V.tensor_reduce(most[:, :], bank[7][:, 80:80 + GROUPS], AXX, ALU.max)
                dve.drain()
                for g in range(GROUPS):
                    a = V.tensor_tensor(
                        one_hot[:, g * 3 * CAP:(g + 1) * 3 * CAP].rearrange("p (i n) -> p i n", i=3),
                        slot_no[:, :].unsqueeze(1).broadcast_to([P, 3, CAP]),
                        place[:, :, g:g + 1].broadcast_to([P, 3, CAP]), ALU.is_equal)
                a.then_inc(oh_set.sem, 1)
                V.tensor_copy(most_i[:, :], most[:, :]).then_inc(most_set.sem, 1)

                def hidden(n, ready1, f, W, c0, gate):
                    dve.wait_ge(u_tanh.sem, u_tanh.value(l, n + 1))
                    V.scalar_tensor_tensor(h1[:, 0:W], ht[:, 0:W], 1.0, bank[UPB[2 * f]][:, 0:W], ALU.add,
                                           ALU.mult)
                    dve.drain()
                    dve.wait_ge(blk_done.sem, blk_done.value(l, ready1))
                    V.tensor_tensor(h1[:, 0:W], h1[:, 0:W], bank[UPB[2 * f + 1]][:, 0:W], ALU.mult
                                    ).then_inc(u_free.sem, 1)
                    dve.drain()
                    if gate is not None:
                        dve.wait_ge(gb_ps.sem, gb_ps.value(l, gate))
                        V.tensor_tensor(h2[:, 0:W], h1[:, 0:W], bank[4][:, 0:W], ALU.mult
                                        ).then_inc(u_prod.sem, 1)
                    else:
                        V.tensor_copy(h2[:, 0:W], h1[:, 0:W]).then_inc(u_prod.sem, 1)
                    dve.wait_ge(u_hi.sem, u_hi.value(l, n + 1))
                    scale = UN * UN * XS / (2 if gate is None else 2 * GS)
                    V.scalar_tensor_tensor(hlo[:, bass.ds(c0, W)], h2[:, 0:W], scale,
                                           hhi[:, bass.ds(c0, W)], ALU.mult, ALU.subtract
                                           ).then_inc(u_lo.sem, 1)

                dve.wait_ge(gt_h.sem, gt_h.value(l, 1))
                V.scalar_tensor_tensor(gt_lo[:, :, :], rt[:, 7], GS, gt_hi[:, :, :], ALU.mult,
                                       ALU.subtract).then_inc(gt_l.sem, 1)
                for f in range(2):
                    if f:
                        dve.wait_ge(most_set.sem, most_set.value(l, 1))
                        lo_lead(U0 + 2)
                        lo_lead(U0 + 3)
                    hidden(f, U0 + (2 * f + 2), f, T, f * T, None)

                def expert_lo(e, W):
                    g0 = e * 4 + (U0 + 4)
                    for f in range(2):
                        lo_at(l, g0 + (2 * f + LEAD), (U0 + 2 * f + LEAD) % SLOTS)
                        lo_at(l, g0 + (2 * f + 1 + LEAD), (U0 + 2 * f + 1 + LEAD) % SLOTS)
                        hidden(e * 2 + (2 + f), g0 + (2 * f + 2), f, W, (e * 2 + f) * W + H0, e + 1)

                def half_out(hf):
                    dve.wait_ge(acc_pre.sem, acc_pre.value(l, 2))
                    dve.wait_ge(sums.sem, sums.value(l, hf + 1))
                    for c in range(4):
                        residual(l, 1, 4 * hf + c, ((0, 1, 2, 3), (4, 5, 0, 1))[hf][c])

                fits = dve.value_load(most_i[0:1, 0:1]) < CAP + 1
                with dve.If(fits):
                    dve.wait_ge(g_hi.sem, g_hi.value(l, 1))
                    V.tensor_tensor(gate_lo[0:EXPERTS, :], bank[7][0:EXPERTS, :], gate_hi[0:EXPERTS, :],
                                    ALU.subtract).then_inc(g_lo.sem, 1)
                    with dve.Fori(0, EXPERTS) as e:
                        expert_lo(e, CAP)

                    def group_out(g, g2, hf):
                        dve.wait_ge(yg_hi.sem, yg_hi.value(l, g + (4 * hf + 1)))
                        V.scalar_tensor_tensor(y_lo[:, bass.ds(g * 512, 512)],
                                               bank[(4, 2)[hf] + g2][:, :], UN * XS,
                                               y_hi[:, bass.ds(g * 512, 512)], ALU.mult, ALU.subtract
                                               ).then_inc(yg_lo.sem, 1)

                    lo_lead(D0)
                    with dve.Fori(0, GROUPS // 2) as gg:
                        for g2 in range(2):
                            for j in range(4):
                                n = D0 + 1 + 4 * g2 + j + LEAD
                                lo_at(l, gg * 8 + n, n % SLOTS)
                            group_out(gg * 2 + g2, g2, 0)
                    lo_lead(D1)
                    half_out(0)
                    for g in range(GROUPS):
                        for j in range(4):
                            lo_lead(D1 + 1 + 4 * g + j)
                        group_out(g, g % 2, 1)
                    half_out(1)
                with dve.Else():
                    dve.sem_inc(yg_lo.sem, 2 * GROUPS)
                    dve.wait_ge(g_hi.sem, g_hi.value(l, 1))
                    V.tensor_tensor(gate_lo[0:EXPERTS, 0:T], gate32[:, :], gate_hi[0:EXPERTS, 0:T],
                                    ALU.subtract).then_inc(g_lo.sem, 1)
                    with dve.Fori(0, EXPERTS) as e:
                        expert_lo(e, T)
                    lo_lead(D0)
                    with dve.Fori(0, 4) as i:
                        for j in range(4):
                            lo_at(l, i * 4 + (D0 + 1 + j + LEAD), (D0 + 1 + j + LEAD) % SLOTS)
                    lo_lead(D1)
                    dve.wait_ge(blk_done.sem, blk_done.value(l, D1))
                    half_out(0)
                    with dve.Fori(0, 3) as i:
                        for j in range(4):
                            lo_at(l, i * 4 + (D1 + 1 + j + LEAD), (D1 + 1 + j + LEAD) % SLOTS)
                    for j in range(4):
                        lo_lead(D1 + 13 + j)
                    dve.wait_ge(blk_done.sem, blk_done.value(l, NB))
                    half_out(1)
                ln_vector(l, 1)

        @block.tensor
        def _(pe):
            M = nc.tensor.matmul
            TR = nc.tensor.transpose

            def group(out, subs, s, rhs):
                n = 0
                for k, sub in enumerate(subs):
                    for w, part in ((whi, 0), (whi, 1), (wlo, 0)):
                        ins = M(out, w[:, s, sub * P:(sub + 1) * P], rhs(part, k), start=(n == 0),
                                stop=(n == 3 * len(subs) - 1))
                        n += 1
                return ins

            def x_rhs(part, k):
                return (xlo if part else xhi)[:, k, :]

            def ready(l, n):
                pe.wait_ge(lo_done.sem, lo_done.value(l, n + 1))

            def z_block(l, n, s, b):
                ready(l, n)
                group(bank[b][:, 0:T], range(8), s, x_rhs).then_inc(blk_done.sem, 1)

            def tok_block(l, n, s, b):
                ready(l, n)
                for i, (t0, m) in enumerate(TILES):
                    j = 0
                    for k in range(KD):
                        for x, w in ((xhi, whi), (xhi, wlo), (xlo, whi)):
                            ins = M(bank[b][0:m, i * P:(i + 1) * P], x[:, k, t0:t0 + m],
                                    w[:, s, k * P:(k + 1) * P], start=(j == 0), stop=(j == 3 * KD - 1))
                            j += 1
                ins.then_inc(blk_done.sem, 1)

            def stats(l, k, c):
                pe.wait_ge(y_sq.sem, y_sq.value(l, KD * k + c + 1))
                M(bank[4 + 2 * k][:, 0:T], ones_dm[:, :], acc[:, c * T:(c + 1) * T], start=(c == 0),
                  stop=(c == KD - 1))
                M(bank[5 + 2 * k][:, 0:T], ones_dm[:, :], ysq[:, c % 4, :], start=(c == 0),
                  stop=(c == KD - 1)).then_inc(ln_ps.sem, 1)

            pe.wait_ge(consts_in.sem, 16 * N_CONST)
            pe.wait_ge(consts_set.sem, N_SET)
            with pe.Fori(0, L) as l:
                def z_wait(n):
                    pe.wait_ge(z_ev.sem, z_ev.value(l, n))

                pe.wait_ge(x_split.sem, x_split.value(l, 0))
                for g in range(6):
                    if g >= 4:
                        z_wait(g - 3)
                    z_block(l, g, g % SLOTS, g % 4)
                for i in range(4):
                    g = 6 + i
                    if g - 4 < 6:
                        z_wait(g - 3)
                    tok_block(l, g, g % SLOTS, g % 4)
                    if i == 0:
                        for k in range(2):
                            pe.wait_ge(sq_c.sem, sq_c.value(l, k + 1))
                            for c in range(2):
                                a = M(bank[4 + k][:, 0:T], ones_dm[:, :], ysq[:, 2 * k + c, :],
                                      start=(c == 0), stop=(c == 1))
                            a.then_inc(rms_ps.sem, 1)
                pe.wait_ge(r_exp.sem, r_exp.value(l, 1))
                pe.wait_ge(rms_std.sem, rms_std.value(l, 2))
                for n in range(3 * MH):
                    h, j = n // 3, n % 3
                    if n >= 4:
                        hh, jj = (n - 4) // 3, (n - 4) % 3
                        if jj == 0:
                            pe.wait_ge(bc_m.sem, bc_m.value(l, hh + 1))
                        else:
                            pe.wait_ge(bc_ie.sem, bc_ie.value(l, 2 * hh + jj))
                    if n == 3:
                        pe.wait_ge(cols_sb.sem, cols_sb.value(l, 1))
                    M(bank[4 + n % 4][:, 0:T], head_sel[:, h, :], r_x[:, j, :], start=True, stop=True
                      ).then_inc(bc_ps.sem, 1)
                    if n == 0:
                        for j, src in enumerate((r_a, r_x[:, 3, :])):
                            for i, (t0, m) in enumerate(TILES):
                                c0 = (3 * j + i) * MH
                                a = TR(bank[7][0:m, c0:c0 + MH], src[:, t0:t0 + m], ident[0:MH, 0:MH])
                        a.then_inc(cols_ps.sem, 1)

                with pe.Fori(0, MH) as h:
                    g0 = h * MPER + M0

                    def zb(step, freed_z, freed_v=None):
                        pe.wait_ge(z_ev.sem, z_ev.value(l, h * 7 + freed_z))
                        if freed_v is not None:
                            pe.wait_ge(tokv.sem, tokv.value(l, freed_v))
                        return (l, g0 + step, (M0 + step) % SLOTS, (M0 + step) % 4)

                    z_block(*zb(0, 3, 1))
                    z_block(*zb(1, 4, 2))
                    tok_block(*zb(2, 5, 3))
                    pe.wait_ge(z_ev.sem, z_ev.value(l, h * 7 + 8))
                    pe.wait_ge(h_done.sem, h_done.value(l, h))
                    pe.wait_ge(bc_ie.sem, bc_ie.value(l, 2 * MH))
                    pe.wait_ge(bc_m.sem, bc_m.value(l, MH))
                    for i, (t0, n) in enumerate(TILES):
                        a = TR(bank[4][0:n, i * P:(i + 1) * P], mk[:, t0:t0 + n], ident[:, :])
                    a.then_inc(k_tr.sem, 1)
                    for i, (t0, n) in enumerate(TILES):
                        a = M(bank[5][0:n, i * P:i * P + n], mk[:, t0:t0 + n], mq[:, t0:t0 + n],
                              start=True, stop=True)
                    a.then_inc(a_ps.sem, 1)
                    z_block(*zb(3, 6, 4))
                    pe.wait_ge(k_sb.sem, k_sb.value(l, h + 1))
                    pe.wait_ge(v_wsd.sem, v_wsd.value(l, h + 1))
                    pe.wait_ge(g_done.sem, g_done.value(l, h))
                    for c in range(NCH):
                        r0, b, o = CH * (c % 2), bank[6 + c % 2], (c // 2) * (DH + 1)
                        a = M(b[:, o:o + DH + 1], k_tok[r0:r0 + CH, c // 2, :],
                              v_ws[r0:r0 + CH, c // 2, :], start=True, stop=True)
                    a.then_inc(dc_ps.sem, 1)
                    z_block(*zb(4, 7))
                    z_block(*zb(5, 8))
                    pe.wait_ge(att_done.sem, att_done.value(l, h + 1))
                    pe.wait_ge(st_done.sem, st_done.value(l, h + 1))
                    for num, b in ((True, bank[4]), (False, bank[5])):
                        for i, (t0, n) in enumerate(TILES):
                            M(b[:, t0:t0 + n], v_tok[0:n, i, :] if num else ones[0:n, :],
                              att[0:n, i, 0:n], start=True, stop=False)
                            for j, (c, st) in enumerate(((1, 0), (2, 1), (3, 2), (4, 4))):
                                if t0 <= c * CH < t0 + n:
                                    last = (c + 1) * CH == t0 + n
                                    a = M(b[:, c * CH:(c + 1) * CH],
                                          c_st[:, st, 0:DH] if num else n_bc[:, j, :],
                                          q_in[:, c * CH:(c + 1) * CH], start=False, stop=last)
                    a.then_inc(num_ps.sem, 1)
                    z_block(*zb(6, 8, 5 + h))
                    pe.wait_ge(vg_done.sem, vg_done.value(l, h + 1))
                    pe.wait_ge(ws_masked.sem, ws_masked.value(l, 1))
                    for i, (t0, n) in enumerate(TILES):
                        off = h * P
                        M(bank[6][:, t0:t0 + n], vg[0:n, i, :], ws_t[0:n, bass.ds(off, n)], start=True,
                          stop=False)
                        a = M(bank[6][:, t0:t0 + n], ones[0:1, :], bs_row[:, bass.ds(off, n)],
                              start=False, stop=True)
                    a.then_inc(sp_ps.sem, 1)
                    z_block(*zb(7, 9))

                with pe.Fori(0, 2) as hf:
                    g0 = hf * APER + A0
                    s0, s1 = A0 % SLOTS, (A0 + 1) % SLOTS
                    ready(l, g0)
                    pe.wait_ge(c_lo.sem, c_lo.value(l, 3))
                    pe.wait_ge(g_done.sem, g_done.value(l, MH))
                    pe.wait_ge(h_done.sem, h_done.value(l, MH))
                    pe.wait_ge(o_lo.sem, o_lo.value(l, hf * 2))
                    for j in range(4):
                        a = group(bank[4 + j][:, 0:T], (2 * j, 2 * j + 1), s0,
                                  lambda part, k: (cq_lo if part else cq_hi)[:, k, :])
                    a.then_inc(blk_done.sem, 1)
                    ready(l, g0 + 1)
                    pe.wait_ge(z_ev.sem, z_ev.value(l, hf * 10 + 34))
                    pe.wait_ge(t_sb.sem, t_sb.value(l, hf * 6))
                    for j in range(4):
                        k0 = (j % 2) * KH
                        group(bank[j][:, 0:KH], (2 * (j // 2), 2 * (j // 2) + 1), s1,
                              lambda part, k: (kv_lo if part else kv_hi)[:, k, k0:k0 + KH])
                    pe.wait_ge(q_ev.sem, q_ev.value(l, hf + 1))
                    pe.wait_ge(q_rot.sem, q_rot.value(l, hf + 1))
                    for i in range(5):
                        n = P if i < 4 else TS
                        j = 0
                        for k in range(2):
                            for x, w in ((kv_hi, whi), (kv_hi, wlo), (kv_lo, whi)):
                                a = M(bank[4 + i // 2][0:n, (i % 2) * 2 * P:(i % 2 + 1) * 2 * P],
                                      x[:, k, i * P:i * P + n],
                                      w[:, s1, (4 + 2 * k) * P:(6 + 2 * k) * P], start=(j == 0),
                                      stop=(j == 5))
                                j += 1
                    a.then_inc(blk_done.sem, 1)

                    def scores(j):
                        p, r = j // 3, j % 3
                        b = bank[4 + j % 2]
                        if j < 2:
                            pe.wait_ge(v_ev.sem, v_ev.value(l, hf + 1))
                        if j >= 2:
                            pe.wait_ge(p_exp.sem, p_exp.value(l, hf * 6 + (j - 1)))
                        if j == 0:
                            pe.wait_ge(kr_done.sem, kr_done.value(l, 1))
                            pe.wait_ge(z_ev.sem, z_ev.value(l, hf * 10 + 38))
                        if r < 2:
                            hh = 2 * p + r
                            for q in range(2):
                                a = M(b[:, P * q:P * q + P * (q + 1)],
                                      q_att[0:KATT, hh, P * q:P * (q + 1)],
                                      k_att[0:KATT, hh, PAST:PAST + P * (q + 1)], start=True, stop=True)
                        else:
                            for r_ in range(2):
                                hh = 2 * p + r_
                                for o, k0, n in ((0, 0, PAST), (PAST, PAST + TP, TS)):
                                    a = M(b[TS * r_:TS * (r_ + 1), o:o + n], q_att[0:KATT, hh, TP:T],
                                          k_att[0:KATT, hh, k0:k0 + n], start=True, stop=True)
                        a.then_inc(s_ps.sem, 1)

                    def transposes(j):
                        pe.wait_ge(p_norm.sem, p_norm.value(l, hf * 6 + (j + 1)))
                        if j:
                            pe.wait_ge(t_sb.sem, t_sb.value(l, hf * 6 + j))
                        for i in range(3):
                            n = P if j % 3 < 2 or i < 2 else TS
                            a = TR(bank[6][0:n, i * P:(i + 1) * P], prob[:, j % 2, i * P:i * P + n],
                                   ident[:, :])
                        a.then_inc(t_ps.sem, 1)

                    def values(j):
                        p, r = j // 3, j % 3
                        pe.wait_ge(t_sb.sem, t_sb.value(l, hf * 6 + (j + 1)))
                        if j == 3:
                            pe.wait_ge(o_lo.sem, o_lo.value(l, hf * 2 + 1))
                        for r_ in ((r,) if r < 2 else (0, 1)):
                            vc = slice((2 * p + r_) * VD, (2 * p + r_ + 1) * VD)
                            o = bank[7][VD * r_:VD * (r_ + 1), :]
                            if r < 2:
                                M(o[:, 0:P], v_kv[:, 2, vc], prob_t[:, j % 2, 0, :], start=True,
                                  stop=True)
                                M(o[:, P:2 * P], v_kv[:, 2, vc], prob_t[:, j % 2, 1, :], start=True,
                                  stop=False)
                                a = M(o[:, P:2 * P], v_kv[:, 3, vc], prob_t[:, j % 2, 2, :],
                                      start=False, stop=True)
                            else:
                                qs = slice(TS * r_, TS * (r_ + 1))
                                for n, (kt, rows_) in enumerate(((0, P), (1, P), (4, TS))):
                                    a = M(o[:, TP:T], v_kv[0:rows_, kt, vc],
                                          prob_t[0:rows_, j % 2, n, qs], start=(n == 0), stop=(n == 2))
                        a.then_inc(o_ps.sem, 1)

                    for j in range(6):
                        scores(j)
                        if j:
                            transposes(j - 1)
                        if j >= 2:
                            values(j - 2)
                        pe.wait_ge(z_ev.sem, z_ev.value(l, hf * 10 + (35 + j)))
                        z_block(l, g0 + (2 + j), (A0 + 2 + j) % SLOTS, (A0 + 2 + j) % 4)
                    transposes(5)
                    values(4)
                    values(5)

                with pe.Fori(0, 3) as k:
                    pe.wait_ge(z_ev.sem, z_ev.value(l, 54))
                    pe.wait_ge(bc_lo.sem, bc_lo.value(l, 2 * MH))
                    pe.wait_ge(o_lo.sem, o_lo.value(l, 4))
                    for j in range(4):
                        ready(l, k * 4 + (B0 + j))
                        for i in range(2):
                            c = 2 * j + i
                            pe.wait_ge(m_used.sem, m_used.value(l, k * 8 + max(0, c - 3)))
                            a = group(bank[c % 4][:, 0:T], range(4 * i, 4 * i + 4), (B0 + j) % SLOTS,
                                      lambda part, kt: (br_lo if part else br_hi)[
                                          :, bass.ds((k * 4 + kt) * T, T)])
                        a.then_inc(blk_done.sem, 1)

                for c in range(KD):
                    ready(l, O0 + c)
                    if c == 0:
                        pe.wait_ge(m_lo.sem, m_lo.value(l, KD))
                    if c >= 4:
                        pe.wait_ge(y_done.sem, y_done.value(l, c - 3))
                    group(bank[(O0 + c) % 4][:, 0:T], range(8), (O0 + c) % SLOTS,
                          lambda part, k: (mlo if part else mhi)[:, k, :]).then_inc(blk_done.sem, 1)
                    if c >= 2:
                        stats(l, 0, c - 2)
                stats(l, 0, KD - 2)
                stats(l, 0, KD - 1)

                UPB = [(U0 + j) % 4 for j in range(4)]
                EYE, LE, ONE = (mats16[:, n, :] for n in range(3))
                pe.wait_ge(x_split.sem, x_split.value(l, KD))
                for i in range(3):
                    t0 = min(i * P, T - P)
                    for k in range(KD):
                        a = M(bank[7][:, i * EXPERTS:(i + 1) * EXPERTS], xT[:, k * T + t0:k * T + t0 + P],
                              rw[:, k, :], start=(k == 0), stop=(k == KD - 1))
                a.then_inc(r_ps.sem, 1)
                for j in range(4):
                    z_block(l, U0 + j, (U0 + j) % SLOTS, UPB[j])
                    if j == 0:
                        pe.wait_ge(gm_set.sem, gm_set.value(l, 1))
                        for i in range(4):
                            for k in range(min(i, 2) + 1):
                                o = 64 + 4 * i if i < 3 else 80
                                a = M(bank[7][:, o:o + GROUPS], LE if k == i else ONE, gm16[:, k, :],
                                      start=(k == 0), stop=(k == min(i, 2)))
                        a.then_inc(pos_ps.sem, 1)
                    if j == 3:
                        pe.wait_ge(most_set.sem, most_set.value(l, 1))
                    for n in range(3 * j, 3 * j + 3):
                        part, half, t0 = n // 6, n // 3 % 2, min(n % 3 * P, T - P)
                        if n >= 3:
                            pe.wait_ge(xt_ev.sem, xt_ev.value(l, n - 2))
                        for c in range(4):
                            a = M(bank[4 + n % 3][:, c * P:(c + 1) * P],
                                  (xlo if part else xhi)[:, 4 * half + c, t0:t0 + P], EYE, start=True,
                                  stop=True)
                        a.then_inc(xt_ps.sem, 1)

                def expert(e, W, gate0, rhs, between=None):
                    g0 = e * 4 + (U0 + 4)
                    for j in range(4):
                        if j % 2 == 0:
                            pe.wait_ge(u_free.sem, u_free.value(l, e * 2 + (1 + j // 2)))
                        ready(l, g0 + j)
                        group(bank[UPB[j]][:, 0:W], range(8), (U0 + j) % SLOTS, rhs
                              ).then_inc(blk_done.sem, 1)
                        if j == 0:
                            pe.wait_ge(g_lo.sem, g_lo.value(l, 1))
                            pe.wait_ge(u_prod.sem, u_prod.value(l, e * 2 + 2))
                            M(bank[4][:, 0:W], exp_sel[:, bass.ds(e * P, P)], gate_hi[:, bass.ds(gate0, W)],
                              start=True, stop=False)
                            M(bank[4][:, 0:W], exp_sel[:, bass.ds(e * P, P)], gate_lo[:, bass.ds(gate0, W)],
                              start=False, stop=True).then_inc(gb_ps.sem, 1)
                        if j == 1 and between:
                            between()

                half0, half1 = (0, 1, 2, 3), (4, 5, 0, 1)

                def down(l, n, s, banks, expert, first, last):
                    ready(l, n)
                    for kt in range(2):
                        for i, b in enumerate(banks):
                            for w, h_ in ((whi, hhi), (whi, hlo), (wlo, hhi)):
                                a = M(bank[b][:, 0:T], w[:, s, (4 * kt + i) * P:(4 * kt + i + 1) * P],
                                      h_[:, bass.ds((expert * 2 + kt) * T, T)],
                                      start=(first and kt == 0 and w is whi and h_ is hhi),
                                      stop=(last and kt == 1 and w is wlo))
                    a.then_inc(blk_done.sem, 1)

                def gather(b, g, q):
                    for c in range(4):
                        for i in range(3):
                            a = M(bank[b][:, c * P:(c + 1) * P],
                                  x_tok[:, bass.ds(q * 1536 + (i * 512 + c * P), P)],
                                  one_hot[:, bass.ds(g * (3 * CAP) + i * CAP, CAP)], start=(i == 0),
                                  stop=(i == 2))
                    a.then_inc(xg_ps.sem, 1)

                fits = pe.value_load(most_i[0:1, 0:1]) < CAP + 1
                with pe.If(fits):
                    pe.wait_ge(xt_ev.sem, xt_ev.value(l, 12))
                    pe.wait_ge(oh_set.sem, oh_set.value(l, 1))
                    for q in range(4):
                        if q >= 2:
                            pe.wait_ge(xg_ev.sem, xg_ev.value(l, q - 1))
                        gather(5 + q % 2, 0, q)
                    pe.wait_ge(gt_l.sem, gt_l.value(l, 1))
                    slots = one_hot[:, 0:GROUPS * 3 * CAP].rearrange("p (g i n) -> p g i n", g=GROUPS, i=3)
                    for i in range(3):
                        for part in (gt_hi, gt_lo):
                            a = M(bank[7][0:EXPERTS, :], part[:, i, :], slots[:, :, i, :],
                                  start=(i == 0 and part is gt_hi), stop=(i == 2 and part is gt_lo))
                    a.then_inc(g_tr.sem, 1)
                    with pe.Fori(0, GROUPS // 2) as gg:
                        for g2 in range(2):
                            g = gg * 2 + g2
                            pe.wait_ge(g_lo.sem, g_lo.value(l, 1))
                            pe.wait_ge(ot_ev.sem, ot_ev.value(l, g))
                            pe.wait_ge(xg_ev.sem, xg_ev.value(l, gg * 8 + (4 * g2 + 4)))
                            for i in range(3):
                                t0, n = TILES[i]
                                a = M(bank[7][:, t0:t0 + n],
                                      one_hot[:, bass.ds(g * (3 * CAP) + i * CAP, CAP)],
                                      mats16[:, 0, P - n:P], start=True, stop=True)
                            a.then_inc(ot_ps.sem, 1)
                            with pe.Fori(0, 4) as q:
                                def between():
                                    pe.wait_ge(xg_ev.sem, xg_ev.value(l, gg * 8 + q + (4 * g2 + 4)))
                                    gather(5, g + 1, q)

                                expert(gg * 8 + q + 4 * g2, CAP, g * CAP,
                                       lambda part, k: x_grp[:, g2, part, k, :], between)

                    def group_down(g, g2, hf):
                        b = bank[(4, 2)[hf] + g2]
                        pe.wait_ge(yg_lo.sem, yg_lo.value(l, g + (4 * hf - 1)))
                        for q in range(4):
                            n = (D0, D1)[hf] + 1 + q
                            ready(l, g * 4 + n)
                            for kt in range(2):
                                for w, h_ in ((whi, hhi), (wlo, hhi), (whi, hlo)):
                                    a = M(b[:, :], h_[:, bass.ds(g * (8 * CAP) + ((2 * q + kt) * CAP + H0),
                                                                 CAP)],
                                          w[:, n % SLOTS, kt * 512:(kt + 1) * 512],
                                          start=(q == 0 and kt == 0 and w is whi and h_ is hhi),
                                          stop=(q == 3 and kt == 1 and h_ is hlo))
                            a.then_inc(blk_done.sem, 1)

                    def scatter(hf, banks):
                        for g in range(GROUPS):
                            pe.wait_ge(yg_lo.sem, yg_lo.value(l, 4 * hf + g + 1))
                            for i, b in enumerate(banks):
                                for y in (y_hi, y_lo):
                                    a = M(bank[b][:, 0:T], y[:, g * 512 + i * P:g * 512 + (i + 1) * P],
                                          slot_tok[:, g * T:(g + 1) * T], start=False,
                                          stop=(g == GROUPS - 1 and y is y_lo))
                        a.then_inc(sums.sem, 1)

                    pe.wait_ge(u_lo.sem, u_lo.value(l, 2 * (EXPERTS + 1)))
                    pe.wait_ge(ot_ev.sem, ot_ev.value(l, GROUPS))
                    pe.wait_ge(xg_ev.sem, xg_ev.value(l, 20))
                    down(l, D0, D0 % SLOTS, half0, 0, True, False)
                    with pe.Fori(0, GROUPS // 2) as gg:
                        for g2 in range(2):
                            group_down(gg * 2 + g2, g2, 0)
                    scatter(0, half0)
                    pe.wait_ge(y_done.sem, y_done.value(l, KD + 4))
                    down(l, D1, D1 % SLOTS, half1, 0, True, False)
                    for c in range(4):
                        stats(l, 1, c)
                    with pe.Fori(0, GROUPS // 2) as gg:
                        for g2 in range(2):
                            group_down(gg * 2 + g2, g2, 1)
                    scatter(1, half1)
                with pe.Else():
                    pe.sem_inc(xg_ps.sem, 20)
                    pe.sem_inc(ot_ps.sem, GROUPS)
                    pe.wait_ge(g_sel.sem, g_sel.value(l, 1))
                    pe.wait_ge(xt_ev.sem, xt_ev.value(l, 12))
                    for i in range(3):
                        a = TR(bank[6][0:EXPERTS, i * P:(i + 1) * P], rt[:, 7, i, :], ident[:, :])
                    a.then_inc(g_tr.sem, 1)
                    with pe.Fori(0, EXPERTS) as e:
                        expert(e, T, 0, x_rhs)
                    pe.wait_ge(u_lo.sem, u_lo.value(l, 2 * (EXPERTS + 1)))
                    down(l, D0, D0 % SLOTS, half0, 0, True, False)
                    with pe.Fori(0, 3) as i:
                        for j in range(4):
                            down(l, i * 4 + (D0 + 1 + j), (D0 + 1 + j) % SLOTS, half0, i * 4 + (1 + j),
                                 False, False)
                    for j in range(4):
                        down(l, D0 + 13 + j, (D0 + 13 + j) % SLOTS, half0, 13 + j, False, j == 3)
                    pe.sem_inc(sums.sem, 1)
                    pe.wait_ge(y_done.sem, y_done.value(l, KD + 2))
                    down(l, D1, D1 % SLOTS, half1, 0, True, False)
                    for c in range(4):
                        stats(l, 1, c)
                    with pe.Fori(0, 3) as i:
                        for j in range(4):
                            down(l, i * 4 + (D1 + 1 + j), (D1 + 1 + j) % SLOTS, half1, i * 4 + (1 + j),
                                 False, False)
                    for j in range(4):
                        down(l, D1 + 13 + j, (D1 + 13 + j) % SLOTS, half1, 13 + j, False, j == 3)
                    pe.sem_inc(sums.sem, 1)
                for c in range(4, KD):
                    stats(l, 1, c)


def _blocks(inp):
    def kt(w):
        return w.reshape(-1, P, w.shape[1]).transpose(1, 0, 2)

    out = np.zeros((L, NB, P, BLK), np.float32)
    half = ROPE // 2
    swap = np.r_[half:ROPE, 0:half]
    zin = np.cumsum([0, RANK, RANK, ROPE, 512, 512, 512, MH, MH, 512, 512, 512])
    cq, ckv, kr, q, k, v, gi, gf, go, gu, gv, gt = (int(n) for n in zin)

    def cols(i):
        gate = np.full(P, -1)
        gate[0:MH] = gi + np.arange(MH)
        gate[32:32 + MH] = gf + np.arange(MH)
        rot = np.full(P, -1)
        rot[0:ROPE] = kr + np.arange(ROPE)
        rot[ROPE:2 * ROPE] = kr + swap
        tile = lambda base, n: base + n * P + np.arange(P)
        front = [gate, tile(cq, 0), tile(cq, 1), tile(ckv, 0), tile(ckv, 1), rot]
        heads = [[tile(q, h), tile(k, h), tile(v, h), tile(go, h), tile(gu, h)] for h in range(MH)]
        return front, [tile(gv, n) for n in range(4)], heads, [tile(gt, n) for n in range(24)]

    front, gvs, heads, gts = cols(0)
    z = {n: c for n, c in enumerate(front)}
    z.update({6 + n: c for n, c in enumerate(gvs)})
    for h in range(MH):
        for n, c in enumerate(heads[h] + gts[3 * h:3 * h + 3]):
            z[M0 + MPER * h + n] = c
    for hf in range(2):
        for n in range(6):
            z[A0 + APER * hf + 2 + n] = gts[12 + 6 * hf + n]
    par = np.zeros((P, L, NPAR), np.float32)
    for l in range(L):
        w, b = inp["w_in"][l], inp["b_in"][l]

        def take(a, c):
            return np.where(c >= 0, a[..., np.maximum(c, 0)], np.float32(0))

        for n, c in z.items():
            out[l, n] = kt(take(w, c)).reshape(P, BLK)
        for n, c in enumerate(front):
            par[:, l, C_FRONT + n] = take(b, c)
        for h in range(MH):
            for n, c in enumerate((heads[h][0], heads[h][1], heads[h][3], heads[h][4])):
                par[:, l, C_MLSTM + 4 * h + n] = take(b, c)
        for n, c in enumerate(gts):
            par[:, l, C_GATE + n] = take(b, c)
        for col, name in ((C_QG, "q_norm_g"), (C_KVG, "kv_norm_g"), (C_L1G, "ln1_g"), (C_L1B, "ln1_b"),
                          (C_L2G, "ln2_g"), (C_L2B, "ln2_b")):
            a = inp[name][l].reshape(-1, P).T
            par[:, l, col:col + a.shape[1]] = a
        uq = inp["w_uq"][l].reshape(RANK, HEADS, NOPE + ROPE)
        ukv = inp["w_ukv"][l].reshape(RANK, HEADS, NOPE + VD)
        for hf in range(2):
            hs = slice(4 * hf, 4 * hf + 4)
            n = A0 + APER * hf
            tiles = [uq[:, 4 * hf:4 * hf + 2, :NOPE], uq[:, 4 * hf + 2:4 * hf + 4, :NOPE],
                     uq[:, hs, NOPE:], uq[:, hs, NOPE:][:, :, swap]]
            out[l, n] = np.concatenate([kt(t.reshape(RANK, P)).reshape(P, 2 * P) for t in tiles], 1)
            kv = [kt(ukv[:, 4 * hf + 2 * j:4 * hf + 2 * j + 2, :NOPE].reshape(RANK, P)).reshape(P, 2 * P)
                  for j in range(2)]
            kv.append(kt(ukv[:, hs, NOPE:].reshape(RANK, 2 * P)).reshape(P, 4 * P))
            out[l, n + 1] = np.concatenate(kv, 1)
        for k_ in range(3):
            w4 = inp["w_branch"][l, k_].reshape(4, P, 4, 2, P).transpose(2, 1, 3, 0, 4)
            out[l, B0 + 4 * k_:B0 + 4 * k_ + 4] = w4.reshape(4, P, BLK)
        out[l, O0:U0] = inp["w_out"][l].reshape(KD, P, KD, P).transpose(2, 1, 0, 3).reshape(KD, P, BLK)
        wg = np.concatenate([inp["shared_w_gate"][l][None], inp["moe_w_gate"][l]])
        wu = np.concatenate([inp["shared_w_up"][l][None], inp["moe_w_up"][l]])
        wd = np.concatenate([inp["shared_w_down"][l][None], inp["moe_w_down"][l]])
        up = np.stack([wg, wu], 1).reshape(EXPERTS + 1, 2, KD, P, 2, P)
        out[l, U0:D0] = up.transpose(0, 4, 1, 3, 2, 5).reshape(-1, P, BLK)
        dn = wd.reshape(EXPERTS + 1, 2, P, 2, 4, P).transpose(3, 0, 2, 1, 4, 5)
        out[l, D0:NB] = dn.reshape(-1, P, BLK)
    rows = np.stack([inp["b_in"][:, gv:gv + 512], inp["b_in"][:, v:v + 512],
                     inp["gmlp_ln_g"], inp["gmlp_ln_b"]], 1)
    return out.reshape(L * NB * P, BLK), par.reshape(P, L * NPAR), rows.reshape(L, 4 * GW)


def _constants():
    half = ROPE // 2
    pos = np.r_[0:TP, PAST:PAST + TS].astype(np.float32)
    inv = (np.float32(10000.0) ** (-np.arange(half, dtype=np.float32) / half)).astype(np.float32)
    ang = pos[None, :] * inv[:, None]
    cos, sin = np.cos(ang), np.sin(ang)
    s, t = np.arange(P)[:, None], np.arange(T)[None, :]
    tt = t % P
    mmask = np.where((s <= tt) & (s // CH == tt // CH), 0, NEG)
    keep = np.broadcast_to(np.arange(T) % CH != 0, (MH, T))
    att = np.zeros((2, T + KEYS))
    for n in range(2):
        att[n, n * P:n * P + CH] = 1
        att[n, T + PAST + n * P + CH:T + PAST + (n + 1) * P] = NEG
    sel = np.zeros((P, EXPERTS, P), np.float16)
    sel[np.arange(EXPERTS), np.arange(EXPERTS)] = 1
    c = dict(
        cos=np.tile(np.concatenate([cos, cos]), (4, 1)), sin=np.tile(np.concatenate([-sin, sin]), (4, 1)),
        ident=np.eye(P), mmask=mmask, scan_keep=keep,
        att_mask=att,
        head_sel=np.broadcast_to(np.eye(MH)[:, :, None], (MH, MH, P)),
        rank4=np.broadcast_to(np.arange(GROUPS, 0, -1), (P, 3, GROUPS)),
        rank16=np.broadcast_to(np.arange(EXPERTS, 0, -1), (P, 3, EXPERTS)))
    c["slot_no"] = np.broadcast_to(np.arange(1, CAP + 1), (P, CAP))
    c = {n: np.ascontiguousarray(a, dtype=np.float32) for n, a in c.items()}
    c["mats16"] = np.stack([np.eye(P), np.triu(np.ones((P, P))), np.ones((P, P))], 1).astype(np.float16)
    c["exp_sel"] = sel.reshape(P, EXPERTS * P)
    return c


_OUTS = dict(y=(P, KD * T), ckv=(L * P, 2 * T), kr_out=(L * ROPE, T), m_out=(L * MH, 8),
             gv_out=(L * TS, GW), c_prompt=(L * MH * P, DH + 1), c_sample=(L * MH * P, DH + 1))


def kernel(**inputs):
    import concourse.bacc as bacc
    from concourse.bass_utils import run_bass_kernel_spmd

    inp = {k: np.asarray(v) for k, v in inputs.items()}
    w, par, rows = _blocks(inp)
    x = np.concatenate([inp["x_prompt"][0], inp["x_sample"][0]])
    c0 = np.concatenate([inp["state_mlstm_c"][:, 0].transpose(0, 1, 3, 2),
                         inp["state_mlstm_n"][:, 0][..., None]], -1)
    arrays = dict(
        x=x.T.reshape(KD, P, T).transpose(1, 0, 2).reshape(P, KD * T), w=w, par=par, rows=rows,
        rb=np.tile(inp["router_b"], 3), rw=inp["router_w"].reshape(KD, P, EXPERTS).transpose(1, 0, 2),
        m_init=inp["state_mlstm_m"][:, 0].T, c_init=c0.transpose(0, 2, 1, 3).reshape(L * P, -1),
        cache=inp["cache_mla_ckv"][:, 0].reshape(L, PAST, 2, P).transpose(0, 3, 2, 1).reshape(L * P, -1),
        krope=inp["cache_mla_krope"][:, 0].transpose(0, 2, 1).reshape(L * ROPE, PAST),
        ws_t=inp["gmlp_ws"].transpose(0, 3, 1, 2).reshape(L * P, -1),
        bs_row=inp["gmlp_bs"].reshape(L, -1), **_constants())
    arrays = {n: np.ascontiguousarray(a) for n, a in arrays.items()}
    nc = bacc.Bacc("TRN2", target_bir_lowering=False, num_devices=1)
    d = {n: nc.dram_tensor(f"in_{n}", a.shape, mybir.dt.from_np(a.dtype), kind="ExternalInput").ap()
         for n, a in arrays.items()}
    d.update({n: nc.dram_tensor(f"out_{n}", s, F32, kind="ExternalOutput").ap() for n, s in _OUTS.items()})
    build_trunk(nc, d)
    r = run_bass_kernel_spmd(nc, [{f"in_{n}": a for n, a in arrays.items()}], core_ids=[0]).results[0]
    o = {n: np.asarray(r[f"out_{n}"]) for n in _OUTS}

    y = o["y"].reshape(P, KD, T).transpose(2, 1, 0).reshape(T, DM)
    ckv = o["ckv"].reshape(L, P, 2, T).transpose(0, 3, 2, 1).reshape(L, 1, T, RANK)
    kr = o["kr_out"].reshape(L, ROPE, T).transpose(0, 2, 1).reshape(L, 1, T, ROPE)
    m = o["m_out"].reshape(L, 1, MH, 8)
    cp, cs = (o[n].reshape(L, 1, MH, DH, DH + 1) for n in ("c_prompt", "c_sample"))
    c = np.ascontiguousarray
    return (c(y[None, :TP]), c(y[None, TP:]), c(ckv[:, :, :TP]), c(kr[:, :, :TP]),
            c(cp[..., :DH].swapaxes(3, 4)), c(cp[..., DH]), c(m[..., 4]),
            c(ckv[:, :, TP:]), c(kr[:, :, TP:]), c(cs[..., :DH].swapaxes(3, 4)), c(cs[..., DH]),
            c(m[..., 6]), c(o["gv_out"].reshape(L, 1, TS, GW)))
```

```python
from contextlib import ExitStack

import concourse.bass as bass
import numpy as np
from concourse import mybir

F32, F16 = mybir.dt.float32, mybir.dt.float16
ALU = mybir.AluOpType
ACT = mybir.ActivationFunctionType
AXX = mybir.AxisListType.X

P = 128
DM, L = 1024, 2
TP, TS, PAST = 256, 64, 256
T = TP + TS
KD = DM // P
HEADS, NOPE, ROPE, VD, RANK = 8, 64, 32, 64, 256
MH, DH, CH = 4, 128, 64
NCH = T // CH
GW = 512
EXPERTS, GROUPS, PER_GROUP, DE = 16, 4, 4, 256
ALPHA = (2 * L) ** 0.25
EPS = 1e-5
ATT_SCALE = (NOPE + ROPE) ** -0.5
KSCALE = DH ** -0.5
NEG = -1e30
MROW = NOPE + ROPE
KATT = MROW + 2
KEYS = PAST + T
KH = KEYS // 2

WS = 64.0
XS = 4.0
UN = 1.0 / (WS * XS)
GS = 1024.0

CAP = P
H0 = 2 * T

SLOTS = 4
LEAD = 3
BLK = 8 * P
FRONT = 10
M0, MPER = FRONT, 8
A0, APER = M0 + MH * MPER, 8
B0 = A0 + 2 * APER
O0 = B0 + 12
U0 = O0 + KD
D0 = U0 + 4 * (EXPERTS + 1)
D1 = D0 + EXPERTS + 1
NB = D1 + EXPERTS + 1
assert NB % SLOTS == 0 and MPER % SLOTS == 0 and APER % SLOTS == 0

C_FRONT, C_MLSTM, C_GATE = 0, 6, 22
C_QG, C_KVG, C_L1G, C_L1B, C_L2G, C_L2B, NPAR = 46, 48, 50, 58, 66, 74, 82

TILES = [(0, P), (P, P), (2 * P, TS)]


class Signal:

    def __init__(self, ctx, nc, name, per, before=0):
        self.sem, self.per, self.before = ctx.enter_context(nc.semaphore(name)), per, before

    def value(self, layer, n):
        return layer * self.per + (n + self.before)


def build_trunk(nc, d):
    with ExitStack() as ctx:
        def sb(name, shape, dt=F32):
            return ctx.enter_context(nc.sbuf_tensor(name, shape, dt))

        def sig(name, per, before=0):
            return Signal(ctx, nc, name, per, before)

        w32 = sb("w32", [P, SLOTS, BLK])
        whi = sb("whi", [P, SLOTS, BLK], F16)
        wlo = sb("wlo", [P, SLOTS, BLK], F16)
        xT = sb("xT", [P, KD * T])
        xhi = sb("xhi", [P, KD, T], F16)
        xlo = sb("xlo", [P, KD, T], F16)
        acc = sb("acc", [P, KD * T])
        ysq = sb("ysq", [P, 4, T])
        br_hi = sb("br_hi", [P, 12 * T], F16)
        br_lo = sb("br_lo", [P, 12 * T], F16)
        arena_a = sb("arena_a", [P, 24 * T])
        arena_b = sb("arena_b", [P, 17 * T])
        gates = arena_a[:, :]
        hhi = arena_a[:, 0:17 * T].bitcast(F16)
        hlo = arena_b[:, :].bitcast(F16)
        f16_a = arena_a[:, :].bitcast(F16)
        f16_b = arena_b[:, :].bitcast(F16)
        HEND = H0 + 2 * EXPERTS * CAP
        x_tok = f16_a[:, HEND:HEND + 12 * 512]
        ONE0 = 34 * T
        one_hot = f16_a[:, ONE0:ONE0 + (GROUPS + 1) * 3 * CAP]
        OT0 = ONE0 + (GROUPS + 1) * 3 * CAP
        slot_tok = f16_a[:, OT0:OT0 + GROUPS * T]
        x_grp = f16_b[:, HEND:HEND + 2 * 4 * 512].rearrange(
            "p (b a k n) -> p b a k n", b=2, a=2, k=KD)
        y_hi = f16_b[:, HEND:HEND + 4 * 512]
        y_lo = f16_b[:, HEND + 4 * 512:HEND + 8 * 512]
        mrow_m = arena_b[:, 0:4 * T]
        mrow_i = arena_b[:, 4 * T:8 * T]
        mrow_e = arena_b[:, 8 * T:12 * T]
        gvt = arena_b[:, 12 * T:12 * T + 3 * GW].rearrange("p (i n) -> p i n", i=3)
        mhi = arena_b[:, 0:4 * T].bitcast(F16).rearrange("p (n t) -> p n t", t=T)
        mlo = arena_b[:, 4 * T:8 * T].bitcast(F16).rearrange("p (n t) -> p n t", t=T)
        par = sb("par", [P, L * NPAR])
        par_c = sb("par_c", [P, NPAR])
        par_h = sb("par_h", [P, NPAR])
        par_x = sb("par_x", [P, NPAR])
        rows = sb("rows", [P, 4 * GW])
        ws_t = sb("ws_t", [P, 4 * P])
        c_init = sb("c_init", [P, MH * (DH + 1)])
        m_init = sb("m_init", [MH, L])
        rw = sb("rw", [P, KD, EXPERTS])
        rw_hi = sb("rw_hi", [P, KD, EXPERTS], F16)
        rw_lo = sb("rw_lo", [P, KD, EXPERTS], F16)
        rb = sb("rb", [P, 3, EXPERTS])
        cosT = sb("cosT", [P, T])
        sinT = sb("sinT", [P, T])
        ident = sb("ident", [P, P])
        ones = sb("ones", [P, P])
        ones_dm = sb("ones_dm", [P, P])
        eps_col = sb("eps_col", [P, 1])
        mmask = sb("mmask", [P, T])
        scan_keep = sb("scan_keep", [MH, T])
        att_mask = sb("att_mask", [MROW + 2, T + KEYS])[MROW:MROW + 2, :]
        bs_row = sb("bs_row", [1, 4 * P])
        mats16 = sb("mats16", [P, 3, P], F16)
        slot_no = sb("slot_no", [P, CAP])
        exp_sel = sb("exp_sel", [P, EXPERTS * P], F16)
        rank4 = sb("rank4", [P, 3, GROUPS])
        rank16 = sb("rank16", [P, 3, EXPERTS])
        acc3 = acc[:, :].rearrange("p (n t) -> p n t", t=T)
        front3 = arena_a[:, :].rearrange("p (n t) -> p n t", t=T)
        zf = acc3[:, 0:6, :]
        rstd = acc3[:, 6:8, :]
        znorm = front3[:, 20:24, :]
        cache = arena_a[:, 0:2 * PAST]
        cq_hi = sb("cq_hi", [P, 2, T], F16)
        cq_lo = sb("cq_lo", [P, 2, T], F16)
        kv_hi = sb("kv_hi", [P, 2, KEYS], F16)
        kv_lo = sb("kv_lo", [P, 2, KEYS], F16)
        kv_out = front3[:, 16:18, :]
        kr_t = front3[0:ROPE, 18:20, :]
        kr = sb("kr", [MROW, KEYS])[NOPE:MROW, :]
        stat = sb("stat", [P, 3, 8])
        r_f = front3[0:MH, 8:12, :]
        r_b = front3[0:MH, 5, :]
        r_a = front3[0:MH, 6, :]
        r_m = front3[0:MH, 7, :]
        scan_drop = front3[0:MH, 4, :]
        r_x = front3[0:MH, 12:16, :]
        m_at = sb("m_at", [MH, 8])
        cols = sb("cols", [P, 6 * MH])
        mq = sb("mq", [P, T])
        mk = sb("mk", [P, T])
        mo = sb("mo", [P, T])
        gu = sb("gu", [P, T])
        k_tok = sb("k_tok", [P, 3, P])
        v_tok = sb("v_tok", [P, 3, P])
        v_ws = sb("v_ws", [P, 3, DH + 1])
        dec_w = sb("dec_w", [P, 3, P])
        att = sb("att", [P, 3, P])
        q_in = sb("q_in", [P, T])
        c_st = sb("c_st", [P, 6, DH + 1])
        n_bc = sb("n_bc", [P, 4, P])
        hden = sb("hden", [P, T])
        hout = sb("hout", [P, T])
        vg = sb("vg", [P, 3, P])
        gout = hden
        q_att = arena_b[:, 0:4 * T].rearrange("p (n t) -> p n t", t=T)
        qr_t = arena_b[:, 4 * T:6 * T].rearrange("p (n t) -> p n t", t=T)
        v_kv = arena_b[:, 6 * T:6 * T + 10 * P].rearrange("p (i n) -> p i n", i=5)
        k_att = acc[:, 0:4 * KEYS].rearrange("p (n t) -> p n t", t=KEYS)
        sm = sb("sm", [P, 8])
        mu_var = sb("mu_var", [P, 4 * T])
        prob = mu_var[:, 0:6 * P].rearrange("p (b n) -> p b n", b=2)
        prob_t = ysq[:, :, :].rearrange("p a t -> p (a t)")[:, 0:6 * P].rearrange(
            "p (b i n) -> p b i n", b=2, i=3)
        mtmp = (gu, mo)
        mu = mu_var[:, 0:2 * T].rearrange("p (n t) -> p n t", t=T)
        var = mu_var[:, 2 * T:4 * T].rearrange("p (n t) -> p n t", t=T)
        ln_r = q_in
        rt = sb("rt", [P, 10, 3, EXPERTS])
        rp = sb("rp", [P, 3 * GROUPS, 6])
        rg = sb("rg", [P, 8, 3, GROUPS])
        gate_hi, gate_lo = (f16_a[:, OT0 + GROUPS * (T + n * CAP):][:, 0:GROUPS * CAP] for n in range(2))
        gate32 = hout[0:EXPERTS, :]
        gt_hi = sb("gt_hi", [P, 3, EXPERTS], F16)
        gt_lo = sb("gt_lo", [P, 3, EXPERTS], F16)
        gm16 = sb("gm16", [P, 3, GROUPS], F16)
        place = sb("place", [P, 3, GROUPS])
        most = sb("most", [P, 1])
        most_i = sb("most_i", [P, 1], mybir.dt.int32)
        ht, h1, h2 = mq, mk, mo

        bank = [ctx.enter_context(nc.psum_tensor(f"bank{i}", [P, 512], F32)) for i in range(8)]

        loaded = [sig(f"loaded{s}", 16 * NB // SLOTS) for s in range(SLOTS)]
        consts_in = sig("consts_in", 0)
        x_in = sig("x_in", 0)
        x_in2 = sig("x_in2", 0)
        par_in = sig("par_in", 0)
        stored = sig("stored", 16 * (4 + 2 * MH), 1)
        consts_set = sig("consts_set", 0)
        ws_masked = sig("ws_masked", 1)
        layer_in = sig("layer_in", 16 * 6)
        hi_done = sig("hi_done", NB)
        lo_done = sig("lo_done", NB)
        blk_done = sig("blk_done", NB)
        x_hi = sig("x_hi", 2 * KD, KD)
        x_split = sig("x_split", 2 * KD, KD)
        pars = sig("pars", 1)
        z_ev = sig("z_ev", 54)
        tokv = sig("tokv", 8)
        gv_act = sig("gv_act", 4)
        sq_c = sig("sq_c", 2)
        rms_ps = sig("rms_ps", 2)
        rms_std = sig("rms_std", 2)
        z_norm = sig("z_norm", 2)
        c_hi = sig("c_hi", 3)
        c_lo = sig("c_lo", 3)
        kr_done = sig("kr_done", 1)
        f_abs = sig("f_abs", 1)
        f_ln = sig("f_ln", 1)
        r_arg = sig("r_arg", 1)
        r_exp = sig("r_exp", 1)
        cols_ps = sig("cols_ps", 1)
        cols_sb = sig("cols_sb", 1)
        rows_out = sig("rows_out", 16)
        rows_in = sig("rows_in", 16)
        bc_m = sig("bc_m", 1)
        gv_std = sig("gv_std", 1)
        gv_var = sig("gv_var", 1)
        k_tr = sig("k_tr", MH)
        a_ps = sig("a_ps", MH)
        k_sb = sig("k_sb", MH)
        dec_done = sig("dec_done", MH)
        v_wsd = sig("v_wsd", MH)
        att_done = sig("att_done", MH, 1)
        dc_ps = sig("dc_ps", MH, 1)
        st_done = sig("st_done", MH)
        num_ps = sig("num_ps", MH, 1)
        h_done = sig("h_done", MH, 1)
        vg_done = sig("vg_done", MH)
        sp_ps = sig("sp_ps", MH, 1)
        g_done = sig("g_done", MH, 1)
        bc_hi = sig("bc_hi", 2 * MH)
        bc_lo = sig("bc_lo", 2 * MH)
        q_ev = sig("q_ev", 2)
        q_rot = sig("q_rot", 2)
        v_ev = sig("v_ev", 2)
        att_rows = sig("att_rows", 2)
        s_ps = sig("s_ps", 12, 1)
        s_max = sig("s_max", 12)
        p_exp = sig("p_exp", 12)
        p_norm = sig("p_norm", 12)
        t_ps = sig("t_ps", 12)
        t_sb = sig("t_sb", 12, 1)
        o_ps = sig("o_ps", 12)
        o_hi = sig("o_hi", 4)
        o_lo = sig("o_lo", 4, 1)
        acc_zero = sig("acc_zero", 1)
        m_used = sig("m_used", 24, 4)
        m_hi = sig("m_hi", KD)
        m_lo = sig("m_lo", KD)
        acc_pre = sig("acc_pre", 2)
        y_done = sig("y_done", 2 * KD)
        y_sq = sig("y_sq", 2 * KD)
        y_sum = sig("y_sum", 2)
        sq_sum = sig("sq_sum", 2 * (KD - 2))
        y_sub = sig("y_sub", 2 * (KD - 1))
        ln_ps = sig("ln_ps", 2)
        ln_mu = sig("ln_mu", 2)
        ln_var = sig("ln_var", 2)
        ln_std = sig("ln_std", 2)
        ln_t = sig("ln_t", 2 * KD)
        rw_h = sig("rw_h", 1)
        rw_l = sig("rw_l", 1)
        r_ps = sig("r_ps", 1)
        r_e = sig("r_e", 1)
        g_sel = sig("g_sel", 1)
        g_tr = sig("g_tr", 1)
        g_hi = sig("g_hi", 1)
        g_lo = sig("g_lo", 1)
        gm_set = sig("gm_set", 1)
        pos_ps = sig("pos_ps", 1)
        oh_set = sig("oh_set", 1)
        most_set = sig("most_set", 1)
        xt_ps = sig("xt_ps", 12)
        xt_ev = sig("xt_ev", 12)
        gt_h = sig("gt_h", 1)
        gt_l = sig("gt_l", 1)
        xg_ps = sig("xg_ps", 20)
        xg_ev = sig("xg_ev", 20)
        ot_ps = sig("ot_ps", GROUPS)
        ot_ev = sig("ot_ev", GROUPS, 1)
        yg_hi = sig("yg_hi", 2 * GROUPS)
        yg_lo = sig("yg_lo", 2 * GROUPS, 2)
        e_tanh = sig("e_tanh", EXPERTS)
        e_free = sig("e_free", EXPERTS, 2)
        e_prod = sig("e_prod", EXPERTS, 2)
        e_hi = sig("e_hi", EXPERTS)
        e_lo = sig("e_lo", EXPERTS)
        sums = sig("sums", 2)
        gb_ps = sig("gb_ps", EXPERTS)
        u_tanh = sig("u_tanh", 2 * (EXPERTS + 1))
        u_free = sig("u_free", 2 * (EXPERTS + 1))
        u_prod = sig("u_prod", 2 * (EXPERTS + 1))
        u_hi = sig("u_hi", 2 * (EXPERTS + 1))
        u_lo = sig("u_lo", 2 * (EXPERTS + 1))

        N_CONST = 14
        block = ctx.enter_context(nc.Block())

        @block.sync
        def _(sp):
            H = KD // 2 * T
            sp.dma_start(xT[:, 0:H], d["x"][:, 0:H]).then_inc(x_in.sem, 16)
            sp.dma_start(xT[:, H:KD * T], d["x"][:, H:KD * T]).then_inc(x_in2.sem, 16)
            for s in range(SLOTS):
                sp.dma_start(w32[:, s, :], d["w"][s * P:(s + 1) * P, :]).then_inc(loaded[s].sem, 16)
                if s == 0:
                    sp.dma_start(par[:, :], d["par"]).then_inc(par_in.sem, 16)
            for dst, name in ((ident[:, :], "ident"), (mmask[:, :], "mmask"),
                              (scan_keep[:, :], "scan_keep"), (mats16[:, :, :], "mats16"),
                              (slot_no[:, :], "slot_no"),
                              (m_init[:, :], "m_init"),
                              (cosT[:, :], "cos"), (sinT[:, :], "sin"),
                              (att_mask, "att_mask"),
                              (rw[:, :, :], "rw"), (exp_sel[:, :], "exp_sel"),
                              (rank4[:, :, :], "rank4"), (rank16[:, :, :], "rank16")):
                sp.dma_start(dst, d[name]).then_inc(consts_in.sem, 16)
            sp.dma_start(rb[:, :, :].rearrange("p a e -> p (a e)"),
                         d["rb"].partition_broadcast(P)).then_inc(consts_in.sem, 16)
            with sp.Fori(1, L * NB // SLOTS) as i:
                for s in range(SLOTS):
                    sp.wait_ge(lo_done.sem, i * SLOTS + (s + 1 - SLOTS))
                    sp.dma_start(w32[:, s, :], d["w"][bass.ds(i * (SLOTS * P) + s * P, P), :]
                                 ).then_inc(loaded[s].sem, 16)
            for s in range(LEAD):
                sp.wait_ge(lo_done.sem, L * NB - SLOTS + s + 1)
                sp.dma_start(w32[:, s, :], d["w"][s * P:(s + 1) * P, :]).then_inc(loaded[s].sem, 16)
            for c in range(2, KD + 1, 2):
                sp.wait_ge(x_split.sem, x_split.value(L, c - KD))
                sp.dma_start(d["y"][:, (c - 2) * T:c * T], xT[:, (c - 2) * T:c * T]
                             ).then_inc(stored.sem, 16)
            sp.wait_ge(stored.sem, stored.value(L, 16 * 4))
            for s in range(SLOTS):
                sp.wait_ge(loaded[s].sem, loaded[s].value(L, 16 if s < LEAD else 0))

        @block.gpsimd
        def _(pool):
            nc.gpsimd.memset(ones[:, :], 1.0).then_inc(consts_set.sem, 1)
            nc.gpsimd.memset(ones_dm[:, :], 1.0 / DM).then_inc(consts_set.sem, 1)
            nc.gpsimd.memset(eps_col[:, :], EPS).then_inc(consts_set.sem, 1)
            nc.gpsimd.memset(m_at[:, :], 0.0).then_inc(consts_set.sem, 1)
            nc.gpsimd.memset(stat[:, :, :], 1.0).then_inc(consts_set.sem, 1)
            nc.gpsimd.memset(gm16[:, :, :], 0.0).then_inc(consts_set.sem, 1)
            for first in (num_ps, att_done, dc_ps, h_done, g_done, s_ps, sp_ps, o_lo, t_sb, stored,
                          m_used, yg_lo, e_free, e_prod, ot_ev):
                pool.sem_inc(first.sem, first.before)
            pool.wait_ge(consts_in.sem, 16 * N_CONST)
            G = nc.gpsimd
            with pool.Fori(0, L) as l:
                pool.wait_ge(c_lo.sem, c_lo.value(l, 3))
                pool.wait_ge(kr_done.sem, kr_done.value(l, 1))
                one_r, one_m = ones[NOPE:MROW, 0:1].unsqueeze(1), ones[MROW:KATT, 0:1].unsqueeze(1)
                G.tensor_tensor(k_att[NOPE:MROW, :, :], kr.unsqueeze(1).broadcast_to([ROPE, 4, KEYS]),
                                one_r.broadcast_to([ROPE, 4, KEYS]), ALU.mult)
                G.tensor_tensor(k_att[MROW:KATT, :, :],
                                att_mask[:, T:T + KEYS].unsqueeze(1).broadcast_to([2, 4, KEYS]),
                                one_m.broadcast_to([2, 4, KEYS]), ALU.mult).then_inc(att_rows.sem, 1)
                pool.wait_ge(num_ps.sem, num_ps.value(l, MH))
                G.tensor_tensor(q_att[MROW:KATT, :, :],
                                att_mask[:, 0:T].unsqueeze(1).broadcast_to([2, 4, T]),
                                one_m.broadcast_to([2, 4, T]), ALU.mult).then_inc(att_rows.sem, 1)
                pool.wait_ge(s_ps.sem, s_ps.value(l, 12))
                pool.wait_ge(p_exp.sem, p_exp.value(l, 11))
                some = eps_col[:, 0:1].broadcast_to([P, KD * T])
                G.tensor_tensor(acc[:, :], some, some, ALU.subtract).then_inc(acc_zero.sem, 1)
                for k in range(2):
                    for c in range(1, KD - 1):
                        pool.wait_ge(y_sq.sem, y_sq.value(l, KD * k + c + 1))
                        if c > 1:
                            pool.wait_ge(sq_sum.sem, sq_sum.value(l, (KD - 2) * k + c - 1))
                        G.tensor_tensor(var[:, 1, :], ysq[:, 0, :] if c == 1 else var[:, 1, :],
                                        ysq[:, c % 4, :], ALU.add).then_inc(sq_sum.sem, 1)
                    pool.wait_ge(ln_mu.sem, ln_mu.value(l, k + 1))
                    for c in range(1, KD):
                        G.tensor_tensor(acc[:, c * T:(c + 1) * T], acc[:, c * T:(c + 1) * T],
                                        mu[:, 0, :], ALU.subtract).then_inc(y_sub.sem, 1)

        N_SET = 6

        @block.scalar
        def _(act):
            A = nc.scalar.activation

            def hi_at(l, n, s):
                act.wait_ge(loaded[s].sem, l * loaded[s].per + (n + (SLOTS - s)) * (16 // SLOTS))
                act.wait_ge(blk_done.sem, blk_done.value(l, n + (1 - SLOTS)))
                A(whi[:, s, :], w32[:, s, :], ACT.Copy, scale=WS).then_inc(hi_done.sem, 1)

            def ln_scalar(l, k, gain, bias):
                act.wait_ge(ln_ps.sem, ln_ps.value(l, k + 1))
                A(mu[:, 0, :], bank[4 + 2 * k][:, 0:T], ACT.Copy)
                A(mu[:, 1, :], bank[4 + 2 * k][:, 0:T], ACT.Square).then_inc(ln_mu.sem, 1)
                act.wait_ge(ln_var.sem, ln_var.value(l, k + 1))
                A(var[:, 1, :], var[:, 0, :], ACT.Ln, bias=eps_col[:, 0:1])
                act.drain()
                A(ln_r[:, :], var[:, 1, :], ACT.Exp, scale=-0.5).then_inc(ln_std.sem, 1)
                for c in range(KD):
                    act.wait_ge(ln_t.sem, ln_t.value(l, KD * k + c + 1))
                    if c % 2 == 0:
                        A(xT[:, c * T:(c + 1) * T], acc[:, c * T:(c + 1) * T], ACT.Identity,
                          scale=par_c[:, gain + c:gain + c + 1], bias=par_c[:, bias + c:bias + c + 1])
                    A(xhi[:, c, :], acc[:, c * T:(c + 1) * T], ACT.Identity,
                      scale=par_x[:, gain + c:gain + c + 1],
                      bias=par_x[:, bias + c:bias + c + 1]).then_inc(x_hi.sem, 1)

            def square(l, k, c):
                act.wait_ge(y_done.sem, y_done.value(l, KD * k + c + 1))
                if c >= 4:
                    act.wait_ge(sq_sum.sem, sq_sum.value(l, (KD - 2) * k + max(1, c - 4)))
                A(ysq[:, c % 4, :], acc[:, c * T:(c + 1) * T], ACT.Square).then_inc(y_sq.sem, 1)

            def hi_first(l, n):
                act.wait_ge(loaded[n].sem, loaded[n].value(l, 16))
                A(whi[:, n, :], w32[:, n, :], ACT.Copy, scale=WS).then_inc(hi_done.sem, 1)

            act.wait_ge(x_in.sem, 16)
            for c in range(KD):
                if c == KD // 2:
                    act.wait_ge(x_in2.sem, 16)
                A(xhi[:, c, :], xT[:, c * T:(c + 1) * T], ACT.Copy, scale=XS).then_inc(x_hi.sem, 1)
            for n in range(LEAD):
                hi_first(0, n)
            act.wait_ge(consts_set.sem, N_SET)
            act.wait_ge(par_in.sem, 16)

            with act.Fori(0, L) as l:
                def hi_lead(g):
                    n = g + LEAD
                    if n < SLOTS:
                        hi_first(l, n)
                    else:
                        hi_at(l, n, n % SLOTS)

                act.wait_ge(x_split.sem, x_split.value(l, 0))
                W4 = MH * (DH + 1)
                for dst, src in ((cache, d["cache"][bass.ds(l * P, P), :]),
                                 (kr[:, 0:PAST], d["krope"][bass.ds(l * ROPE, ROPE), :]),
                                 (rows[:, :], d["rows"][bass.ds(l, 1), :].broadcast_to([P, 4 * GW])),
                                 (ws_t[:, :], d["ws_t"][bass.ds(l * P, P), :]),
                                 (bs_row[:, :], d["bs_row"][bass.ds(l, 1), :]),
                                 (c_init[:, :], d["c_init"][bass.ds(l * P, P), :])):
                    act.dma_start(dst, src).then_inc(layer_in.sem, 16)
                layer_par = par[:, bass.ds(l * NPAR, NPAR)]
                A(par_c[:, :], layer_par, ACT.Copy)
                A(par_h[:, :], layer_par, ACT.Copy, scale=0.5)
                A(par_x[:, :], layer_par, ACT.Copy, scale=XS).then_inc(pars.sem, 1)
                act.wait_ge(pars.sem, pars.value(l, 1))

                for g in range(6):
                    hi_lead(g)
                    act.wait_ge(blk_done.sem, blk_done.value(l, g + 1))
                    A(zf[:, g, :], bank[g % 4][:, 0:T], ACT.Identity, scale=UN,
                      bias=par_c[:, C_FRONT + g:C_FRONT + g + 1]).then_inc(z_ev.sem, 1)
                    if g == 1:
                        act.wait_ge(f_abs.sem, f_abs.value(l, 1))
                        A(r_f[:, 2, :], r_f[:, 1, :], ACT.Exp, scale=-1.0)
                        act.drain()
                        A(r_f[:, 3, :], r_f[:, 2, :], ACT.Ln, bias=1.0).then_inc(f_ln.sem, 1)
                    if g == 2:
                        act.wait_ge(layer_in.sem, layer_in.value(l, 96))
                        A(kv_hi[:, :, 0:PAST], cache.rearrange("p (k t) -> p k t", k=2), ACT.Copy,
                          scale=XS).then_inc(c_hi.sem, 1)
                    if g == 3:
                        act.wait_ge(z_ev.sem, z_ev.value(l, 3))
                        A(ysq[:, 0:2, :], zf[:, 1:3, :], ACT.Square).then_inc(sq_c.sem, 1)
                    if g == 5:
                        act.wait_ge(z_ev.sem, z_ev.value(l, 5))
                        A(ysq[:, 2:4, :], zf[:, 3:5, :], ACT.Square).then_inc(sq_c.sem, 1)
                for i in range(4):
                    hi_lead(6 + i)
                    if i == 1:
                        for k in range(2):
                            act.wait_ge(rms_ps.sem, rms_ps.value(l, k + 1))
                            A(rstd[:, k, :], bank[4 + k][:, 0:T], ACT.Ln, scale=DM / RANK,
                              bias=eps_col[:, 0:1])
                        act.drain()
                        for k in range(2):
                            A(rstd[:, k, :], rstd[:, k, :], ACT.Exp, scale=-0.5
                              ).then_inc(rms_std.sem, 1)
                        act.wait_ge(r_arg.sem, r_arg.value(l, 1))
                        A(r_x[:, 1:4, :], r_x[:, 1:4, :], ACT.Exp).then_inc(r_exp.sem, 1)
                        act.wait_ge(r_exp.sem, r_exp.value(l, 1))
                        act.dma_start(d["head_rows"].rearrange("o (j h t) -> (o h) j t", j=3, h=MH),
                                      r_x[:, 0:3, :]).then_inc(rows_out.sem, 16)
                    if i == 2:
                        act.wait_ge(rows_out.sem, rows_out.value(l, 16))
                        act.dma_start(arena_b[:, 0:3 * MH * T],
                                      d["head_rows"].broadcast_to([P, 3 * MH * T])
                                      ).then_inc(rows_in.sem, 16)
                    if i == 3:
                        act.wait_ge(z_norm.sem, z_norm.value(l, 2))
                        A(cq_hi[:, 0, :], znorm[:, 0, :], ACT.Copy, scale=par_x[:, C_QG:C_QG + 1])
                        A(cq_hi[:, 1, :], znorm[:, 1, :], ACT.Copy,
                          scale=par_x[:, C_QG + 1:C_QG + 2]).then_inc(c_hi.sem, 1)
                        act.wait_ge(stored.sem, stored.value(l, 0))
                        for c in range(2):
                            A(kv_out[:, c, :], znorm[:, 2 + c, :], ACT.Copy,
                              scale=par_c[:, C_KVG + c:C_KVG + c + 1])
                        A(kv_hi[:, 0, PAST:KEYS], znorm[:, 2, :], ACT.Copy,
                          scale=par_x[:, C_KVG:C_KVG + 1])
                        A(kv_hi[:, 1, PAST:KEYS], znorm[:, 3, :], ACT.Copy,
                          scale=par_x[:, C_KVG + 1:C_KVG + 2]).then_inc(c_hi.sem, 1)
                    act.wait_ge(tokv.sem, tokv.value(l, i + 1))
                    A(gvt[:, 0:2, i * P:(i + 1) * P], gvt[:, 0:2, i * P:(i + 1) * P], ACT.Gelu_apprx_tanh)
                    A(gvt[0:TS, 2, i * P:(i + 1) * P], gvt[0:TS, 2, i * P:(i + 1) * P],
                      ACT.Gelu_apprx_tanh).then_inc(gv_act.sem, 1)
                act.wait_ge(c_hi.sem, c_hi.value(l, 3))
                act.dma_start(d["ckv"][bass.ds(l * P, P), :],
                              kv_out[:, :, :].rearrange("p k t -> p (k t)")).then_inc(stored.sem, 16)
                act.wait_ge(kr_done.sem, kr_done.value(l, 1))
                act.dma_start(d["kr_out"][bass.ds(l * ROPE, ROPE), :],
                              kr[:, PAST:KEYS]).then_inc(stored.sem, 16)
                act.dma_start(d["m_out"][bass.ds(l * MH, MH), :], m_at[:, :]).then_inc(stored.sem, 16)
                act.wait_ge(gv_var.sem, gv_var.value(l, 1))
                A(stat[:, :, 2:3], stat[:, :, 1:2], ACT.Sqrt, bias=eps_col[:, 0:1]).then_inc(gv_std.sem, 1)

                with act.Fori(0, MH) as h:
                    g0 = h * MPER + M0

                    def evac(step, dst, func, par_t, col, scale=UN):
                        act.wait_ge(blk_done.sem, blk_done.value(l, g0 + (step + 1)))
                        A(dst, bank[(M0 + step) % 4][:, 0:T], func, scale=scale,
                          bias=par_t[:, bass.ds(col, 1)]).then_inc(z_ev.sem, 1)

                    def hi_m(step):
                        hi_at(l, g0 + (step + LEAD), (M0 + step + LEAD) % SLOTS)

                    hi_m(0)
                    act.wait_ge(num_ps.sem, num_ps.value(l, h))
                    evac(0, mq[:, :], ACT.Identity, par_c, h * 4 + C_MLSTM)
                    hi_m(1)
                    evac(1, mk[:, :], ACT.Identity, par_c, h * 4 + (C_MLSTM + 1))
                    hi_m(2)
                    act.wait_ge(att_done.sem, att_done.value(l, h))
                    act.wait_ge(cols_sb.sem, cols_sb.value(l, 1))
                    act.wait_ge(bc_m.sem, bc_m.value(l, 1))
                    for i, (t0, n) in enumerate(TILES):
                        a = A(dec_w[0:n, i, 0:n], mrow_m[0:n, bass.ds(h * T + t0, n)], ACT.Exp,
                              bias=cols[0:n, bass.ds(h + i * MH, 1)])
                    a.then_inc(dec_done.sem, 1)
                    act.wait_ge(k_tr.sem, k_tr.value(l, h + 1))
                    act.wait_ge(dc_ps.sem, dc_ps.value(l, h))
                    A(k_tok[:, 0:2, :], bank[4][:, 0:2 * P].rearrange("p (i n) -> p i n", i=2), ACT.Copy)
                    A(k_tok[0:TS, 2, :], bank[4][0:TS, 2 * P:3 * P], ACT.Copy).then_inc(k_sb.sem, 1)
                    hi_m(3)
                    act.wait_ge(h_done.sem, h_done.value(l, h))
                    evac(3, mo[:, :], ACT.Tanh, par_h, h * 4 + (C_MLSTM + 2), scale=UN / 2)
                    hi_m(4)
                    act.wait_ge(g_done.sem, g_done.value(l, h))
                    evac(4, gu[:, :], ACT.Gelu_apprx_tanh, par_c, h * 4 + (C_MLSTM + 3))
                    for j in range(3):
                        hi_m(5 + j)
                        evac(5 + j, gates[:, bass.ds((h * 3 + j) * T, T)], ACT.Tanh, par_h,
                             h * 3 + (C_GATE + j), scale=UN / 2)
                    act.wait_ge(st_done.sem, st_done.value(l, h + 1))
                    act.dma_start(d["c_prompt"][bass.ds((l * MH + h) * P, P), :], c_st[:, 3, :]
                                  ).then_inc(stored.sem, 16)
                    act.dma_start(d["c_sample"][bass.ds((l * MH + h) * P, P), :], c_st[:, 5, :]
                                  ).then_inc(stored.sem, 16)
                    act.wait_ge(h_done.sem, h_done.value(l, h + 1))
                    A(br_hi[:, bass.ds((h + 4) * T, T)], hout[:, :], ACT.Copy, scale=XS / 2
                      ).then_inc(bc_hi.sem, 1)
                    act.wait_ge(g_done.sem, g_done.value(l, h + 1))
                    A(br_hi[:, bass.ds((h + 8) * T, T)], gout[:, :], ACT.Copy, scale=XS
                      ).then_inc(bc_hi.sem, 1)

                act.wait_ge(vg_done.sem, vg_done.value(l, MH))
                act.dma_start(d["gv_out"][bass.ds(l * TS, TS), :], gvt[0:TS, 2, :]).then_inc(stored.sem, 16)

                with act.Fori(0, 2) as hf:
                    g0 = hf * APER + A0

                    def hi_a(step):
                        hi_at(l, g0 + (step + LEAD), (A0 + step + LEAD) % SLOTS)

                    act.wait_ge(blk_done.sem, blk_done.value(l, g0 + 1))
                    act.wait_ge(s_ps.sem, s_ps.value(l, hf * 6))
                    for j in range(4):
                        r0 = NOPE * (j % 2)
                        a = A(q_att[0:NOPE, j, :], bank[4 + j // 2][r0:r0 + NOPE, 0:T], ACT.Copy,
                              scale=UN)
                    a.then_inc(q_ev.sem, 1)
                    hi_a(0)
                    hi_a(1)
                    act.wait_ge(blk_done.sem, blk_done.value(l, g0 + 2))
                    for j in range(4):
                        for r in range(2):
                            a = A(k_att[0:NOPE, 2 * (j // 2) + r, (j % 2) * KH:(j % 2 + 1) * KH],
                                  bank[j][NOPE * r:NOPE * (r + 1), 0:KH], ACT.Copy, scale=UN)
                        a.then_inc(z_ev.sem, 1)

                    def gate_tanh(j):
                        act.wait_ge(blk_done.sem, blk_done.value(l, g0 + (3 + j)))
                        A(gates[:, bass.ds((hf * 6 + (12 + j)) * T, T)],
                          bank[(A0 + 2 + j) % 4][:, 0:T], ACT.Tanh, scale=UN / 2,
                          bias=par_h[:, bass.ds(hf * 6 + (C_GATE + 12 + j), 1)]).then_inc(z_ev.sem, 1)

                    def exps(j):
                        u = hf * 6 + j
                        act.wait_ge(s_max.sem, s_max.value(l, u + 1))
                        if j >= 2:
                            act.wait_ge(t_ps.sem, t_ps.value(l, u - 1))
                        b = bank[4 + j % 2]
                        if j % 3 < 2:
                            A(prob[:, j % 2, 0:P], b[:, 0:P], ACT.Exp, scale=ATT_SCALE,
                              bias=sm[:, 2:3], accum_out=sm[:, 4:5])
                            A(prob[:, j % 2, P:3 * P], b[:, P:3 * P], ACT.Exp, scale=ATT_SCALE,
                              bias=sm[:, 3:4], accum_out=sm[:, 5:6]).then_inc(p_exp.sem, 1)
                        else:
                            A(prob[:, j % 2, 0:T], b[:, 0:T], ACT.Exp, scale=ATT_SCALE,
                              bias=sm[:, 2:3], accum_out=sm[:, 4:5]).then_inc(p_exp.sem, 1)

                    def probs_out(j):
                        u = hf * 6 + j
                        act.wait_ge(t_ps.sem, t_ps.value(l, u + 1))
                        if j >= 2:
                            act.wait_ge(o_ps.sem, o_ps.value(l, u - 1))
                        if j % 3 < 2:
                            A(prob_t[:, j % 2, :, :], bank[6][:, 0:3 * P].rearrange(
                                "p (i n) -> p i n", i=3), ACT.Copy).then_inc(t_sb.sem, 1)
                        else:
                            A(prob_t[:, j % 2, 0:2, :], bank[6][:, 0:2 * P].rearrange(
                                "p (i n) -> p i n", i=2), ACT.Copy)
                            A(prob_t[0:TS, j % 2, 2, :], bank[6][0:TS, 2 * P:3 * P], ACT.Copy
                              ).then_inc(t_sb.sem, 1)

                    def out_hi(p):
                        act.wait_ge(o_ps.sem, o_ps.value(l, hf * 6 + (3 * p + 3)))
                        A(br_hi[:, bass.ds((hf * 2 + p) * T, T)], bank[7][:, 0:T], ACT.Copy,
                          scale=XS).then_inc(o_hi.sem, 1)

                    for j in range(6):
                        if j == 5:
                            out_hi(0)
                        hi_a(2 + j)
                        if j:
                            gate_tanh(j - 1)
                        exps(j)
                        if j:
                            probs_out(j - 1)
                    gate_tanh(5)
                    probs_out(5)
                    out_hi(1)

                with act.Fori(0, 3) as k:
                    for j in range(4):
                        hi_at(l, k * 4 + (B0 + j + LEAD), (B0 + j + LEAD) % SLOTS)
                for c in range(KD):
                    act.wait_ge(m_used.sem, m_used.value(l, 17 + c))
                    A(mhi[:, c, :], acc[:, c * T:(c + 1) * T], ACT.Copy, scale=UN * XS / 2
                      ).then_inc(m_hi.sem, 1)
                act.wait_ge(m_lo.sem, m_lo.value(l, KD))
                A(acc[:, :], xT[:, :], ACT.Copy, scale=ALPHA).then_inc(acc_pre.sem, 1)

                act.wait_ge(stored.sem, stored.value(l, 16 * (4 + 2 * MH)))
                A(rw_hi[:, :, :], rw[:, :, :], ACT.Copy, scale=WS).then_inc(rw_h.sem, 1)
                for c in range(KD):
                    hi_lead(O0 + c)
                    square(l, 0, c)
                ln_scalar(l, 0, C_L1G, C_L1B)
                act.wait_ge(x_split.sem, x_split.value(l, KD))
                A(acc[:, :], xT[:, :], ACT.Copy, scale=ALPHA).then_inc(acc_pre.sem, 1)

                UPB = [(U0 + j) % 4 for j in range(4)]
                UE = 2 * (EXPERTS + 1)

                def x_tokens(j):
                    for n in range(3 * j, 3 * j + 3):
                        act.wait_ge(xt_ps.sem, xt_ps.value(l, n + 1))
                        A(x_tok[:, n * 512:(n + 1) * 512], bank[4 + n % 3][:, :], ACT.Copy
                          ).then_inc(xt_ev.sem, 1)

                act.wait_ge(r_ps.sem, r_ps.value(l, 1))
                for i, b in enumerate((4, 5, 7)):
                    a = A(rt[:, 0, i, :], bank[b][:, i * EXPERTS:(i + 1) * EXPERTS], ACT.Exp, scale=-UN)
                a.then_inc(r_e.sem, 1)
                hi_lead(U0)
                hi_lead(U0 + 1)
                x_tokens(0)

                def shared_tanh(f):
                    act.wait_ge(blk_done.sem, blk_done.value(l, U0 + 2 * f + 1))
                    A(ht[:, :], bank[UPB[2 * f]][:, 0:T], ACT.Tanh, scale=UN / 2).then_inc(u_tanh.sem, 1)

                def shared_hi(f):
                    act.wait_ge(u_prod.sem, u_prod.value(l, f + 1))
                    A(hhi[:, f * T:(f + 1) * T], h2[:, :], ACT.Copy, scale=UN * UN * XS / 2
                      ).then_inc(u_hi.sem, 1)

                shared_tanh(0)
                for j in range(1, 4):
                    x_tokens(j)
                    if j < 3:
                        hi_lead(U0 + 1 + j)
                act.wait_ge(g_sel.sem, g_sel.value(l, 1))
                act.wait_ge(most_set.sem, most_set.value(l, 1))
                A(gt_hi[:, :, :], rt[:, 7], ACT.Copy, scale=GS).then_inc(gt_h.sem, 1)

                def expert_hi(e, W, h0):
                    g0 = e * 4 + (U0 + 4)
                    for f in range(2):
                        hi_at(l, g0 + (2 * f + LEAD), (U0 + 2 * f + LEAD) % SLOTS)
                        hi_at(l, g0 + (2 * f + 1 + LEAD), (U0 + 2 * f + 1 + LEAD) % SLOTS)
                        n = e * 2 + (2 + f)
                        act.wait_ge(blk_done.sem, blk_done.value(l, g0 + (2 * f + 1)))
                        act.wait_ge(u_free.sem, u_free.value(l, n))
                        A(ht[:, 0:W], bank[UPB[2 * f]][:, 0:W], ACT.Tanh, scale=UN / 2
                          ).then_inc(u_tanh.sem, 1)
                        act.wait_ge(u_prod.sem, u_prod.value(l, n + 1))
                        A(hhi[:, bass.ds((e * 2 + f) * W + h0, W)], h2[:, 0:W], ACT.Copy,
                          scale=UN * UN * XS / (2 * GS)).then_inc(u_hi.sem, 1)

                fits = act.value_load(most_i[0:1, 0:1]) < CAP + 1
                with act.If(fits):
                    for q in range(4):
                        if q == 2:
                            shared_hi(0)
                        act.wait_ge(xg_ps.sem, xg_ps.value(l, q + 1))
                        A(x_grp[:, 0, q // 2, 4 * (q % 2):4 * (q % 2) + 4, :], bank[5 + q % 2][:, :]
                          .rearrange("p (k n) -> p k n", k=4), ACT.Copy).then_inc(xg_ev.sem, 1)
                    act.wait_ge(u_free.sem, u_free.value(l, 1))
                    shared_tanh(1)
                    act.wait_ge(g_tr.sem, g_tr.value(l, 1))
                    A(gate_hi[0:EXPERTS, :], bank[4][0:EXPERTS, :], ACT.Copy).then_inc(g_hi.sem, 1)
                    shared_hi(1)
                    hi_lead(U0 + 4)
                    with act.Fori(0, GROUPS // 2) as gg:
                        for g2 in range(2):
                            act.wait_ge(ot_ps.sem, ot_ps.value(l, gg * 2 + (g2 + 1)))
                            A(slot_tok[:, bass.ds((gg * 2 + g2) * T, T)], bank[7][:, 0:T], ACT.Copy,
                              scale=1 / (UN * XS)).then_inc(ot_ev.sem, 1)
                            with act.Fori(0, 2) as qq:
                                for e2 in range(2):
                                    e = gg * 8 + qq * 2 + (4 * g2 + e2)
                                    g0 = e * 4 + (U0 + 4)

                                    def hi_e(j):
                                        hi_at(l, g0 + (j + LEAD), (U0 + j + LEAD) % SLOTS)

                                    hi_e(1)
                                    hi_e(2)
                                    act.wait_ge(blk_done.sem, blk_done.value(l, g0 + 3))
                                    act.wait_ge(e_free.sem, e_free.value(l, e))
                                    A(ht[:, 0:2 * CAP], bank[UPB[2 * e2]][:, 0:2 * CAP], ACT.Tanh,
                                      scale=UN / 2).then_inc(e_tanh.sem, 1)
                                    hi_e(3)
                                    act.wait_ge(xg_ps.sem, xg_ps.value(l, e + 5))
                                    A(f16_b[:, bass.ds(qq * 1024 + (e2 * 512 + HEND + (1 - g2) * 2048),
                                                       512)], bank[5][:, :], ACT.Copy
                                      ).then_inc(xg_ev.sem, 1)
                                    hi_e(4)
                                    act.wait_ge(e_prod.sem, e_prod.value(l, e + 1))
                                    A(hhi[:, bass.ds(e * (2 * CAP) + H0, 2 * CAP)], h2[:, 0:2 * CAP],
                                      ACT.Copy, scale=UN * UN * XS / (2 * GS)).then_inc(e_hi.sem, 1)

                    def group_out(g, g2, hf):
                        act.wait_ge(blk_done.sem, blk_done.value(l, g * 4 + ((D0, D1)[hf] + 5)))
                        A(y_hi[:, bass.ds(g * 512, 512)], bank[(4, 2)[hf] + g2][:, :], ACT.Copy,
                          scale=UN * XS).then_inc(yg_hi.sem, 1)

                    with act.Fori(0, GROUPS // 2) as gg:
                        for g2 in range(2):
                            for j in range(4):
                                n = D0 + 4 + 4 * g2 + j
                                hi_at(l, gg * 8 + n, n % SLOTS)
                            group_out(gg * 2 + g2, g2, 0)
                    for c in range(4):
                        square(l, 1, c)
                    for g in range(GROUPS):
                        for j in range(4):
                            hi_lead(D1 + 3 + 4 * g + j - LEAD)
                        group_out(g, g % 2, 1)
                    hi_lead(NB - 1)
                    act.sem_inc(u_tanh.sem, 2 * EXPERTS)
                    act.sem_inc(u_hi.sem, 2 * EXPERTS)
                with act.Else():
                    for s_, n in ((xg_ev, 20), (ot_ev, GROUPS), (yg_hi, 2 * GROUPS), (e_tanh, EXPERTS),
                                  (e_hi, EXPERTS)):
                        act.sem_inc(s_.sem, n)
                    shared_hi(0)
                    act.wait_ge(u_free.sem, u_free.value(l, 1))
                    shared_tanh(1)
                    shared_hi(1)
                    act.wait_ge(g_tr.sem, g_tr.value(l, 1))
                    A(gate32[:, 0:TP], bank[6][0:EXPERTS, 0:TP], ACT.Copy, scale=GS)
                    A(gate32[:, TP:T], bank[6][0:EXPERTS, 3 * P - TS:3 * P], ACT.Copy, scale=GS)
                    A(gate_hi[0:EXPERTS, 0:TP], bank[6][0:EXPERTS, 0:TP], ACT.Copy, scale=GS)
                    A(gate_hi[0:EXPERTS, TP:T], bank[6][0:EXPERTS, 3 * P - TS:3 * P], ACT.Copy, scale=GS
                      ).then_inc(g_hi.sem, 1)
                    with act.Fori(0, EXPERTS) as e:
                        expert_hi(e, T, H0)
                    hi_lead(D0)
                    with act.Fori(0, 4) as i:
                        for j in range(4):
                            hi_at(l, i * 4 + (D0 + 1 + j + LEAD), (D0 + 1 + j + LEAD) % SLOTS)
                    hi_lead(D1)
                    for c in range(4):
                        square(l, 1, c)
                    with act.Fori(0, 3) as i:
                        for j in range(4):
                            hi_at(l, i * 4 + (D1 + 1 + j + LEAD), (D1 + 1 + j + LEAD) % SLOTS)
                    for j in range(4):
                        hi_lead(D1 + 13 + j)
                for c in range(4, KD):
                    square(l, 1, c)
                ln_scalar(l, 1, C_L2G, C_L2B)


        @block.vector
        def _(dve):
            V = nc.vector

            def lo_at(l, n, s):
                dve.wait_ge(hi_done.sem, hi_done.value(l, n + 1))
                V.scalar_tensor_tensor(wlo[:, s, :], w32[:, s, :], WS, whi[:, s, :], ALU.mult,
                                       ALU.subtract).then_inc(lo_done.sem, 1)

            def ln_vector(l, k, gain, bias):
                dve.wait_ge(ln_mu.sem, ln_mu.value(l, k + 1))
                V.tensor_tensor(var[:, 0, :], bank[5 + 2 * k][:, 0:T], mu[:, 1, :], ALU.subtract)
                dve.drain()
                V.tensor_scalar(var[:, 0, :], var[:, 0, :], 0.0, None, ALU.max).then_inc(ln_var.sem, 1)
                y = [acc[:, c * T:(c + 1) * T] for c in range(KD)]
                V.tensor_tensor(y[0], y[0], mu[:, 0, :], ALU.subtract)
                dve.drain()
                dve.wait_ge(ln_std.sem, ln_std.value(l, k + 1))

                def split(c):
                    if c % 2:
                        dve.drain()
                    dve.wait_ge(x_hi.sem, x_hi.value(l, KD * k + c + 1))
                    V.scalar_tensor_tensor(xlo[:, c, :], xT[:, c * T:(c + 1) * T], XS, xhi[:, c, :],
                                           ALU.mult, ALU.subtract).then_inc(x_split.sem, 1)

                for c in range(KD):
                    if c:
                        dve.wait_ge(y_sub.sem, y_sub.value(l, (KD - 1) * k + c))
                    V.tensor_tensor(y[c], y[c], ln_r[:, :], ALU.mult).then_inc(ln_t.sem, 1)
                    if c % 2:
                        dve.drain()
                        V.tensor_scalar(xT[:, c * T:(c + 1) * T], y[c], par_c[:, gain + c:gain + c + 1],
                                        par_c[:, bias + c:bias + c + 1], ALU.mult, ALU.add)
                    if c:
                        split(c - 1)
                split(KD - 1)

            def residual(l, k, c, b):
                V.scalar_tensor_tensor(acc[:, c * T:(c + 1) * T], bank[b][:, 0:T], UN,
                                       acc[:, c * T:(c + 1) * T], ALU.mult, ALU.add
                                       ).then_inc(y_done.sem, 1)
                if 0 < c < KD - 1:
                    dve.drain()
                    a = V.tensor_tensor(var[:, 0, :], acc[:, 0:T] if c == 1 else var[:, 0, :],
                                        acc[:, c * T:(c + 1) * T], ALU.add)
                if c == KD - 2:
                    a.then_inc(y_sum.sem, 1)

            for c in range(KD):
                dve.wait_ge(x_hi.sem, c + 1)
                V.scalar_tensor_tensor(xlo[:, c, :], xT[:, c * T:(c + 1) * T], XS, xhi[:, c, :],
                                       ALU.mult, ALU.subtract).then_inc(x_split.sem, 1)
            for n in range(LEAD):
                lo_at(0, n, n)
            dve.wait_ge(consts_set.sem, N_SET)

            with dve.Fori(0, L) as l:
                def lo_lead(g):
                    n = g + LEAD
                    lo_at(l, n, n % SLOTS)

                lo_lead(0)
                dve.wait_ge(z_ev.sem, z_ev.value(l, 1))
                V.tensor_copy(r_f[:, 0, :], zf[32:32 + MH, 0, :])
                dve.drain()
                V.scalar_tensor_tensor(r_f[:, 1, :], r_f[:, 0, :], -1.0, r_f[:, 0, :], ALU.mult, ALU.max
                                       ).then_inc(f_abs.sem, 1)
                lo_lead(1)
                lo_lead(2)
                dve.wait_ge(consts_in.sem, 16 * N_CONST)
                dve.wait_ge(stored.sem, stored.value(l, 0))
                V.tensor_scalar(scan_drop, scan_keep[:, :], -1.0, -NEG, ALU.add, ALU.mult)
                V.tensor_copy(m_at[:, 5:6], m_init[:, bass.ds(l, 1)])
                dve.wait_ge(f_ln.sem, f_ln.value(l, 1))
                V.scalar_tensor_tensor(r_f[:, 0, :], r_f[:, 0, :], 0.0, r_f[:, 3, :], ALU.min,
                                       ALU.subtract)
                dve.drain()
                V.tensor_tensor_scan(r_b, scan_keep[:, :], r_f[:, 0, :], 0.0, ALU.mult, ALU.add)
                dve.drain()
                V.tensor_tensor(r_a, zf[0:MH, 0, :], r_b, ALU.subtract)
                dve.drain()
                V.tensor_tensor_scan(r_m, scan_drop, r_a, 0.0, ALU.add, ALU.max)
                lo_lead(3)
                dve.wait_ge(c_hi.sem, c_hi.value(l, 1))
                V.scalar_tensor_tensor(kv_lo[:, :, 0:PAST], cache.rearrange("p (k t) -> p k t", k=2),
                                       XS, kv_hi[:, :, 0:PAST], ALU.mult, ALU.subtract
                                       ).then_inc(c_lo.sem, 1)
                ws3 = ws_t[:, :].rearrange("p (n t) -> p n t", t=P)
                V.tensor_tensor(ws3, ws3, mats16[:, 1:2, :].broadcast_to([P, 4, P]), ALU.mult
                                ).then_inc(ws_masked.sem, 1)
                for c in range(NCH):
                    s = c if c < 4 else 5
                    e = (c + 1) * CH - 1
                    dve.drain()
                    V.scalar_tensor_tensor(m_at[:, s + 1:s + 2], r_m[:, e:e + 1], m_at[:, s:s + 1],
                                           r_b[:, e:e + 1], ALU.max, ALU.add)
                dve.drain()
                m_p = m_at[:, 0:4].unsqueeze(2).broadcast_to([MH, 4, CH])
                rm_p = r_m[:, 0:TP].rearrange("p (c t) -> p c t", t=CH)
                V.tensor_tensor(rm_p, rm_p, m_p, ALU.max)
                V.tensor_scalar(r_m[:, TP:T], r_m[:, TP:T], m_at[:, 5:6], None, ALU.max)
                dve.drain()
                V.tensor_scalar(r_x[:, 0, :], r_m, -1.0, None, ALU.mult)
                dve.drain()

                def chunks(ap):
                    return ap.rearrange("p (c t) -> p c t", t=CH)

                V.tensor_tensor(chunks(r_x[:, 1, 0:TP]), chunks(r_x[:, 0, 0:TP]), m_p, ALU.add)
                V.tensor_scalar(r_x[:, 1, TP:T], r_x[:, 0, TP:T], m_at[:, 5:6], None, ALU.add)
                V.tensor_tensor(r_x[:, 2, :], r_x[:, 0, :], r_b, ALU.subtract)
                V.tensor_tensor(chunks(r_x[:, 3, :]), chunks(r_a),
                                chunks(r_x[:, 0, :])[:, :, CH - 1:CH].broadcast_to([MH, NCH, CH]),
                                ALU.add).then_inc(r_arg.sem, 1)
                lo_lead(4)
                lo_lead(5)
                dve.wait_ge(z_ev.sem, z_ev.value(l, 6))
                V.tensor_tensor(kr_t[:, 0, :], zf[0:ROPE, 5, :], cosT[0:ROPE, :], ALU.mult)
                V.tensor_tensor(kr_t[:, 1, :], zf[ROPE:2 * ROPE, 5, :], sinT[ROPE:2 * ROPE, :], ALU.mult)
                dve.drain()
                V.tensor_tensor(kr[:, PAST:KEYS], kr_t[:, 0, :], kr_t[:, 1, :], ALU.add
                                ).then_inc(kr_done.sem, 1)

                def tok_out(b, dst2, dst1, row, last):
                    V.scalar_tensor_tensor(dst2, bank[b][:, 0:2 * P].rearrange("p (i n) -> p i n", i=2),
                                           UN, row.unsqueeze(1).broadcast_to([P, 2, P]), ALU.mult,
                                           ALU.add)
                    V.scalar_tensor_tensor(dst1, bank[b][0:TS, 2 * P:3 * P], UN, row[0:TS, :],
                                           ALU.mult, ALU.add).then_inc(last.sem, 1)

                for i in range(4):
                    lo_lead(6 + i)
                    if i == 1:
                        for k in range(2):
                            dve.wait_ge(rms_std.sem, rms_std.value(l, k + 1))
                            V.tensor_tensor(znorm[:, 2 * k:2 * k + 2, :], zf[:, 1 + 2 * k:3 + 2 * k, :],
                                            rstd[:, k:k + 1, :].broadcast_to([P, 2, T]), ALU.mult
                                            ).then_inc(z_norm.sem, 1)
                    dve.wait_ge(blk_done.sem, blk_done.value(l, 7 + i))
                    tok_out((6 + i) % 4, gvt[:, 0:2, i * P:(i + 1) * P],
                            gvt[0:TS, 2, i * P:(i + 1) * P],
                            rows[:, i * P:(i + 1) * P], tokv)
                dve.wait_ge(c_hi.sem, c_hi.value(l, 2))
                V.scalar_tensor_tensor(cq_lo[:, 0, :], znorm[:, 0, :], par_x[:, C_QG:C_QG + 1],
                                       cq_hi[:, 0, :], ALU.mult, ALU.subtract)
                V.scalar_tensor_tensor(cq_lo[:, 1, :], znorm[:, 1, :], par_x[:, C_QG + 1:C_QG + 2],
                                       cq_hi[:, 1, :], ALU.mult, ALU.subtract).then_inc(c_lo.sem, 1)
                dve.wait_ge(c_hi.sem, c_hi.value(l, 3))
                V.scalar_tensor_tensor(kv_lo[:, 0, PAST:KEYS], znorm[:, 2, :],
                                       par_x[:, C_KVG:C_KVG + 1], kv_hi[:, 0, PAST:KEYS], ALU.mult,
                                       ALU.subtract)
                V.scalar_tensor_tensor(kv_lo[:, 1, PAST:KEYS], znorm[:, 3, :],
                                       par_x[:, C_KVG + 1:C_KVG + 2], kv_hi[:, 1, PAST:KEYS], ALU.mult,
                                       ALU.subtract).then_inc(c_lo.sem, 1)
                dve.wait_ge(cols_ps.sem, cols_ps.value(l, 1))
                V.tensor_copy(cols[:, 0:2 * MH], bank[7][:, 0:2 * MH])
                V.tensor_copy(cols[0:TS, 2 * MH:3 * MH], bank[7][0:TS, 2 * MH:3 * MH])
                V.tensor_scalar(cols[:, 3 * MH:5 * MH], bank[7][:, 3 * MH:5 * MH], KSCALE, None, ALU.mult)
                V.tensor_scalar(cols[0:TS, 5 * MH:6 * MH], bank[7][0:TS, 5 * MH:6 * MH], KSCALE, None,
                                ALU.mult).then_inc(cols_sb.sem, 1)
                dve.wait_ge(gv_act.sem, gv_act.value(l, 4))
                for i, (t0, n) in enumerate(TILES):
                    V.bn_stats(rp[0:n, i, :], gvt[0:n, i, :])
                dve.drain()
                for i, (t0, n) in enumerate(TILES):
                    a = V.bn_aggr(stat[0:n, i, 0:2], rp[0:n, i, :])
                a.then_inc(gv_var.sem, 1)
                dve.wait_ge(rows_in.sem, rows_in.value(l, 16))
                rows_m = mrow_m.rearrange("p (h t) -> p h t", h=MH)
                V.tensor_tensor(rows_m, rows_m, mmask[:, :].unsqueeze(1).broadcast_to([P, MH, T]), ALU.add
                                ).then_inc(bc_m.sem, 1)
                dve.wait_ge(gv_std.sem, gv_std.value(l, 1))
                V.reciprocal(stat[:, :, 3:4], stat[:, :, 2:3])

                with dve.Fori(0, MH) as h:
                    g0 = h * MPER + M0

                    def lo_m(step):
                        lo_at(l, g0 + (step + LEAD), (M0 + step + LEAD) % SLOTS)

                    lo_m(0)
                    lo_m(1)
                    dve.wait_ge(z_ev.sem, z_ev.value(l, h * 7 + 7))
                    dve.wait_ge(rows_in.sem, rows_in.value(l, 16))
                    V.tensor_tensor(q_in[:, :], mq[:, :], mrow_i[:, bass.ds(h * T, T)], ALU.mult)
                    lo_m(2)
                    dve.wait_ge(blk_done.sem, blk_done.value(l, g0 + 3))
                    tok_out((M0 + 2) % 4, v_tok[:, 0:2, :], v_tok[0:TS, 2, :],
                            rows[:, bass.ds(h * P + GW, P)], tokv)
                    dve.drain()
                    for i, (t0, n) in enumerate(TILES):
                        w = cols[0:n, bass.ds(h + (3 + i) * MH, 1)]
                        V.tensor_scalar(v_ws[0:n, i, 0:DH], v_tok[0:n, i, :], w, None, ALU.mult)
                        a = V.tensor_copy(v_ws[0:n, i, DH:DH + 1], w)
                    a.then_inc(v_wsd.sem, 1)
                    dve.wait_ge(dec_done.sem, dec_done.value(l, h + 1))
                    dve.wait_ge(a_ps.sem, a_ps.value(l, h + 1))
                    V.scalar_tensor_tensor(att[:, 0:2, :], bank[5][:, 0:2 * P].rearrange(
                        "p (i n) -> p i n", i=2), KSCALE, dec_w[:, 0:2, :], ALU.mult, ALU.mult)
                    V.scalar_tensor_tensor(att[0:TS, 2, 0:TS], bank[5][0:TS, 2 * P:2 * P + TS], KSCALE,
                                           dec_w[0:TS, 2, 0:TS], ALU.mult, ALU.mult
                                           ).then_inc(att_done.sem, 1)
                    lo_m(3)
                    dve.wait_ge(dc_ps.sem, dc_ps.value(l, h + 1))
                    dve.wait_ge(stored.sem, stored.value(l, h * 32 + 48))

                    def decay(c):
                        return mrow_i[:, bass.ds(h * T + (c * CH + CH - 1), 1)]

                    W1 = DH + 1
                    V.tensor_copy(c_st[:, 4, :], c_init[:, bass.ds(h * W1, W1)])
                    V.tensor_copy(c_st[:, 0, :], bank[6][:, 0:W1])
                    dve.drain()
                    V.scalar_tensor_tensor(c_st[:, 5, :], c_st[:, 4, :], decay(4),
                                           bank[6][:, 2 * W1:3 * W1], ALU.mult, ALU.add)
                    V.scalar_tensor_tensor(c_st[:, 1, :], c_st[:, 0, :], decay(1),
                                           bank[7][:, 0:W1], ALU.mult, ALU.add)
                    dve.drain()
                    V.scalar_tensor_tensor(c_st[:, 2, :], c_st[:, 1, :], decay(2),
                                           bank[6][:, W1:2 * W1], ALU.mult, ALU.add)
                    dve.drain()
                    V.scalar_tensor_tensor(c_st[:, 3, :], c_st[:, 2, :], decay(3),
                                           bank[7][:, W1:2 * W1], ALU.mult, ALU.add)
                    for j, c in enumerate((0, 1, 2, 4)):
                        a = V.tensor_scalar(n_bc[:, j, :], ones[:, :], c_st[:, c, DH:DH + 1], None,
                                            ALU.mult)
                    a.then_inc(st_done.sem, 1)
                    lo_m(4)
                    dve.wait_ge(sp_ps.sem, sp_ps.value(l, h))
                    for i, (t0, n) in enumerate(TILES):
                        V.scalar_tensor_tensor(vg[0:n, i, :], gvt[0:n, i, bass.ds(h * P, P)],
                                               stat[0:n, i, 0:1], rows[0:n, bass.ds(h * P + 2 * GW, P)],
                                               ALU.subtract, ALU.mult)
                    dve.drain()
                    for i, (t0, n) in enumerate(TILES):
                        V.scalar_tensor_tensor(vg[0:n, i, :], vg[0:n, i, :], stat[0:n, i, 3:4],
                                               rows[0:n, bass.ds(h * P + 3 * GW, P)], ALU.mult, ALU.add)
                    dve.drain()
                    V.tensor_copy(gvt[0:TS, 2, bass.ds(h * P, P)], vg[0:TS, 2, :]).then_inc(vg_done.sem, 1)
                    lo_m(5)
                    dve.wait_ge(num_ps.sem, num_ps.value(l, h + 1))
                    dve.wait_ge(z_ev.sem, z_ev.value(l, h * 7 + 9))
                    V.tensor_scalar(hden[:, :], bank[5][:, 0:T], -1.0, None, ALU.mult)
                    dve.drain()
                    V.tensor_tensor(hden[:, :], hden[:, :], bank[5][:, 0:T], ALU.max)
                    dve.drain()
                    V.tensor_tensor(hden[:, :], hden[:, :], mrow_e[:, bass.ds(h * T, T)], ALU.max)
                    dve.drain()
                    V.reciprocal(hden[:, :], hden[:, :])
                    dve.drain()
                    V.scalar_tensor_tensor(hout[:, :], mo[:, :], 1.0, hden[:, :], ALU.add, ALU.mult)
                    dve.drain()
                    V.tensor_tensor(hout[:, :], hout[:, :], bank[4][:, 0:T], ALU.mult
                                    ).then_inc(h_done.sem, 1)
                    lo_m(6)
                    dve.wait_ge(sp_ps.sem, sp_ps.value(l, h + 1))
                    dve.wait_ge(z_ev.sem, z_ev.value(l, h * 7 + 10))
                    V.tensor_tensor(gout[:, :], gu[:, :], bank[6][:, 0:T], ALU.mult
                                    ).then_inc(g_done.sem, 1)
                    lo_m(7)
                    dve.wait_ge(bc_hi.sem, bc_hi.value(l, h * 2 + 1))
                    V.scalar_tensor_tensor(br_lo[:, bass.ds((h + 4) * T, T)], hout[:, :], XS / 2,
                                           br_hi[:, bass.ds((h + 4) * T, T)], ALU.mult, ALU.subtract
                                           ).then_inc(bc_lo.sem, 1)
                    dve.wait_ge(bc_hi.sem, bc_hi.value(l, h * 2 + 2))
                    V.scalar_tensor_tensor(br_lo[:, bass.ds((h + 8) * T, T)], gout[:, :], XS,
                                           br_hi[:, bass.ds((h + 8) * T, T)], ALU.mult, ALU.subtract
                                           ).then_inc(bc_lo.sem, 1)

                with dve.Fori(0, 2) as hf:
                    g0 = hf * APER + A0

                    def lo_a(step):
                        lo_at(l, g0 + (step + LEAD), (A0 + step + LEAD) % SLOTS)

                    dve.wait_ge(s_ps.sem, s_ps.value(l, hf * 6))
                    dve.wait_ge(blk_done.sem, blk_done.value(l, g0 + 1))
                    V.scalar_tensor_tensor(qr_t[:, 0, :], bank[6][:, 0:T], UN, cosT[:, :], ALU.mult,
                                           ALU.mult)
                    V.scalar_tensor_tensor(qr_t[:, 1, :], bank[7][:, 0:T], UN, sinT[:, :], ALU.mult,
                                           ALU.mult)
                    dve.drain()
                    for j in range(4):
                        rs = slice(ROPE * j, ROPE * (j + 1))
                        a = V.tensor_tensor(q_att[NOPE:MROW, j, :], qr_t[rs, 0, :], qr_t[rs, 1, :],
                                            ALU.add)
                    a.then_inc(q_rot.sem, 1)
                    lo_a(0)
                    lo_a(1)
                    dve.wait_ge(blk_done.sem, blk_done.value(l, g0 + 2))
                    for j in range(2):
                        V.tensor_scalar(v_kv[:, 2 * j:2 * j + 2, :], bank[4 + j][:, :].rearrange(
                            "p (i n) -> p i n", i=2), UN, None, ALU.mult)
                    V.tensor_scalar(v_kv[0:TS, 4, :], bank[6][0:TS, 0:2 * P], UN, None, ALU.mult
                                    ).then_inc(v_ev.sem, 1)

                    def out_lo(p):
                        dve.wait_ge(o_hi.sem, o_hi.value(l, hf * 2 + (p + 1)))
                        V.scalar_tensor_tensor(br_lo[:, bass.ds((hf * 2 + p) * T, T)],
                                               bank[7][:, 0:T], XS,
                                               br_hi[:, bass.ds((hf * 2 + p) * T, T)], ALU.mult,
                                               ALU.subtract).then_inc(o_lo.sem, 1)

                    for j in range(6):
                        if j == 5:
                            out_lo(0)
                        lo_a(2 + j)
                        u = hf * 6 + j
                        b = bank[4 + j % 2]
                        dve.wait_ge(s_ps.sem, s_ps.value(l, u + 1))
                        w = 2 if j % 3 < 2 else 1
                        if w == 2:
                            V.tensor_reduce(sm[:, 0:1], b[:, 0:P], AXX, ALU.max)
                            V.tensor_reduce(sm[:, 1:2], b[:, P:3 * P], AXX, ALU.max)
                        else:
                            V.tensor_reduce(sm[:, 0:1], b[:, 0:T], AXX, ALU.max)
                        dve.drain()
                        V.tensor_scalar(sm[:, 2:2 + w], sm[:, 0:w], -ATT_SCALE, None, ALU.mult
                                        ).then_inc(s_max.sem, 1)
                        dve.wait_ge(p_exp.sem, p_exp.value(l, u + 1))
                        V.reciprocal(sm[:, 6:6 + w], sm[:, 4:4 + w])
                        dve.drain()
                        if w == 2:
                            V.tensor_scalar(prob[:, j % 2, 0:P], prob[:, j % 2, 0:P], sm[:, 6:7], None,
                                            ALU.mult)
                            V.tensor_scalar(prob[:, j % 2, P:3 * P], prob[:, j % 2, P:3 * P],
                                            sm[:, 7:8], None, ALU.mult).then_inc(p_norm.sem, 1)
                        else:
                            V.tensor_scalar(prob[:, j % 2, 0:T], prob[:, j % 2, 0:T], sm[:, 6:7], None,
                                            ALU.mult).then_inc(p_norm.sem, 1)
                    out_lo(1)

                with dve.Fori(0, 3) as k:
                    for j in range(4):
                        lo_at(l, k * 4 + (B0 + j + LEAD), (B0 + j + LEAD) % SLOTS)
                        dve.wait_ge(blk_done.sem, blk_done.value(l, k * 4 + (B0 + j + 1)))
                        dve.wait_ge(acc_zero.sem, acc_zero.value(l, 1))
                        dve.wait_ge(z_ev.sem, z_ev.value(l, 54))
                        for i in range(2):
                            c = 2 * j + i
                            V.scalar_tensor_tensor(mtmp[c % 2][:, :],
                                                   gates[:, bass.ds((k * 8 + c) * T, T)], 1.0,
                                                   bank[c % 4][:, 0:T], ALU.add, ALU.mult)
                            dve.drain()
                            V.tensor_tensor(acc[:, c * T:(c + 1) * T], acc[:, c * T:(c + 1) * T],
                                            mtmp[c % 2][:, :], ALU.add).then_inc(m_used.sem, 1)
                for c in range(KD):
                    dve.wait_ge(m_hi.sem, m_hi.value(l, c + 1))
                    V.scalar_tensor_tensor(mlo[:, c, :], acc[:, c * T:(c + 1) * T], UN * XS / 2,
                                           mhi[:, c, :], ALU.mult, ALU.subtract).then_inc(m_lo.sem, 1)

                dve.wait_ge(rw_h.sem, rw_h.value(l, 1))
                V.scalar_tensor_tensor(rw_lo[:, :, :], rw[:, :, :], WS, rw_hi[:, :, :], ALU.mult,
                                       ALU.subtract).then_inc(rw_l.sem, 1)
                for c in range(KD):
                    lo_lead(O0 + c)
                    dve.wait_ge(acc_pre.sem, acc_pre.value(l, 1))
                    dve.wait_ge(blk_done.sem, blk_done.value(l, O0 + c + 1))
                    residual(l, 0, c, (O0 + c) % 4)
                ln_vector(l, 0, C_L1G, C_L1B)

                UPB = [(U0 + j) % 4 for j in range(4)]
                UE = 2 * (EXPERTS + 1)
                lo_lead(U0)
                V.memset(gate_hi, 0.0)
                V.memset(gate_lo, 0.0)
                V.memset(one_hot[:, GROUPS * 3 * CAP:], 0.0)
                dve.wait_ge(r_e.sem, r_e.value(l, 1))
                S, SB, SM, EQ, KY, O1, O2 = range(1, 8)
                V.tensor_scalar(rt[:, S], rt[:, 0], 1.0, None, ALU.add)
                dve.drain()
                V.reciprocal(rt[:, S], rt[:, S])
                dve.drain()
                V.tensor_tensor(rt[:, SB], rt[:, S], rb[:, :, :], ALU.add)
                dve.drain()
                v4 = rt[:, SB].rearrange("p i (g q) -> p (i g) q", q=PER_GROUP)
                for n, (a, b) in enumerate(((0, 1), (0, 2), (0, 3), (1, 2), (1, 3), (2, 3))):
                    V.tensor_tensor(rp[:, :, n:n + 1], v4[:, :, a:a + 1], v4[:, :, b:b + 1], ALU.add)
                dve.drain()
                lo_lead(U0 + 1)

                def g3(n):
                    return rg[:, n]

                V.tensor_reduce(g3(0).rearrange("p i g -> p (i g)"), rp[:, :, :], AXX, ALU.max)
                dve.drain()
                V.tensor_reduce(rg[:, 1, :, 0:1], g3(0), AXX, ALU.max)
                dve.drain()
                V.tensor_tensor(g3(2), g3(0), rg[:, 1, :, 0:1].broadcast_to([P, 3, GROUPS]), ALU.is_equal)
                dve.drain()
                V.tensor_tensor(g3(3), g3(2), rank4[:, :, :], ALU.mult)
                dve.drain()
                V.tensor_reduce(rg[:, 1, :, 1:2], g3(3), AXX, ALU.max)
                dve.drain()
                V.tensor_tensor(g3(4), g3(3), rg[:, 1, :, 1:2].broadcast_to([P, 3, GROUPS]), ALU.is_equal)
                dve.drain()
                V.tensor_copy(gm16[:, 0:2, :], rg[:, 4, 0:2, :])
                V.tensor_copy(gm16[P - TS:P, 2, :], rg[P - TS:P, 4, 2, :]).then_inc(gm_set.sem, 1)
                V.tensor_scalar(g3(5), g3(4), -1.0, -NEG, ALU.add, ALU.mult)
                dve.drain()
                V.tensor_tensor(rt[:, SM].rearrange("p i (g q) -> p (i g) q", q=PER_GROUP), v4,
                                g3(5).rearrange("p i g -> p (i g)").unsqueeze(2).broadcast_to(
                                    [P, 3 * GROUPS, PER_GROUP]), ALU.add)
                for n, o in enumerate((O1, O2)):
                    dve.drain()
                    V.tensor_reduce(rg[:, 6, :, n:n + 1], rt[:, SM], AXX, ALU.max)
                    dve.drain()
                    V.tensor_tensor(rt[:, EQ], rt[:, SM],
                                    rg[:, 6, :, n:n + 1].broadcast_to([P, 3, EXPERTS]), ALU.is_equal)
                    dve.drain()
                    V.tensor_tensor(rt[:, KY], rt[:, EQ], rank16[:, :, :], ALU.mult)
                    dve.drain()
                    V.tensor_reduce(rg[:, 6, :, 2 + n:3 + n], rt[:, KY], AXX, ALU.max)
                    dve.drain()
                    V.tensor_tensor(rt[:, o], rt[:, KY],
                                    rg[:, 6, :, 2 + n:3 + n].broadcast_to([P, 3, EXPERTS]), ALU.is_equal)
                    if n == 0:
                        dve.drain()
                        V.scalar_tensor_tensor(rt[:, SM], rt[:, O1], 3 * NEG, rt[:, SM], ALU.mult,
                                               ALU.add)
                dve.drain()
                V.tensor_tensor(rt[:, O1], rt[:, O1], rt[:, O2], ALU.add)
                dve.drain()
                V.tensor_tensor(rt[:, O1], rt[:, O1], rt[:, S], ALU.mult)
                dve.drain()
                V.tensor_reduce(rg[:, 7, :, 0:1], rt[:, O1], AXX, ALU.add)
                dve.drain()
                V.reciprocal(rg[:, 7, :, 1:2], rg[:, 7, :, 0:1])
                dve.drain()
                V.tensor_tensor(rt[:, O2], rt[:, O1], rg[:, 7, :, 1:2].broadcast_to([P, 3, EXPERTS]),
                                ALU.mult).then_inc(g_sel.sem, 1)

                dve.wait_ge(pos_ps.sem, pos_ps.value(l, 1))
                V.tensor_tensor(place[:, :, :], bank[7][:, 64:64 + 3 * GROUPS].rearrange(
                    "p (i g) -> p i g", i=3), gm16[:, :, :], ALU.mult)
                V.tensor_reduce(most[:, :], bank[7][:, 80:80 + GROUPS], AXX, ALU.max)
                dve.drain()
                for g in range(GROUPS):
                    a = V.tensor_tensor(
                        one_hot[:, g * 3 * CAP:(g + 1) * 3 * CAP].rearrange("p (i n) -> p i n", i=3),
                        slot_no[:, :].unsqueeze(1).broadcast_to([P, 3, CAP]),
                        place[:, :, g:g + 1].broadcast_to([P, 3, CAP]), ALU.is_equal)
                a.then_inc(oh_set.sem, 1)
                V.tensor_copy(most_i[:, :], most[:, :]).then_inc(most_set.sem, 1)

                def hidden(n, ready1, f, W, c0, gate):
                    dve.wait_ge(u_tanh.sem, u_tanh.value(l, n + 1))
                    V.scalar_tensor_tensor(h1[:, 0:W], ht[:, 0:W], 1.0, bank[UPB[2 * f]][:, 0:W], ALU.add,
                                           ALU.mult)
                    dve.drain()
                    dve.wait_ge(blk_done.sem, blk_done.value(l, ready1))
                    V.tensor_tensor(h1[:, 0:W], h1[:, 0:W], bank[UPB[2 * f + 1]][:, 0:W], ALU.mult
                                    ).then_inc(u_free.sem, 1)
                    dve.drain()
                    if gate is not None:
                        dve.wait_ge(gb_ps.sem, gb_ps.value(l, gate))
                        V.tensor_tensor(h2[:, 0:W], h1[:, 0:W], bank[4][:, 0:W], ALU.mult
                                        ).then_inc(u_prod.sem, 1)
                    else:
                        V.tensor_copy(h2[:, 0:W], h1[:, 0:W]).then_inc(u_prod.sem, 1)
                    dve.wait_ge(u_hi.sem, u_hi.value(l, n + 1))
                    scale = UN * UN * XS / (2 if gate is None else 2 * GS)
                    V.scalar_tensor_tensor(hlo[:, bass.ds(c0, W)], h2[:, 0:W], scale,
                                           hhi[:, bass.ds(c0, W)], ALU.mult, ALU.subtract
                                           ).then_inc(u_lo.sem, 1)

                dve.wait_ge(most_set.sem, most_set.value(l, 1))
                lo_lead(U0 + 2)
                dve.wait_ge(gt_h.sem, gt_h.value(l, 1))
                V.scalar_tensor_tensor(gt_lo[:, :, :], rt[:, 7], GS, gt_hi[:, :, :], ALU.mult,
                                       ALU.subtract).then_inc(gt_l.sem, 1)
                lo_lead(U0 + 3)

                def shared_lo():
                    for f in range(2):
                        hidden(f, U0 + (2 * f + 2), f, T, f * T, None)

                def expert_lo(e, W):
                    g0 = e * 4 + (U0 + 4)
                    for f in range(2):
                        lo_at(l, g0 + (2 * f + LEAD), (U0 + 2 * f + LEAD) % SLOTS)
                        lo_at(l, g0 + (2 * f + 1 + LEAD), (U0 + 2 * f + 1 + LEAD) % SLOTS)
                        hidden(e * 2 + (2 + f), g0 + (2 * f + 2), f, W, (e * 2 + f) * W + H0, e + 1)

                def half_out(hf):
                    dve.wait_ge(acc_pre.sem, acc_pre.value(l, 2))
                    dve.wait_ge(sums.sem, sums.value(l, hf + 1))
                    for c in range(4):
                        residual(l, 1, 4 * hf + c, ((0, 1, 2, 3), (4, 5, 0, 1))[hf][c])

                fits = dve.value_load(most_i[0:1, 0:1]) < CAP + 1
                with dve.If(fits):
                    shared_lo()
                    dve.wait_ge(g_hi.sem, g_hi.value(l, 1))
                    V.tensor_tensor(gate_lo[0:EXPERTS, :], bank[4][0:EXPERTS, :], gate_hi[0:EXPERTS, :],
                                    ALU.subtract).then_inc(g_lo.sem, 1)
                    lo_lead(U0 + 4)
                    W2 = 2 * CAP

                    def two(ap):
                        return ap.rearrange("p (f n) -> p f n", f=2)

                    with dve.Fori(0, EXPERTS // 2) as ee:
                        for e2 in range(2):
                            e = ee * 2 + e2
                            g0 = e * 4 + (U0 + 4)

                            def lo_e(j):
                                lo_at(l, g0 + (j + LEAD), (U0 + j + LEAD) % SLOTS)

                            lo_e(1)
                            lo_e(2)
                            lo_e(3)
                            dve.wait_ge(e_tanh.sem, e_tanh.value(l, e + 1))
                            V.scalar_tensor_tensor(h1[:, 0:W2], ht[:, 0:W2], 1.0,
                                                   bank[UPB[2 * e2]][:, 0:W2], ALU.add, ALU.mult)
                            dve.drain()
                            dve.wait_ge(blk_done.sem, blk_done.value(l, g0 + 4))
                            V.tensor_tensor(h1[:, 0:W2], h1[:, 0:W2], bank[UPB[2 * e2 + 1]][:, 0:W2],
                                            ALU.mult).then_inc(e_free.sem, 1)
                            dve.drain()
                            dve.wait_ge(gb_ps.sem, gb_ps.value(l, e + 1))
                            V.tensor_tensor(two(h2[:, 0:W2]), two(h1[:, 0:W2]),
                                            bank[4 + 2 * e2][:, 0:CAP].unsqueeze(1).broadcast_to(
                                                [P, 2, CAP]), ALU.mult).then_inc(e_prod.sem, 1)
                            lo_e(4)
                            dve.wait_ge(e_hi.sem, e_hi.value(l, e + 1))
                            V.scalar_tensor_tensor(hlo[:, bass.ds(e * W2 + H0, W2)], h2[:, 0:W2],
                                                   UN * UN * XS / (2 * GS),
                                                   hhi[:, bass.ds(e * W2 + H0, W2)], ALU.mult,
                                                   ALU.subtract).then_inc(e_lo.sem, 1)

                    def group_out(g, g2, hf):
                        dve.wait_ge(yg_hi.sem, yg_hi.value(l, g + (4 * hf + 1)))
                        V.scalar_tensor_tensor(y_lo[:, bass.ds(g * 512, 512)],
                                               bank[(4, 2)[hf] + g2][:, :], UN * XS,
                                               y_hi[:, bass.ds(g * 512, 512)], ALU.mult, ALU.subtract
                                               ).then_inc(yg_lo.sem, 1)

                    with dve.Fori(0, GROUPS // 2) as gg:
                        for g2 in range(2):
                            for j in range(4):
                                n = D0 + 4 + 4 * g2 + j
                                lo_at(l, gg * 8 + n, n % SLOTS)
                            group_out(gg * 2 + g2, g2, 0)
                    half_out(0)
                    for g in range(GROUPS):
                        for j in range(4):
                            lo_lead(D1 + 3 + 4 * g + j - LEAD)
                        group_out(g, g % 2, 1)
                    lo_lead(NB - 1)
                    for s_ in (u_free, u_prod, u_lo):
                        dve.sem_inc(s_.sem, 2 * EXPERTS)
                    half_out(1)
                with dve.Else():
                    dve.sem_inc(yg_lo.sem, 2 * GROUPS)
                    for s_ in (e_free, e_prod, e_lo):
                        dve.sem_inc(s_.sem, EXPERTS)
                    shared_lo()
                    dve.wait_ge(g_hi.sem, g_hi.value(l, 1))
                    V.tensor_tensor(gate_lo[0:EXPERTS, 0:T], gate32[:, :], gate_hi[0:EXPERTS, 0:T],
                                    ALU.subtract).then_inc(g_lo.sem, 1)
                    with dve.Fori(0, EXPERTS) as e:
                        expert_lo(e, T)
                    lo_lead(D0)
                    with dve.Fori(0, 4) as i:
                        for j in range(4):
                            lo_at(l, i * 4 + (D0 + 1 + j + LEAD), (D0 + 1 + j + LEAD) % SLOTS)
                    lo_lead(D1)
                    dve.wait_ge(blk_done.sem, blk_done.value(l, D1))
                    half_out(0)
                    with dve.Fori(0, 3) as i:
                        for j in range(4):
                            lo_at(l, i * 4 + (D1 + 1 + j + LEAD), (D1 + 1 + j + LEAD) % SLOTS)
                    for j in range(4):
                        lo_lead(D1 + 13 + j)
                    dve.wait_ge(blk_done.sem, blk_done.value(l, NB))
                    half_out(1)
                ln_vector(l, 1, C_L2G, C_L2B)

        @block.tensor
        def _(pe):
            M = nc.tensor.matmul
            TR = nc.tensor.transpose

            def group(out, subs, s, rhs):
                n = 0
                for k, sub in enumerate(subs):
                    for w, part in ((whi, 0), (whi, 1), (wlo, 0)):
                        ins = M(out, w[:, s, sub * P:(sub + 1) * P], rhs(part, k), start=(n == 0),
                                stop=(n == 3 * len(subs) - 1))
                        n += 1
                return ins

            def x_rhs(part, k):
                return (xlo if part else xhi)[:, k, :]

            def ready(l, n):
                pe.wait_ge(lo_done.sem, lo_done.value(l, n + 1))

            def z_block(l, n, s, b):
                ready(l, n)
                group(bank[b][:, 0:T], range(8), s, x_rhs).then_inc(blk_done.sem, 1)

            def tok_block(l, n, s, b):
                ready(l, n)
                for i, (t0, m) in enumerate(TILES):
                    j = 0
                    for k in range(KD):
                        for x, w in ((xhi, whi), (xhi, wlo), (xlo, whi)):
                            ins = M(bank[b][0:m, i * P:(i + 1) * P], x[:, k, t0:t0 + m],
                                    w[:, s, k * P:(k + 1) * P], start=(j == 0), stop=(j == 3 * KD - 1))
                            j += 1
                ins.then_inc(blk_done.sem, 1)

            def stats(l, k):
                last = slice((KD - 1) * T, KD * T)
                pe.wait_ge(y_sum.sem, y_sum.value(l, k + 1))
                M(bank[4 + 2 * k][:, 0:T], ones_dm[:, :], var[:, 0, :], start=True, stop=False)
                pe.wait_ge(sq_sum.sem, sq_sum.value(l, (k + 1) * (KD - 2)))
                M(bank[5 + 2 * k][:, 0:T], ones_dm[:, :], var[:, 1, :], start=True, stop=False)
                pe.wait_ge(y_done.sem, y_done.value(l, (k + 1) * KD))
                M(bank[4 + 2 * k][:, 0:T], ones_dm[:, :], acc[:, last], start=False, stop=True)
                pe.wait_ge(y_sq.sem, y_sq.value(l, (k + 1) * KD))
                M(bank[5 + 2 * k][:, 0:T], ones_dm[:, :], ysq[:, (KD - 1) % 4, :], start=False, stop=True
                  ).then_inc(ln_ps.sem, 1)

            pe.wait_ge(consts_set.sem, N_SET)
            with pe.Fori(0, L) as l:
                def z_wait(n):
                    pe.wait_ge(z_ev.sem, z_ev.value(l, n))

                for g in range(6):
                    if g >= 4:
                        z_wait(g - 3)
                    if g:
                        z_block(l, g, g % SLOTS, g % 4)
                        continue
                    ready(l, 0)
                    for k in range(KD):
                        pe.wait_ge(x_split.sem, x_split.value(l, k + 1 - KD))
                        for w, part in ((whi, 0), (whi, 1), (wlo, 0)):
                            a = M(bank[0][:, 0:T], w[:, 0, k * P:(k + 1) * P], x_rhs(part, k),
                                  start=(k == 0 and w is whi and part == 0),
                                  stop=(k == KD - 1 and w is wlo))
                    a.then_inc(blk_done.sem, 1)
                for i in range(4):
                    g = 6 + i
                    if i == 3:
                        pe.wait_ge(consts_in.sem, 16 * N_CONST)
                        pe.wait_ge(r_exp.sem, r_exp.value(l, 1))
                    if g - 4 < 6:
                        z_wait(g - 3)
                    tok_block(l, g, g % SLOTS, g % 4)
                    if i == 0:
                        for k in range(2):
                            pe.wait_ge(sq_c.sem, sq_c.value(l, k + 1))
                            for c in range(2):
                                a = M(bank[4 + k][:, 0:T], ones_dm[:, :], ysq[:, 2 * k + c, :],
                                      start=(c == 0), stop=(c == 1))
                            a.then_inc(rms_ps.sem, 1)
                for j, src in enumerate((r_a, r_x[:, 3, :])):
                    for i, (t0, m) in enumerate(TILES):
                        c0 = (3 * j + i) * MH
                        a = TR(bank[7][0:m, c0:c0 + MH], src[:, t0:t0 + m], ident[0:MH, 0:MH])
                a.then_inc(cols_ps.sem, 1)

                with pe.Fori(0, MH) as h:
                    g0 = h * MPER + M0

                    def zb(step, freed_z, freed_v=None):
                        pe.wait_ge(z_ev.sem, z_ev.value(l, h * 7 + freed_z))
                        if freed_v is not None:
                            pe.wait_ge(tokv.sem, tokv.value(l, freed_v))
                        return (l, g0 + step, (M0 + step) % SLOTS, (M0 + step) % 4)

                    z_block(*zb(0, 3, 1))
                    z_block(*zb(1, 4, 2))
                    tok_block(*zb(2, 5, 3))
                    pe.wait_ge(z_ev.sem, z_ev.value(l, h * 7 + 8))
                    pe.wait_ge(h_done.sem, h_done.value(l, h))
                    pe.wait_ge(rms_std.sem, rms_std.value(l, 2))
                    pe.wait_ge(cols_sb.sem, cols_sb.value(l, 1))
                    for i, (t0, n) in enumerate(TILES):
                        a = TR(bank[4][0:n, i * P:(i + 1) * P], mk[:, t0:t0 + n], ident[:, :])
                    a.then_inc(k_tr.sem, 1)
                    for i, (t0, n) in enumerate(TILES):
                        a = M(bank[5][0:n, i * P:i * P + n], mk[:, t0:t0 + n], mq[:, t0:t0 + n],
                              start=True, stop=True)
                    a.then_inc(a_ps.sem, 1)
                    z_block(*zb(3, 6, 4))
                    pe.wait_ge(k_sb.sem, k_sb.value(l, h + 1))
                    pe.wait_ge(v_wsd.sem, v_wsd.value(l, h + 1))
                    pe.wait_ge(g_done.sem, g_done.value(l, h))
                    for c in range(NCH):
                        r0, b, o = CH * (c % 2), bank[6 + c % 2], (c // 2) * (DH + 1)
                        a = M(b[:, o:o + DH + 1], k_tok[r0:r0 + CH, c // 2, :],
                              v_ws[r0:r0 + CH, c // 2, :], start=True, stop=True)
                    a.then_inc(dc_ps.sem, 1)
                    z_block(*zb(4, 7))
                    z_block(*zb(5, 8))
                    pe.wait_ge(att_done.sem, att_done.value(l, h + 1))
                    pe.wait_ge(st_done.sem, st_done.value(l, h + 1))
                    for num, b in ((True, bank[4]), (False, bank[5])):
                        for i, (t0, n) in enumerate(TILES):
                            M(b[:, t0:t0 + n], v_tok[0:n, i, :] if num else ones[0:n, :],
                              att[0:n, i, 0:n], start=True, stop=False)
                            for j, (c, st) in enumerate(((1, 0), (2, 1), (3, 2), (4, 4))):
                                if t0 <= c * CH < t0 + n:
                                    last = (c + 1) * CH == t0 + n
                                    a = M(b[:, c * CH:(c + 1) * CH],
                                          c_st[:, st, 0:DH] if num else n_bc[:, j, :],
                                          q_in[:, c * CH:(c + 1) * CH], start=False, stop=last)
                    a.then_inc(num_ps.sem, 1)
                    z_block(*zb(6, 8, 5 + h))
                    pe.wait_ge(vg_done.sem, vg_done.value(l, h + 1))
                    pe.wait_ge(ws_masked.sem, ws_masked.value(l, 1))
                    for i, (t0, n) in enumerate(TILES):
                        off = h * P
                        M(bank[6][:, t0:t0 + n], vg[0:n, i, :], ws_t[0:n, bass.ds(off, n)], start=True,
                          stop=False)
                        a = M(bank[6][:, t0:t0 + n], ones[0:1, :], bs_row[:, bass.ds(off, n)],
                              start=False, stop=True)
                    a.then_inc(sp_ps.sem, 1)
                    z_block(*zb(7, 9))

                with pe.Fori(0, 2) as hf:
                    g0 = hf * APER + A0
                    s0, s1 = A0 % SLOTS, (A0 + 1) % SLOTS
                    ready(l, g0)
                    pe.wait_ge(c_lo.sem, c_lo.value(l, 3))
                    pe.wait_ge(g_done.sem, g_done.value(l, MH))
                    pe.wait_ge(h_done.sem, h_done.value(l, MH))
                    pe.wait_ge(o_lo.sem, o_lo.value(l, hf * 2))
                    for j in range(4):
                        a = group(bank[4 + j][:, 0:T], (2 * j, 2 * j + 1), s0,
                                  lambda part, k: (cq_lo if part else cq_hi)[:, k, :])
                    a.then_inc(blk_done.sem, 1)
                    ready(l, g0 + 1)
                    pe.wait_ge(z_ev.sem, z_ev.value(l, hf * 10 + 34))
                    pe.wait_ge(t_sb.sem, t_sb.value(l, hf * 6))
                    for j in range(4):
                        k0 = (j % 2) * KH
                        group(bank[j][:, 0:KH], (2 * (j // 2), 2 * (j // 2) + 1), s1,
                              lambda part, k: (kv_lo if part else kv_hi)[:, k, k0:k0 + KH])
                    pe.wait_ge(q_ev.sem, q_ev.value(l, hf + 1))
                    pe.wait_ge(q_rot.sem, q_rot.value(l, hf + 1))
                    for i in range(5):
                        n = P if i < 4 else TS
                        j = 0
                        for k in range(2):
                            for x, w in ((kv_hi, whi), (kv_hi, wlo), (kv_lo, whi)):
                                a = M(bank[4 + i // 2][0:n, (i % 2) * 2 * P:(i % 2 + 1) * 2 * P],
                                      x[:, k, i * P:i * P + n],
                                      w[:, s1, (4 + 2 * k) * P:(6 + 2 * k) * P], start=(j == 0),
                                      stop=(j == 5))
                                j += 1
                    a.then_inc(blk_done.sem, 1)

                    def scores(j):
                        p, r = j // 3, j % 3
                        b = bank[4 + j % 2]
                        if j < 2:
                            pe.wait_ge(v_ev.sem, v_ev.value(l, hf + 1))
                        if j >= 2:
                            pe.wait_ge(p_exp.sem, p_exp.value(l, hf * 6 + (j - 1)))
                        if j == 0:
                            pe.wait_ge(att_rows.sem, att_rows.value(l, 2))
                            pe.wait_ge(z_ev.sem, z_ev.value(l, hf * 10 + 36))
                        if r < 2:
                            hh = 2 * p + r
                            for q in range(2):
                                a = M(b[:, P * q:P * q + P * (q + 1)],
                                      q_att[0:KATT, hh, P * q:P * (q + 1)],
                                      k_att[0:KATT, hh, PAST:PAST + P * (q + 1)], start=True, stop=True)
                        else:
                            for r_ in range(2):
                                hh = 2 * p + r_
                                for o, k0, n in ((0, 0, PAST), (PAST, PAST + TP, TS)):
                                    a = M(b[TS * r_:TS * (r_ + 1), o:o + n], q_att[0:KATT, hh, TP:T],
                                          k_att[0:KATT, hh, k0:k0 + n], start=True, stop=True)
                        a.then_inc(s_ps.sem, 1)

                    def transposes(j):
                        pe.wait_ge(p_norm.sem, p_norm.value(l, hf * 6 + (j + 1)))
                        if j:
                            pe.wait_ge(t_sb.sem, t_sb.value(l, hf * 6 + j))
                        for i in range(3):
                            n = P if j % 3 < 2 or i < 2 else TS
                            a = TR(bank[6][0:n, i * P:(i + 1) * P], prob[:, j % 2, i * P:i * P + n],
                                   ident[:, :])
                        a.then_inc(t_ps.sem, 1)

                    def values(j):
                        p, r = j // 3, j % 3
                        pe.wait_ge(t_sb.sem, t_sb.value(l, hf * 6 + (j + 1)))
                        if j == 3:
                            pe.wait_ge(o_lo.sem, o_lo.value(l, hf * 2 + 1))
                        for r_ in ((r,) if r < 2 else (0, 1)):
                            vc = slice((2 * p + r_) * VD, (2 * p + r_ + 1) * VD)
                            o = bank[7][VD * r_:VD * (r_ + 1), :]
                            if r < 2:
                                M(o[:, 0:P], v_kv[:, 2, vc], prob_t[:, j % 2, 0, :], start=True,
                                  stop=True)
                                M(o[:, P:2 * P], v_kv[:, 2, vc], prob_t[:, j % 2, 1, :], start=True,
                                  stop=False)
                                a = M(o[:, P:2 * P], v_kv[:, 3, vc], prob_t[:, j % 2, 2, :],
                                      start=False, stop=True)
                            else:
                                qs = slice(TS * r_, TS * (r_ + 1))
                                for n, (kt, rows_) in enumerate(((0, P), (1, P), (4, TS))):
                                    a = M(o[:, TP:T], v_kv[0:rows_, kt, vc],
                                          prob_t[0:rows_, j % 2, n, qs], start=(n == 0), stop=(n == 2))
                        a.then_inc(o_ps.sem, 1)

                    for j in range(6):
                        scores(j)
                        if j:
                            transposes(j - 1)
                        if j >= 2:
                            values(j - 2)
                        pe.wait_ge(z_ev.sem, z_ev.value(l, hf * 10 + (35 + j)))
                        z_block(l, g0 + (2 + j), (A0 + 2 + j) % SLOTS, (A0 + 2 + j) % 4)
                    transposes(5)
                    values(4)
                    values(5)

                with pe.Fori(0, 3) as k:
                    pe.wait_ge(z_ev.sem, z_ev.value(l, 54))
                    pe.wait_ge(bc_lo.sem, bc_lo.value(l, 2 * MH))
                    pe.wait_ge(o_lo.sem, o_lo.value(l, 4))
                    for j in range(4):
                        ready(l, k * 4 + (B0 + j))
                        for i in range(2):
                            c = 2 * j + i
                            pe.wait_ge(m_used.sem, m_used.value(l, k * 8 + (c - 3)))
                            a = group(bank[c % 4][:, 0:T], range(4 * i, 4 * i + 4), (B0 + j) % SLOTS,
                                      lambda part, kt: (br_lo if part else br_hi)[
                                          :, bass.ds((k * 4 + kt) * T, T)])
                        a.then_inc(blk_done.sem, 1)

                for c in range(KD):
                    ready(l, O0 + c)
                    if c >= 4:
                        pe.wait_ge(y_done.sem, y_done.value(l, c - 3))
                    for k in range(KD):
                        if c == 0:
                            pe.wait_ge(m_lo.sem, m_lo.value(l, k + 1))
                        for w, m in ((whi, mhi), (whi, mlo), (wlo, mhi)):
                            a = M(bank[(O0 + c) % 4][:, 0:T], w[:, (O0 + c) % SLOTS, k * P:(k + 1) * P],
                                  m[:, k, :], start=(k == 0 and w is whi and m is mhi),
                                  stop=(k == KD - 1 and w is wlo))
                    a.then_inc(blk_done.sem, 1)
                stats(l, 0)

                UPB = [(U0 + j) % 4 for j in range(4)]
                EYE, LE, ONE = (mats16[:, n, :] for n in range(3))
                pe.wait_ge(rw_l.sem, rw_l.value(l, 1))
                ready(l, U0)
                for k in range(KD):
                    pe.wait_ge(x_split.sem, x_split.value(l, k + 1))
                    for w, part in ((whi, 0), (whi, 1), (wlo, 0)):
                        u0 = M(bank[UPB[0]][:, 0:T], w[:, U0 % SLOTS, k * P:(k + 1) * P], x_rhs(part, k),
                               start=(k == 0 and w is whi and part == 0), stop=(k == KD - 1 and w is wlo))
                    for i in range(3):
                        t0 = min(i * P, T - P)
                        for x, w in ((xhi, rw_hi), (xhi, rw_lo), (xlo, rw_hi)):
                            a = M(bank[(4, 5, 7)[i]][:, i * EXPERTS:(i + 1) * EXPERTS], x[:, k, t0:t0 + P],
                                  w[:, k, :], start=(k == 0 and x is xhi and w is rw_hi),
                                  stop=(k == KD - 1 and x is xlo))
                    if k == KD - 1:
                        u0.then_inc(blk_done.sem, 1)
                a.then_inc(r_ps.sem, 1)
                for j in range(4):
                    if j:
                        z_block(l, U0 + j, (U0 + j) % SLOTS, UPB[j])
                    if j == 2:
                        pe.wait_ge(gm_set.sem, gm_set.value(l, 1))
                        for i in range(4):
                            for k in range(min(i, 2) + 1):
                                o = 64 + 4 * i if i < 3 else 80
                                a = M(bank[7][:, o:o + GROUPS], LE if k == i else ONE, gm16[:, k, :],
                                      start=(k == 0), stop=(k == min(i, 2)))
                        a.then_inc(pos_ps.sem, 1)
                    if j == 3:
                        pe.wait_ge(most_set.sem, most_set.value(l, 1))
                    for n in range(3 * j, 3 * j + 3):
                        part, half, t0 = n // 6, n // 3 % 2, min(n % 3 * P, T - P)
                        if n == 0:
                            pe.wait_ge(r_e.sem, r_e.value(l, 1))
                        if n >= 3:
                            pe.wait_ge(xt_ev.sem, xt_ev.value(l, n - 2))
                        for c in range(4):
                            a = M(bank[4 + n % 3][:, c * P:(c + 1) * P],
                                  (xlo if part else xhi)[:, 4 * half + c, t0:t0 + P], EYE, start=True,
                                  stop=True)
                        a.then_inc(xt_ps.sem, 1)

                def gate_rows(out, e, col, W):
                    M(out, exp_sel[:, bass.ds(e * P, P)], gate_hi[:, bass.ds(col, W)], start=True,
                      stop=False)
                    M(out, exp_sel[:, bass.ds(e * P, P)], gate_lo[:, bass.ds(col, W)], start=False,
                      stop=True).then_inc(gb_ps.sem, 1)

                half0, half1 = (0, 1, 2, 3), (4, 5, 0, 1)

                def down(l, n, s, banks, expert, first, last):
                    ready(l, n)
                    for kt in range(2):
                        for i, b in enumerate(banks):
                            for w, h_ in ((whi, hhi), (whi, hlo), (wlo, hhi)):
                                a = M(bank[b][:, 0:T], w[:, s, (4 * kt + i) * P:(4 * kt + i + 1) * P],
                                      h_[:, bass.ds((expert * 2 + kt) * T, T)],
                                      start=(first and kt == 0 and w is whi and h_ is hhi),
                                      stop=(last and kt == 1 and w is wlo))
                    a.then_inc(blk_done.sem, 1)

                def gather(b, g, q):
                    for c in range(4):
                        for i in range(3):
                            a = M(bank[b][:, c * P:(c + 1) * P],
                                  x_tok[:, bass.ds(q * 1536 + (i * 512 + c * P), P)],
                                  one_hot[:, bass.ds(g * (3 * CAP) + i * CAP, CAP)], start=(i == 0),
                                  stop=(i == 2))
                    a.then_inc(xg_ps.sem, 1)

                fits = pe.value_load(most_i[0:1, 0:1]) < CAP + 1
                with pe.If(fits):
                    pe.wait_ge(xt_ev.sem, xt_ev.value(l, 12))
                    pe.wait_ge(oh_set.sem, oh_set.value(l, 1))
                    for q in range(4):
                        if q >= 2:
                            pe.wait_ge(xg_ev.sem, xg_ev.value(l, q - 1))
                        gather(5 + q % 2, 0, q)
                    pe.wait_ge(gt_l.sem, gt_l.value(l, 1))
                    slots = one_hot[:, 0:GROUPS * 3 * CAP].rearrange("p (g i n) -> p g i n", g=GROUPS, i=3)
                    for i in range(3):
                        for part in (gt_hi, gt_lo):
                            a = M(bank[4][0:EXPERTS, :], part[:, i, :], slots[:, :, i, :],
                                  start=(i == 0 and part is gt_hi), stop=(i == 2 and part is gt_lo))
                    a.then_inc(g_tr.sem, 1)
                    with pe.Fori(0, GROUPS // 2) as gg:
                        for g2 in range(2):
                            g = gg * 2 + g2
                            pe.wait_ge(ot_ev.sem, ot_ev.value(l, g))
                            pe.wait_ge(xg_ev.sem, xg_ev.value(l, gg * 8 + (4 * g2 + 4)))
                            for i in range(3):
                                t0, n = TILES[i]
                                a = M(bank[7][:, t0:t0 + n],
                                      one_hot[:, bass.ds(g * (3 * CAP) + i * CAP, CAP)],
                                      mats16[:, 0, P - n:P], start=True, stop=True)
                            a.then_inc(ot_ps.sem, 1)
                            with pe.Fori(0, 2) as qq:
                                for e2 in range(2):
                                    e = gg * 8 + qq * 2 + (4 * g2 + e2)
                                    g0 = e * 4 + (U0 + 4)
                                    pe.wait_ge(u_free.sem, u_free.value(l, 1 + e2))
                                    pe.wait_ge(e_free.sem, e_free.value(l, e - 1))
                                    for j in range(4):
                                        ready(l, g0 + j)
                                        b = bank[UPB[2 * e2 + j % 2]]
                                        group(b[:, j // 2 * CAP:(j // 2 + 1) * CAP], range(8),
                                              (U0 + j) % SLOTS,
                                              lambda part, k: x_grp[:, g2, part, k, :]
                                              ).then_inc(blk_done.sem, 1)
                                        if j == 0:
                                            pe.wait_ge(g_lo.sem, g_lo.value(l, 1))
                                            pe.wait_ge(e_prod.sem, e_prod.value(l, e - 1))
                                            gate_rows(bank[4 + 2 * e2][:, 0:CAP], e, g * CAP, CAP)
                                        if j == 1:
                                            pe.wait_ge(xg_ev.sem, xg_ev.value(l, e + 4))
                                            gather(5, g + 1, qq * 2 + e2)

                    def group_down(g, g2, hf):
                        b = bank[(4, 2)[hf] + g2]
                        pe.wait_ge(e_lo.sem, e_lo.value(l, EXPERTS))
                        pe.wait_ge(xg_ev.sem, xg_ev.value(l, 20))
                        pe.wait_ge(ot_ev.sem, ot_ev.value(l, GROUPS))
                        if hf:
                            pe.wait_ge(y_done.sem, y_done.value(l, KD + 4))
                        pe.wait_ge(yg_lo.sem, yg_lo.value(l, g + (4 * hf - 1)))
                        for q in range(4):
                            n = (D0, D1)[hf] + 1 + q
                            ready(l, g * 4 + n)
                            for kt in range(2):
                                for w, h_ in ((whi, hhi), (wlo, hhi), (whi, hlo)):
                                    a = M(b[:, :], h_[:, bass.ds(g * (8 * CAP) + ((2 * q + kt) * CAP + H0),
                                                                 CAP)],
                                          w[:, n % SLOTS, kt * 512:(kt + 1) * 512],
                                          start=(q == 0 and kt == 0 and w is whi and h_ is hhi),
                                          stop=(q == 3 and kt == 1 and h_ is hlo))
                            a.then_inc(blk_done.sem, 1)

                    def scatter(hf, banks):
                        for g in range(GROUPS):
                            pe.wait_ge(yg_lo.sem, yg_lo.value(l, 4 * hf + g + 1))
                            for i, b in enumerate(banks):
                                for y in (y_hi, y_lo):
                                    a = M(bank[b][:, 0:T], y[:, g * 512 + i * P:g * 512 + (i + 1) * P],
                                          slot_tok[:, g * T:(g + 1) * T], start=False,
                                          stop=(g == GROUPS - 1 and y is y_lo))
                        a.then_inc(sums.sem, 1)

                    pe.wait_ge(u_lo.sem, u_lo.value(l, 2))
                    pe.wait_ge(e_free.sem, e_free.value(l, EXPERTS))
                    down(l, D0, D0 % SLOTS, half0, 0, True, False)
                    with pe.Fori(0, GROUPS // 2) as gg:
                        for g2 in range(2):
                            group_down(gg * 2 + g2, g2, 0)
                    scatter(0, half0)
                    pe.wait_ge(y_done.sem, y_done.value(l, KD + 2))
                    down(l, D1, D1 % SLOTS, half1, 0, True, False)
                    with pe.Fori(0, GROUPS // 2) as gg:
                        for g2 in range(2):
                            group_down(gg * 2 + g2, g2, 1)
                    scatter(1, half1)
                with pe.Else():
                    pe.sem_inc(xg_ps.sem, 20)
                    pe.sem_inc(ot_ps.sem, GROUPS)
                    pe.wait_ge(g_sel.sem, g_sel.value(l, 1))
                    pe.wait_ge(xt_ev.sem, xt_ev.value(l, 12))
                    for i in range(3):
                        a = TR(bank[6][0:EXPERTS, i * P:(i + 1) * P], rt[:, 7, i, :], ident[:, :])
                    a.then_inc(g_tr.sem, 1)
                    with pe.Fori(0, EXPERTS) as e:
                        g0 = e * 4 + (U0 + 4)
                        for j in range(4):
                            if j % 2 == 0:
                                pe.wait_ge(u_free.sem, u_free.value(l, e * 2 + (1 + j // 2)))
                            z_block(l, g0 + j, (U0 + j) % SLOTS, UPB[j])
                            if j == 0:
                                pe.wait_ge(g_lo.sem, g_lo.value(l, 1))
                                pe.wait_ge(u_prod.sem, u_prod.value(l, e * 2 + 2))
                                gate_rows(bank[4][:, 0:T], e, 0, T)
                    pe.wait_ge(u_lo.sem, u_lo.value(l, 2 * (EXPERTS + 1)))
                    down(l, D0, D0 % SLOTS, half0, 0, True, False)
                    with pe.Fori(0, 3) as i:
                        for j in range(4):
                            down(l, i * 4 + (D0 + 1 + j), (D0 + 1 + j) % SLOTS, half0, i * 4 + (1 + j),
                                 False, False)
                    for j in range(4):
                        down(l, D0 + 13 + j, (D0 + 13 + j) % SLOTS, half0, 13 + j, False, j == 3)
                    pe.sem_inc(sums.sem, 1)
                    pe.wait_ge(y_done.sem, y_done.value(l, KD + 2))
                    down(l, D1, D1 % SLOTS, half1, 0, True, False)
                    with pe.Fori(0, 3) as i:
                        for j in range(4):
                            down(l, i * 4 + (D1 + 1 + j), (D1 + 1 + j) % SLOTS, half1, i * 4 + (1 + j),
                                 False, False)
                    for j in range(4):
                        down(l, D1 + 13 + j, (D1 + 13 + j) % SLOTS, half1, 13 + j, False, j == 3)
                    pe.sem_inc(sums.sem, 1)
                stats(l, 1)


def _blocks(inp):
    def kt(w):
        return w.reshape(-1, P, w.shape[1]).transpose(1, 0, 2)

    out = np.zeros((L, NB, P, BLK), np.float32)
    half = ROPE // 2
    swap = np.r_[half:ROPE, 0:half]
    zin = np.cumsum([0, RANK, RANK, ROPE, 512, 512, 512, MH, MH, 512, 512, 512])
    cq, ckv, kr, q, k, v, gi, gf, go, gu, gv, gt = (int(n) for n in zin)

    def cols(i):
        gate = np.full(P, -1)
        gate[0:MH] = gi + np.arange(MH)
        gate[32:32 + MH] = gf + np.arange(MH)
        rot = np.full(P, -1)
        rot[0:ROPE] = kr + np.arange(ROPE)
        rot[ROPE:2 * ROPE] = kr + swap
        tile = lambda base, n: base + n * P + np.arange(P)
        front = [gate, tile(cq, 0), tile(cq, 1), tile(ckv, 0), tile(ckv, 1), rot]
        heads = [[tile(q, h), tile(k, h), tile(v, h), tile(go, h), tile(gu, h)] for h in range(MH)]
        return front, [tile(gv, n) for n in range(4)], heads, [tile(gt, n) for n in range(24)]

    front, gvs, heads, gts = cols(0)
    z = {n: c for n, c in enumerate(front)}
    z.update({6 + n: c for n, c in enumerate(gvs)})
    for h in range(MH):
        for n, c in enumerate(heads[h] + gts[3 * h:3 * h + 3]):
            z[M0 + MPER * h + n] = c
    for hf in range(2):
        for n in range(6):
            z[A0 + APER * hf + 2 + n] = gts[12 + 6 * hf + n]
    par = np.zeros((P, L, NPAR), np.float32)
    for l in range(L):
        w, b = inp["w_in"][l], inp["b_in"][l]

        def take(a, c):
            return np.where(c >= 0, a[..., np.maximum(c, 0)], np.float32(0))

        for n, c in z.items():
            out[l, n] = kt(take(w, c)).reshape(P, BLK)
        for n, c in enumerate(front):
            par[:, l, C_FRONT + n] = take(b, c)
        for h in range(MH):
            for n, c in enumerate((heads[h][0], heads[h][1], heads[h][3], heads[h][4])):
                par[:, l, C_MLSTM + 4 * h + n] = take(b, c)
        for n, c in enumerate(gts):
            par[:, l, C_GATE + n] = take(b, c)
        for col, name in ((C_QG, "q_norm_g"), (C_KVG, "kv_norm_g"), (C_L1G, "ln1_g"), (C_L1B, "ln1_b"),
                          (C_L2G, "ln2_g"), (C_L2B, "ln2_b")):
            a = inp[name][l].reshape(-1, P).T
            par[:, l, col:col + a.shape[1]] = a
        uq = inp["w_uq"][l].reshape(RANK, HEADS, NOPE + ROPE)
        ukv = inp["w_ukv"][l].reshape(RANK, HEADS, NOPE + VD)
        for hf in range(2):
            hs = slice(4 * hf, 4 * hf + 4)
            n = A0 + APER * hf
            tiles = [uq[:, 4 * hf:4 * hf + 2, :NOPE], uq[:, 4 * hf + 2:4 * hf + 4, :NOPE],
                     uq[:, hs, NOPE:], uq[:, hs, NOPE:][:, :, swap]]
            out[l, n] = np.concatenate([kt(t.reshape(RANK, P)).reshape(P, 2 * P) for t in tiles], 1)
            kv = [kt(ukv[:, 4 * hf + 2 * j:4 * hf + 2 * j + 2, :NOPE].reshape(RANK, P)).reshape(P, 2 * P)
                  for j in range(2)]
            kv.append(kt(ukv[:, hs, NOPE:].reshape(RANK, 2 * P)).reshape(P, 4 * P))
            out[l, n + 1] = np.concatenate(kv, 1)
        for k_ in range(3):
            w4 = inp["w_branch"][l, k_].reshape(4, P, 4, 2, P).transpose(2, 1, 3, 0, 4)
            out[l, B0 + 4 * k_:B0 + 4 * k_ + 4] = w4.reshape(4, P, BLK)
        out[l, O0:U0] = inp["w_out"][l].reshape(KD, P, KD, P).transpose(2, 1, 0, 3).reshape(KD, P, BLK)
        wg = np.concatenate([inp["shared_w_gate"][l][None], inp["moe_w_gate"][l]])
        wu = np.concatenate([inp["shared_w_up"][l][None], inp["moe_w_up"][l]])
        wd = np.concatenate([inp["shared_w_down"][l][None], inp["moe_w_down"][l]])
        up = np.stack([wg, wu], 1).reshape(EXPERTS + 1, 2, KD, P, 2, P)
        out[l, U0:D0] = up.transpose(0, 4, 1, 3, 2, 5).reshape(-1, P, BLK)
        dn = wd.reshape(EXPERTS + 1, 2, P, 2, 4, P).transpose(3, 0, 2, 1, 4, 5)
        out[l, D0:NB] = dn.reshape(-1, P, BLK)
    rows = np.stack([inp["b_in"][:, gv:gv + 512], inp["b_in"][:, v:v + 512],
                     inp["gmlp_ln_g"], inp["gmlp_ln_b"]], 1)
    return out.reshape(L * NB * P, BLK), par.reshape(P, L * NPAR), rows.reshape(L, 4 * GW)


def _constants():
    half = ROPE // 2
    pos = np.r_[0:TP, PAST:PAST + TS].astype(np.float32)
    inv = (np.float32(10000.0) ** (-np.arange(half, dtype=np.float32) / half)).astype(np.float32)
    ang = pos[None, :] * inv[:, None]
    cos, sin = np.cos(ang), np.sin(ang)
    s, t = np.arange(P)[:, None], np.arange(T)[None, :]
    tt = t % P
    mmask = np.where((s <= tt) & (s // CH == tt // CH), 0, NEG)
    keep = np.broadcast_to(np.arange(T) % CH != 0, (MH, T))
    att = np.zeros((2, T + KEYS))
    for n in range(2):
        att[n, n * P:n * P + CH] = 1
        att[n, T + PAST + n * P + CH:T + PAST + (n + 1) * P] = NEG
    sel = np.zeros((P, EXPERTS, P), np.float16)
    sel[np.arange(EXPERTS), np.arange(EXPERTS)] = 1
    c = dict(
        cos=np.tile(np.concatenate([cos, cos]), (4, 1)), sin=np.tile(np.concatenate([-sin, sin]), (4, 1)),
        ident=np.eye(P), mmask=mmask, scan_keep=keep,
        att_mask=att,
        rank4=np.broadcast_to(np.arange(GROUPS, 0, -1), (P, 3, GROUPS)),
        rank16=np.broadcast_to(np.arange(EXPERTS, 0, -1), (P, 3, EXPERTS)))
    c["slot_no"] = np.broadcast_to(np.arange(1, CAP + 1), (P, CAP))
    c = {n: np.ascontiguousarray(a, dtype=np.float32) for n, a in c.items()}
    c["mats16"] = np.stack([np.eye(P), np.triu(np.ones((P, P))), np.ones((P, P))], 1).astype(np.float16)
    c["exp_sel"] = sel.reshape(P, EXPERTS * P)
    return c


_OUTS = dict(y=(P, KD * T), ckv=(L * P, 2 * T), kr_out=(L * ROPE, T), m_out=(L * MH, 8),
             gv_out=(L * TS, GW), c_prompt=(L * MH * P, DH + 1), c_sample=(L * MH * P, DH + 1))


def kernel(**inputs):
    import concourse.bacc as bacc
    from concourse.bass_utils import run_bass_kernel_spmd

    inp = {k: np.asarray(v) for k, v in inputs.items()}
    w, par, rows = _blocks(inp)
    x = np.concatenate([inp["x_prompt"][0], inp["x_sample"][0]])
    c0 = np.concatenate([inp["state_mlstm_c"][:, 0].transpose(0, 1, 3, 2),
                         inp["state_mlstm_n"][:, 0][..., None]], -1)
    arrays = dict(
        x=x.T.reshape(KD, P, T).transpose(1, 0, 2).reshape(P, KD * T), w=w, par=par, rows=rows,
        rb=np.tile(inp["router_b"], 3), rw=inp["router_w"].reshape(KD, P, EXPERTS).transpose(1, 0, 2),
        m_init=inp["state_mlstm_m"][:, 0].T, c_init=c0.transpose(0, 2, 1, 3).reshape(L * P, -1),
        cache=inp["cache_mla_ckv"][:, 0].reshape(L, PAST, 2, P).transpose(0, 3, 2, 1).reshape(L * P, -1),
        krope=inp["cache_mla_krope"][:, 0].transpose(0, 2, 1).reshape(L * ROPE, PAST),
        ws_t=inp["gmlp_ws"].transpose(0, 3, 1, 2).reshape(L * P, -1),
        bs_row=inp["gmlp_bs"].reshape(L, -1), **_constants())
    arrays = {n: np.ascontiguousarray(a) for n, a in arrays.items()}
    nc = bacc.Bacc("TRN2", target_bir_lowering=False, num_devices=1)
    d = {n: nc.dram_tensor(f"in_{n}", a.shape, mybir.dt.from_np(a.dtype), kind="ExternalInput").ap()
         for n, a in arrays.items()}
    d.update({n: nc.dram_tensor(f"out_{n}", s, F32, kind="ExternalOutput").ap() for n, s in _OUTS.items()})
    d["head_rows"] = nc.dram_tensor("head_rows", (1, 3 * MH * T), F32, kind="Internal").ap()
    build_trunk(nc, d)
    r = run_bass_kernel_spmd(nc, [{f"in_{n}": a for n, a in arrays.items()}], core_ids=[0]).results[0]
    o = {n: np.asarray(r[f"out_{n}"]) for n in _OUTS}

    y = o["y"].reshape(P, KD, T).transpose(2, 1, 0).reshape(T, DM)
    ckv = o["ckv"].reshape(L, P, 2, T).transpose(0, 3, 2, 1).reshape(L, 1, T, RANK)
    kr = o["kr_out"].reshape(L, ROPE, T).transpose(0, 2, 1).reshape(L, 1, T, ROPE)
    m = o["m_out"].reshape(L, 1, MH, 8)
    cp, cs = (o[n].reshape(L, 1, MH, DH, DH + 1) for n in ("c_prompt", "c_sample"))
    c = np.ascontiguousarray
    return (c(y[None, :TP]), c(y[None, TP:]), c(ckv[:, :, :TP]), c(kr[:, :, :TP]),
            c(cp[..., :DH].swapaxes(3, 4)), c(cp[..., DH]), c(m[..., 4]),
            c(ckv[:, :, TP:]), c(kr[:, :, TP:]), c(cs[..., :DH].swapaxes(3, 4)), c(cs[..., DH]),
            c(m[..., 6]), c(o["gv_out"].reshape(L, 1, TS, GW)))
```
